# Optimizing a Trainium2 kernel written in Bass

```python
import jax, jax.numpy as jnp
from jax import lax
import numpy as np

D_MODEL = 1024
BATCH = 1
SEQ = 128
DEPTH = 2
DEC_BATCH = 1
DEC_SEQ = 512
PAST_LEN = 128

GRID_W = 64
HEAD_DIM = 64
ATTN_WIDTH = D_MODEL // 2
ATTN_HEADS = ATTN_WIDTH // HEAD_DIM
ATTN_KV_HEADS = ATTN_HEADS // 4
ATTN_GROUP = ATTN_HEADS // ATTN_KV_HEADS
KV_WIDTH = ATTN_KV_HEADS * HEAD_DIM
HG_WIDTH = D_MODEL // 4
HG_DK = 64
HG_DV = 64
HG_HEADS = HG_WIDTH // HG_DK
FT_WIDTH = D_MODEL // 4
FT_CH = 64
FT_GROUPS = FT_WIDTH // FT_CH
MIX_WIDTH = ATTN_WIDTH + HG_WIDTH + FT_WIDTH
IN_WIDTH = ATTN_WIDTH + 2 * KV_WIDTH + 5 * HG_WIDTH + FT_WIDTH
IN_SPLITS = (
    ATTN_WIDTH,
    ATTN_WIDTH + KV_WIDTH,
    ATTN_WIDTH + 2 * KV_WIDTH,
    ATTN_WIDTH + 2 * KV_WIDTH + HG_WIDTH,
    ATTN_WIDTH + 2 * KV_WIDTH + 2 * HG_WIDTH,
    ATTN_WIDTH + 2 * KV_WIDTH + 3 * HG_WIDTH,
    ATTN_WIDTH + 2 * KV_WIDTH + 4 * HG_WIDTH,
    ATTN_WIDTH + 2 * KV_WIDTH + 5 * HG_WIDTH,
)
N_GROUPS = 4
EXPERTS_PER_GROUP = 4
N_EXPERTS = N_GROUPS * EXPERTS_PER_GROUP
MOE_TOP_K = 2
D_EXPERT = 256
Q_BLOCK = 128
CHUNK = 64
ROPE_THETA = 10000.0
EPS = 1e-6
EXP_CLIP = 80.0

kernel_name = 'hybrid_prefix_diffusion_step'

F32 = jnp.float32

def _rms(x, w):
    xf = x.astype(F32)
    y = xf * lax.rsqrt(jnp.mean(xf * xf, axis=-1, keepdims=True) + EPS)
    return (y * w.astype(F32)).astype(x.dtype)

def _modulation(cond, w_ada, b_ada):
    m = jnp.einsum('bd,de->be', jax.nn.silu(cond), w_ada) + b_ada
    return tuple(jnp.split(m[:, None, :], 6, axis=-1))

def _axial_angles(n_tokens):
    rows = n_tokens // GRID_W
    row = jnp.repeat(jnp.arange(rows, dtype=F32), GRID_W)
    col = jnp.tile(jnp.arange(GRID_W, dtype=F32), rows)
    half = HEAD_DIM // 2
    inv = 1.0 / (ROPE_THETA ** (jnp.arange(0, half, 2, dtype=F32) / half))
    return row[:, None] * inv[None, :], col[:, None] * inv[None, :]

def _rotate_half(x, ang):
    cos = jnp.cos(ang)[None, :, None, :].astype(x.dtype)
    sin = jnp.sin(ang)[None, :, None, :].astype(x.dtype)
    x1, x2 = jnp.split(x, 2, axis=-1)
    return jnp.concatenate([x1 * cos - x2 * sin, x2 * cos + x1 * sin], axis=-1)

def _axial_rope(x, ang_row, ang_col):
    half = HEAD_DIM // 2
    return jnp.concatenate([_rotate_half(x[..., :half], ang_row), _rotate_half(x[..., half:], ang_col)], axis=-1)

def _attend(q, k, v):
    B, Lq = q.shape[0], q.shape[1]
    nb = Lq // Q_BLOCK
    qb = q.reshape(B, nb, Q_BLOCK, ATTN_KV_HEADS, ATTN_GROUP, HEAD_DIM).transpose(1, 0, 2, 3, 4, 5)
    scale = HEAD_DIM ** -0.5

    def one_block(qblk):
        s = jnp.einsum('bqkgd,bskd->bkgqs', qblk, k).astype(F32) * scale
        p = jax.nn.softmax(s, axis=-1).astype(v.dtype)
        return jnp.einsum('bkgqs,bskd->bqkgd', p, v)

    o = lax.map(one_block, qb)
    return o.transpose(1, 0, 2, 3, 4, 5).reshape(B, Lq, ATTN_WIDTH)

def _forget_gate(z, lb):
    z = z.astype(F32)
    logf = jax.nn.log_sigmoid(z) + jnp.log1p(lb * jnp.exp(jnp.minimum(-z, EXP_CLIP)))
    k = (1.0 - lb) * jax.nn.sigmoid(-z)
    shp = z.shape[:-1] + (HG_HEADS, HG_DK)
    return logf.reshape(shp), k.reshape(shp)

def _chunk_gla(q, k, v, logf, s0):
    B, L, H, DK = q.shape
    DV = v.shape[-1]
    n = L // CHUNK

    def chunks(a):
        return a.reshape(B, n, CHUNK, H, a.shape[-1]).transpose(1, 0, 3, 2, 4)

    lower = jnp.tril(jnp.ones((CHUNK, CHUNK), dtype=bool))[:, :, None]

    def step(S, inp):
        qc, kc, vc, gc = inp
        b = jnp.cumsum(gc, axis=2)
        o_inter = jnp.einsum('bhtk,bhkv->bhtv', qc * jnp.exp(b), S)
        diff = b[:, :, :, None, :] - b[:, :, None, :, :]
        rel = jnp.where(lower, jnp.exp(jnp.minimum(diff, 0.0)), 0.0)
        a = jnp.einsum('bhtk,bhsk,bhtsk->bhts', qc, kc, rel)
        o_intra = jnp.einsum('bhts,bhsv->bhtv', a, vc)
        b_end = b[:, :, -1:, :]
        S = jnp.exp(b_end[:, :, 0, :])[..., None] * S + jnp.einsum('bhsk,bhsv->bhkv', kc * jnp.exp(b_end - b), vc)
        return S, o_inter + o_intra

    S, o = lax.scan(step, s0, (chunks(q), chunks(k), chunks(v), chunks(logf)))
    return o.transpose(1, 0, 3, 2, 4).reshape(B, L, H, DV), S

def _hier_moe(h, w_gr, b_gr, w_er, b_er, w_gate, w_up, w_down):
    B, L, D = h.shape
    t = h.reshape(B * L, D)
    lg = (jnp.einsum('td,dg->tg', t, w_gr) + b_gr).astype(F32)
    pg = jax.nn.softmax(lg, axis=-1)
    g_idx = jnp.argmax(lg, axis=-1)
    g_w = jnp.take_along_axis(pg, g_idx[:, None], axis=-1)
    le = (jnp.einsum('td,de->te', t, w_er) + b_er).astype(F32).reshape(-1, N_GROUPS, EXPERTS_PER_GROUP)
    le_sel = jnp.take_along_axis(le, g_idx[:, None, None], axis=1)[:, 0]
    top_v, top_i = lax.top_k(le_sel, MOE_TOP_K)
    w2 = jax.nn.softmax(top_v, axis=-1) * g_w
    w_in_group = jnp.einsum('tk,tke->te', w2, jax.nn.one_hot(top_i, EXPERTS_PER_GROUP, dtype=F32))
    gate = (jax.nn.one_hot(g_idx, N_GROUPS, dtype=F32)[:, :, None] * w_in_group[:, None, :]).astype(h.dtype)
    out = jnp.zeros_like(t)
    for g in range(N_GROUPS):
        e0 = g * EXPERTS_PER_GROUP
        e1 = e0 + EXPERTS_PER_GROUP
        a = jnp.einsum('td,edf->tef', t, w_gate[e0:e1])
        u = jnp.einsum('td,edf->tef', t, w_up[e0:e1])
        hid = jax.nn.silu(a) * u * gate[:, g, :, None]
        out = out + jnp.einsum('tef,efd->td', hid, w_down[e0:e1])
    return out.reshape(B, L, D)

def _block(x, mods, angles, ctx_k, ctx_v, s_f0, s_b0, lb,
           norm1_w, norm2_w, w_in, q_norm_w, k_norm_w, hg_norm_w, w_ft, w_out,
           w_gr, b_gr, w_er, b_er, w_gate, w_up, w_down):
    shift1, scale1, gate1, shift2, scale2, gate2 = mods
    B, L, _ = x.shape
    h = _rms(x, norm1_w) * (1 + scale1) + shift1
    p = jnp.einsum('bld,de->ble', h, w_in)
    pq, pk, pv, hq, hf_f, hf_b, hi, hg, pft = jnp.split(p, IN_SPLITS, axis=-1)

    q = _rms(pq.reshape(B, L, ATTN_HEADS, HEAD_DIM), q_norm_w)
    k = _rms(pk.reshape(B, L, ATTN_KV_HEADS, HEAD_DIM), k_norm_w)
    v = pv.reshape(B, L, ATTN_KV_HEADS, HEAD_DIM)
    if angles is None:
        kk, vv = k, v
    else:
        q = _axial_rope(q, *angles)
        kk = jnp.concatenate([_axial_rope(k, *angles), ctx_k.astype(k.dtype)], axis=1)
        vv = jnp.concatenate([v, ctx_v.astype(v.dtype)], axis=1)
    o_attn = _attend(q.reshape(B, L, ATTN_KV_HEADS, ATTN_GROUP, HEAD_DIM), kk, vv)

    qh = jax.nn.silu(hq.astype(F32)).reshape(B, L, HG_HEADS, HG_DK)
    vh = hi.astype(F32).reshape(B, L, HG_HEADS, HG_DV)
    logf_f, k_f = _forget_gate(hf_f, lb[0])
    logf_b, k_b = _forget_gate(hf_b, lb[1])
    o_f, s_f = _chunk_gla(qh, k_f, vh, logf_f, s_f0.astype(F32))
    o_b, s_b = _chunk_gla(jnp.flip(qh, 1), jnp.flip(k_b, 1), jnp.flip(vh, 1), jnp.flip(logf_b, 1), s_b0.astype(F32))
    o_h = o_f + jnp.flip(o_b, 1)
    o_h = (_rms(o_h, hg_norm_w) * jax.nn.silu(hg.astype(F32).reshape(B, L, HG_HEADS, HG_DV)))
    o_h = o_h.reshape(B, L, HG_WIDTH).astype(x.dtype)

    xf = pft.astype(F32).reshape(B, L, FT_GROUPS, FT_CH)
    mixed = jnp.real(jnp.fft.fft2(xf, axes=(1, 3), norm='ortho'))
    o_ft = jnp.einsum('blgc,gce->blge', mixed, w_ft.astype(F32)).reshape(B, L, FT_WIDTH).astype(x.dtype)

    mix = jnp.concatenate([o_attn, o_h, o_ft], axis=-1)
    x = x + gate1 * jnp.einsum('blm,md->bld', mix, w_out)
    h2 = _rms(x, norm2_w) * (1 + scale2) + shift2
    x = x + gate2 * _hier_moe(h2, w_gr, b_gr, w_er, b_er, w_gate, w_up, w_down)
    return x, k, v, s_f, s_b

def setup_inputs(seed: int = 0) -> dict:
    key = jax.random.key(seed)
    ks = jax.random.split(key, 32)
    nrm = jax.random.normal
    D = D_MODEL
    return {
        'x_prompt': nrm(ks[0], (BATCH, SEQ, D), F32),
        'x_sample': nrm(ks[1], (DEC_BATCH, DEC_SEQ, D), F32),
        'cache_k': nrm(ks[2], (DEC_BATCH, DEPTH, PAST_LEN, ATTN_KV_HEADS, HEAD_DIM), F32),
        'cache_v': nrm(ks[3], (DEC_BATCH, DEPTH, PAST_LEN, ATTN_KV_HEADS, HEAD_DIM), F32),
        'state_fwd': 0.5 * nrm(ks[4], (DEC_BATCH, DEPTH, HG_HEADS, HG_DK, HG_DV), F32),
        'state_bwd': 0.5 * nrm(ks[5], (DEC_BATCH, DEPTH, HG_HEADS, HG_DK, HG_DV), F32),
        'c': nrm(ks[6], (DEC_BATCH, D), F32),
        'c_ctx': nrm(ks[7], (D,), F32),
        'w_ada': 0.5 * D ** -0.5 * nrm(ks[8], (DEPTH, D, 6 * D), F32),
        'b_ada': 0.01 * nrm(ks[9], (DEPTH, 6 * D), F32),
        'norm1_w': 1.0 + 0.02 * nrm(ks[10], (DEPTH, D), F32),
        'norm2_w': 1.0 + 0.02 * nrm(ks[11], (DEPTH, D), F32),
        'w_in': D ** -0.5 * nrm(ks[12], (DEPTH, D, IN_WIDTH), F32),
        'q_norm_w': 1.0 + 0.02 * nrm(ks[13], (DEPTH, HEAD_DIM), F32),
        'k_norm_w': 1.0 + 0.02 * nrm(ks[14], (DEPTH, HEAD_DIM), F32),
        'hg_lb': 0.5 * nrm(ks[15], (DEPTH, 2, HG_WIDTH), F32),
        'hg_norm_w': 1.0 + 0.02 * nrm(ks[16], (DEPTH, HG_DV), F32),
        'w_ft': FT_CH ** -0.5 * nrm(ks[17], (DEPTH, FT_GROUPS, FT_CH, FT_CH), F32),
        'w_out': MIX_WIDTH ** -0.5 * nrm(ks[18], (DEPTH, MIX_WIDTH, D), F32),
        'w_gr': D ** -0.5 * nrm(ks[19], (DEPTH, D, N_GROUPS), F32),
        'b_gr': 0.01 * nrm(ks[20], (DEPTH, N_GROUPS), F32),
        'w_er': D ** -0.5 * nrm(ks[21], (DEPTH, D, N_EXPERTS), F32),
        'b_er': 0.01 * nrm(ks[22], (DEPTH, N_EXPERTS), F32),
        'w_gate': D ** -0.5 * nrm(ks[23], (DEPTH, N_EXPERTS, D, D_EXPERT), F32),
        'w_up': D ** -0.5 * nrm(ks[24], (DEPTH, N_EXPERTS, D, D_EXPERT), F32),
        'w_down': D_EXPERT ** -0.5 * nrm(ks[25], (DEPTH, N_EXPERTS, D_EXPERT, D), F32),
    }

def reference(x_prompt, x_sample, cache_k, cache_v, state_fwd, state_bwd, c, c_ctx,
              w_ada, b_ada, norm1_w, norm2_w, w_in, q_norm_w, k_norm_w, hg_lb, hg_norm_w,
              w_ft, w_out, w_gr, b_gr, w_er, b_er, w_gate, w_up, w_down):
    lb_soft = jax.nn.softmax(hg_lb.astype(F32), axis=0)
    lower_bounds = jnp.cumsum(lb_soft, axis=0) - lb_soft[0]
    angles = _axial_angles(x_sample.shape[1])
    zero_state = jnp.zeros((x_prompt.shape[0], HG_HEADS, HG_DK, HG_DV), F32)
    hp, hs = x_prompt, x_sample
    ks, vs, sfs, sbs = [], [], [], []
    for l in range(DEPTH):
        lw = (norm1_w[l], norm2_w[l], w_in[l], q_norm_w[l], k_norm_w[l], hg_norm_w[l], w_ft[l], w_out[l],
              w_gr[l], b_gr[l], w_er[l], b_er[l], w_gate[l], w_up[l], w_down[l])
        mods_ctx = _modulation(c_ctx[None, :], w_ada[l], b_ada[l])
        hp, k_l, v_l, sf_l, sb_l = _block(hp, mods_ctx, None, None, None, zero_state, zero_state,
                                          lower_bounds[l], *lw)
        ks.append(k_l)
        vs.append(v_l)
        sfs.append(sf_l)
        sbs.append(sb_l)
        mods_lat = _modulation(c, w_ada[l], b_ada[l])
        hs, _, _, _, _ = _block(hs, mods_lat, angles, cache_k[:, l], cache_v[:, l], state_fwd[:, l],
                                state_bwd[:, l], lower_bounds[l], *lw)
    new_cache_k = jnp.stack(ks, axis=1).astype(x_prompt.dtype)
    new_cache_v = jnp.stack(vs, axis=1).astype(x_prompt.dtype)
    new_state_fwd = jnp.stack(sfs, axis=1).astype(x_prompt.dtype)
    new_state_bwd = jnp.stack(sbs, axis=1).astype(x_prompt.dtype)
    return (hp, hs, new_cache_k, new_cache_v, new_state_fwd, new_state_bwd)


_drawn_inputs = setup_inputs


def setup_inputs(seed=0):
    import zlib

    import numpy as np

    out = dict(_drawn_inputs(seed))
    spreads = {}
    factors = {'cache_k': 4.991,
     'cache_v': 4.945,
     'state_fwd': 8.0,
     'state_bwd': 8.0,
     'b_ada': 2.848,
     'norm2_w': 3.804,
     'q_norm_w': 8.0,
     'k_norm_w': 2.816,
     'hg_norm_w': 8.0,
     'b_gr': 7.465,
     'b_er': 8.0}
    for name, (base, spread) in spreads.items():
        noise = np.random.default_rng([zlib.crc32(name.encode()), seed]).standard_normal(out[name].shape)
        drawn = base * np.exp(spread * noise) if base else spread * noise
        out[name] = __import__('jax').numpy.asarray(drawn.astype(out[name].dtype))
    for name, factor in factors.items():
        out[name] = (out[name] * factor).astype(out[name].dtype)
    return out
```

```python
from contextlib import ExitStack

import concourse.bass as bass
from concourse import mybir

ALU = mybir.AluOpType
ACT = mybir.ActivationFunctionType
AX_X = mybir.AxisListType.X
F32 = mybir.dt.float32
I32 = mybir.dt.int32
U8 = mybir.dt.uint8

P = 128
D = 1024
KC = D // P
DEPTH = 2
NP, NS = 128, 512
TOK = NP + NS
TT = TOK // P
GROUPS = ((0, 0, NP), (1, NP, TOK))
HD = 64
CH = 64
NCH = TOK // CH
PROMPT_CH = NP // CH
HALVES = (32, 16, 8, 4, 2, 1)
NE, TOPK = 16, 2
NEG, EPG = 4, 4
DE = 256
MT = (TOPK * TOK + NE * (P - 1)) // P
SLOTS = MT * P
EPS = 1e-6
IN_W = 2304
BIG = 3.0e38

C_Q, C_K, C_HQ, C_HF, C_HG, C_FT = 0, 4, 5, 7, 11, 13
MIX = (0, 1, 2, 3, 11, 12, 13, 14)

RING = 6
ADA_ITEMS, IN_ITEMS, OUT_ITEMS = 24, 9, 4
PRE = ADA_ITEMS + IN_ITEMS + OUT_ITEMS
PER_LAYER = PRE + 3 * MT

PA_COND, PA_N1, PA_N2, PA_QN, PA_KN, PA_HN, PA_LB, PA_ROWS = 0, 16, 32, 48, 50, 52, 54, 62
PB0 = 64

NU = 8 * TT
N_PARAM_DMAS = 12

CONSTS = ("ident", "blockones", "ones", "rot", "tri", "dft64", "cosT", "sinT",
          "dft_s", "dft_p", "lvl", "restart", "tileno")


def shape_constants():
    import numpy as np
    c = {}
    c["ident"] = np.eye(P, dtype=np.float32)
    bo = np.zeros((P, P), np.float32)
    bo[:64, :64] = 1
    bo[64:, 64:] = 1
    c["blockones"] = bo
    c["ones"] = np.ones((P, P), np.float32)
    rot = np.zeros((P, P), np.float32)
    for m in range(P):
        if m % 32 < 16:
            rot[m + 16, m] = -1.0
        else:
            rot[m - 16, m] = 1.0
    c["rot"] = rot
    c["tri"] = np.triu(np.ones((P, P), np.float32), 1)
    k = np.arange(64)
    th = 2 * np.pi * ((k[:, None] * k[None, :]) % 64) / 64
    d64 = np.zeros((P, 2, P), np.float32)
    for b in range(2):
        d64[64 * b:64 * b + 64, 0, 64 * b:64 * b + 64] = np.cos(th)
        d64[64 * b:64 * b + 64, 1, 64 * b:64 * b + 64] = -np.sin(th)
    c["dft64"] = d64
    half = 32
    inv = (1.0 / (np.float32(10000.0) ** (np.arange(0, half, 2, dtype=np.float32) / np.float32(half)))).astype(np.float32)
    t = np.arange(NS)
    row, col = (t // 64).astype(np.float32), (t % 64).astype(np.float32)
    cosT, sinT = np.zeros((P, NS), np.float32), np.zeros((P, NS), np.float32)
    for p in range(P):
        d = p % 64
        ang = ((row if d < 32 else col) * inv[d % 16]).astype(np.float32)
        cosT[p], sinT[p] = np.cos(ang), np.sin(ang)
    c["cosT"], c["sinT"] = cosT, sinT

    def dft(n):
        i = np.arange(n)
        a = 2 * np.pi * ((i[:, None] * i[None, :]) % n) / n
        s = 1.0 / np.sqrt(n * 64.0)
        both = np.stack([np.cos(a) * s, np.sin(a) * s], 0)
        return both.reshape(2, n // P, P, n).transpose(2, 0, 1, 3).astype(np.float32).copy()
    c["dft_s"], c["dft_p"] = dft(NS), dft(NP)
    lvl = np.zeros((P, 2, len(HALVES), P), np.float32)
    s, q = np.arange(P)[:, None], np.arange(P)[None, :]
    for i, m in enumerate(HALVES):
        same = (s // (2 * m)) == (q // (2 * m))
        lvl[:, 0, i] = same & (s % (2 * m) < m) & (q % (2 * m) >= m)
        lvl[:, 1, i] = same & (s % (2 * m) >= m) & (q % (2 * m) < m)
    c["lvl"] = lvl
    c["restart"] = np.broadcast_to((np.arange(TOK) % CH != 0).astype(np.float32), (P, TOK)).copy()
    tn = np.zeros((P, 64), np.float32)
    tn[:, 0:MT] = np.arange(MT)
    tn[:, 32:36] = np.arange(4)
    tn[:, 40:40 + TT] = np.arange(TT)[None] * P + np.arange(P)[:, None]
    c["tileno"] = tn
    return c


def nth(l, n, i):
    return l * ((n + 1 - i % 2) // 2) + i // 2 + 1


def all_of(eng, sems, l, n, each):
    for i in range(2):
        eng.wait_ge(sems[i], each * nth(l, n, n - 1 if (n - 1) % 2 == i else n - 2))


def _proj_unit(u):
    def pair(ps):
        return ps[:, 1024 * (u % 3):1024 * (u % 3) + 1024]
    if u == 5:
        return lambda pT, v, i, ps: (v[:, :, :], pair(ps)[:, 0:TOK].rearrange("p (t e) -> p t e", t=TT))
    if u == 12:
        return lambda pT, v, i, ps: (i[:, 0:4, :], pair(ps).rearrange("p (t e) -> p t e", t=4))
    if u == 13:
        return lambda pT, v, i, ps: (i[:, 4, :], pair(ps)[:, 0:256])
    c = u if u < 5 else u - 1 if u < 12 else u - 3
    return lambda pT, v, i, ps: (pT[:, c, :], pair(ps)[:, 0:TOK])


PROJ_EVAC = [_proj_unit(u) for u in range(18)]


def build_program(nc, A, C, outs):
    y_prompt, y_sample, o_ck, o_cv, o_sf, o_sb = outs
    ctx = ExitStack()
    with ctx:
        def sb(name, shape, dt=F32):
            return ctx.enter_context(nc.sbuf_tensor(name, shape, dt))

        def sem(name):
            return ctx.enter_context(nc.semaphore(name))

        K = {n: sb("c_" + n, list(C[n].shape), U8 if n == "lvl" else F32) for n in CONSTS}
        ident, blockones, ones, rot, tri = (K[n] for n in ("ident", "blockones", "ones", "rot", "tri"))

        xT = sb("xT", [P, KC, TOK])
        hT = sb("hT", [P, KC, TOK])
        hT_flat = hT[:, :, :].rearrange("p k t -> p (k t)")
        xrow = hT_flat.rearrange("p (t d) -> p t d", t=TT)
        pT = sb("pT", [P, 15, TOK])
        pT_flat = pT[:, :, :].rearrange("p k t -> p (k t)")
        v_tok = sb("v_tok", [P, TT, P])
        i_tok = sb("i_tok", [P, TT, 256])
        ring = sb("ring", [P, RING, 2048])
        rows = sb("rows", [P, 2, P])
        par = sb("par", [P, 160])
        cond = sb("cond", [P, 2, KC])
        csc = sb("csc", [P, 2, 16])
        lbt = sb("lbt", [P, 4, 4])
        lb = sb("lb", [P, DEPTH, 4])
        omlb = sb("omlb", [P, DEPTH, 4])
        eps_t = sb("eps_t", [P, 1])
        ck_row = sb("ck_row", [P, DEPTH, P])
        ckT = sb("ckT", [P, DEPTH, P])
        cv_tok = sb("cv_tok", [P, DEPTH, P])
        wr = sb("wr", [P, DEPTH, KC, NEG + NE])
        br = sb("br", [1, DEPTH, NEG + NE])
        wft = sb("wft", [P, DEPTH, 2, P])
        s_init = sb("s_init", [P, DEPTH, 2, 2, P])
        mods = sb("mods", [P, DEPTH, 6, KC, 2])
        amul = sb("amul", [P, DEPTH, 2, KC, 2])
        scr = sb("scr", [P, 12, TOK])
        scr_flat = scr[:, :, :].rearrange("p k t -> p (k t)")
        st = sb("st", [P, 2, 8])
        kout = sb("kout", [P, P])
        rt = scr_flat[:, 6144:6844]
        slot_i = sb("slot_i", [P, TT, TOPK], I32)
        slot_tok = sb("slot_tok", [P, MT], I32)
        tokid = sb("tokid", [P, TT], I32)
        zeros_i = sb("zeros_i", [P, MT], I32)
        tile_e = sb("tile_e", [P, 32], I32)
        wgt = sb("wgt", [P, TT, TOPK])

        S = hT_flat[:, 0:9 * P].rearrange("p (n v) -> p n v", v=P)
        aT = hT_flat[:, 1280:2560].rearrange("p (n v) -> p n v", v=P)
        decayed = hT_flat[:, 2560:5120].rearrange("p (n v) -> p n v", v=TOK)
        lvl_f = pT_flat[:, 0:2 * len(HALVES) * P].rearrange("p (d i t) -> p d i t", d=2, t=P)
        xg = pT_flat[:, 0:2048].rearrange("p (b d) -> p b d", b=2)
        xgT = pT_flat[:, 2048:4096].rearrange("p (b k t) -> p b k t", b=2, k=KC)
        sg = pT_flat[:, 4096:4608].rearrange("p (b f) -> p b f", b=2)
        hid = pT_flat[:, 4608:5120].rearrange("p (b f) -> p b f", b=2)
        hidT = pT_flat[:, 5120:5632].rearrange("p (b k t) -> p b k t", b=2, k=2)
        yb = pT_flat[:, 5632:7680].rearrange("p (b d) -> p b d", b=2)
        hrow = scr_flat[:, 0:2048].rearrange("p (b d) -> p b d", b=2)
        y1 = scr_flat[:, 2048:4096].rearrange("p (b d) -> p b d", b=2)
        y2 = scr_flat[:, 4096:6144].rearrange("p (b d) -> p b d", b=2)

        ps = ctx.enter_context(nc.psum_tensor("ps", [P, 8 * 512], F32))

        def bank(b, n=512, off=0):
            return ps[:, b * 512 + off:b * 512 + off + n]

        h_dram = nc.dram_tensor("h_rows", (TOK, D), F32).ap()
        table = nc.dram_tensor("slot_table", (SLOTS, 1), I32).ap()
        y_dram = nc.dram_tensor("y_rows", (SLOTS, D), F32).ap()

        consts_in = sem("consts_in"); params_in = sem("params_in"); x_in = sem("x_in")
        late_in = sem("late_in")
        slot_in = [sem(f"slot_in{i}") for i in range(RING)]
        ada_ps = sem("ada_ps"); gate_ps = sem("gate_ps")
        zero_done = sem("zero_done")
        xt_ps = sem("xt_ps"); xt_act = sem("xt_act"); xt_dve = sem("xt_dve")
        par_ps = sem("par_ps"); par_sb = sem("par_sb")
        cond_e = sem("cond_e"); cond_ok = sem("cond_ok"); lb_d = sem("lb_d"); lb_e = sem("lb_e")
        mods_ok = sem("mods_ok")
        nsq = sem("nsq"); nsum = sem("nsum"); nrs = sem("nrs"); nscaled = sem("nscaled"); h_ok = sem("h_ok")
        proj_ps = sem("proj_ps"); proj_act = sem("proj_act"); proj_dve = sem("proj_dve")
        qsq = sem("qsq"); qsum = sem("qsum"); qrs = sem("qrs"); qnorm = sem("qnorm")
        qrot = sem("qrot"); qcos = sem("qcos"); qk_ok = sem("qk_ok")
        ck_ps = sem("ck_ps"); ck_sb = sem("ck_sb"); cache_out = sem("cache_out"); ko_sb = sem("ko_sb"); rt_e = sem("rt_e")
        sc_ps = sem("sc_ps"); sc_max = sem("sc_max"); sc_exp = sem("sc_exp"); sc_norm = sem("sc_norm")
        pt_ps = sem("pt_ps"); pt_sb = sem("pt_sb"); av_ps = sem("av_ps"); av_sb = sem("av_sb")
        sl_e = sem("sl_e"); sl_ok = sem("sl_ok")
        gt_in = sem("gt_in"); gt_e = sem("gt_e"); gt_den = sem("gt_den"); gt_ln = sem("gt_ln"); gt_ok = sem("gt_ok")
        dk_d = sem("dk_d"); dk_e = sem("dk_e"); dk_ok = sem("dk_ok")
        lv_d = sem("lv_d"); lv_e = sem("lv_e"); lv_ok = sem("lv_ok")
        g_ps = sem("g_ps"); mid_ps = sem("mid_ps"); g_used = sem("g_used"); s_ok = sem("s_ok")
        inter_ps = sem("inter_ps"); intra_ps = sem("intra_ps")
        on_sq = sem("on_sq"); on_sum = sem("on_sum"); on_rs = sem("on_rs"); on_ok = sem("on_ok")
        state_out = sem("state_out")
        f_ab = sem("f_ab"); f_abs = sem("f_abs"); f_z = sem("f_z"); f_zs = sem("f_zs"); f_o = sem("f_o"); f_os = sem("f_os")
        op_ps = sem("op_ps"); x_mid = sem("x_mid")
        lg_ps = sem("lg_ps"); rt_m = sem("rt_m"); rk_ps = sem("rk_ps"); rt_ok = sem("rt_ok")
        hr_ps = sem("hr_ps"); hr_sb = sem("hr_sb"); hr_out = [sem(f"hr_out{i}") for i in range(2)]
        tb_zero = sem("tb_zero"); tb_out = sem("tb_out"); tb_in = sem("tb_in")
        xg_in = [sem(f"xg_in{i}") for i in range(2)]; xg_ps = sem("xg_ps"); xg_sb = sem("xg_sb")
        gu_ps = sem("gu_ps"); gu_s = sem("gu_s"); hid_ok = sem("hid_ok"); hid_ps = sem("hid_ps"); hid_sb = sem("hid_sb")
        dn_ps = sem("dn_ps"); dn_sb = sem("dn_sb"); y_out = [sem(f"y_out{i}") for i in range(2)]
        y_in = [sem(f"y_in{i}") for i in range(2)]; y_sum = sem("y_sum"); yt_ps = sem("yt_ps"); x_new = sem("x_new")
        fin_ps = sem("fin_ps"); fin_sb = sem("fin_sb"); fin_out = sem("fin_out")
        dve_step = sem("dve_step"); act_step = sem("act_step"); pool_step = sem("pool_step")

        N_CONST = len(CONSTS) - 1

        def item_dmas(i):
            if i < ADA_ITEMS:
                return 1
            if i < ADA_ITEMS + 2:
                return 4
            if i < ADA_ITEMS + IN_ITEMS:
                return 1
            return 3 if i < PRE else 1

        landed, slot_total = [], [0] * RING
        for n in range(DEPTH * PER_LAYER):
            slot_total[n % RING] += 16 * item_dmas(n % PER_LAYER)
            landed.append(slot_total[n % RING])

        def multiplied(n):
            l, i = n // PER_LAYER, n % PER_LAYER
            if i < ADA_ITEMS:
                return ada_ps, l * ADA_ITEMS + i + 1
            i -= ADA_ITEMS
            if i < IN_ITEMS:
                return proj_ps, 2 * (l * IN_ITEMS + i + 1)
            i -= IN_ITEMS
            if i < OUT_ITEMS:
                return op_ps, 2 * (l * OUT_ITEMS + i + 1)
            i -= OUT_ITEMS
            return (gate_ps, gu_ps, dn_ps)[i % 3], l * MT + i // 3 + 1

        def slot(n):
            return ring[:, n % RING, :]

        def x_whole(eng, l):
            if l == 0:
                eng.wait_ge(xt_act, 3)
                eng.wait_ge(xt_dve, 2)
            else:
                eng.wait_ge(x_new, KC * TT * l)

        block = ctx.enter_context(nc.Block())

        @block.sync
        def _(sp):
            sp.dma_start(K["ident"][:], C["ident"]).then_inc(x_in, 16)
            sp.dma_start(xrow[:, 0, :], A["x_prompt"][0]).then_inc(x_in, 16)
            sp.dma_start(xrow[:, 1:TT, :], A["x_sample"][0].rearrange("(t p) d -> p t d", p=P)).then_inc(x_in, 16)
            for n in CONSTS[1:]:
                sp.dma_start(lvl_f if n == "lvl" else K[n][:], C[n]).then_inc(consts_in, 16)

            def next_item(n):
                if n >= RING:
                    sp.wait_ge(*multiplied(n - RING))
                return slot(n), slot_in[n % RING]

            for l in range(DEPTH):
                base = l * PER_LAYER
                for i in range(ADA_ITEMS):
                    dst, s = next_item(base + i)
                    sp.dma_start(dst.rearrange("p (k n) -> p k n", k=KC),
                                 A["w_ada"][l].rearrange("(k p) n -> p k n", p=P)[:, :, 256 * i:256 * i + 256]).then_inc(s, 16)
                w_in = A["w_in"][l].rearrange("(k p) n -> p k n", p=P)
                for i in range(IN_ITEMS):
                    dst, s = next_item(base + ADA_ITEMS + i)
                    if i < 2:
                        view = dst.rearrange("p (k c b j) -> p k c b j", k=KC, c=2, b=2)
                        for b in range(2):
                            for c in range(2):
                                at = 256 * b + 128 * i + 64 * c
                                sp.dma_start(view[:, :, c, b, :], w_in[:, :, at:at + 64]).then_inc(s, 16)
                    else:
                        sp.dma_start(dst.rearrange("p (k n) -> p k n", k=KC),
                                     w_in[:, :, 256 * i:256 * i + 256]).then_inc(s, 16)
                w_out = A["w_out"][l]
                for i in range(OUT_ITEMS):
                    dst, s = next_item(base + ADA_ITEMS + IN_ITEMS + i)
                    view = dst.rearrange("p (k n) -> p k n", k=KC)
                    for b in range(2):
                        sp.dma_start(view[64 * b:64 * b + 64, 0:4, :],
                                     w_out[256 * b:256 * b + 256, 256 * i:256 * i + 256]
                                     .rearrange("(c p) n -> p c n", p=64)).then_inc(s, 16)
                    sp.dma_start(view[:, 4:8, :], w_out[512:1024, 256 * i:256 * i + 256]
                                 .rearrange("(c p) n -> p c n", p=P)).then_inc(s, 16)
                sp.wait_ge(rt_ok, l + 1)
                for j in range(MT):
                    e = sp.value_load(tile_e[0:1, j:j + 1], min_val=0, max_val=NE - 1)
                    for w, name in enumerate(("w_gate", "w_up")):
                        dst, s = next_item(base + PRE + 3 * j + w)
                        sp.dma_start(dst.rearrange("p (k n) -> p k n", k=KC),
                                     A[name][l, bass.ds(e, 1)].rearrange("e (k p) n -> p (e k) n", p=P)).then_inc(s, 16)
                    dst, s = next_item(base + PRE + 3 * j + 2)
                    sp.dma_start(dst.rearrange("p (k n) -> p k n", k=2),
                                 A["w_down"][l, bass.ds(e, 1)].rearrange("e (k p) n -> p (e k) n", p=P)).then_inc(s, 16)
            sp.wait_ge(cache_out, 16 * 2 * DEPTH)
            sp.wait_ge(state_out, 16 * 8 * DEPTH)
            all_of(sp, hr_out, DEPTH - 1, TT, 16)
            sp.wait_ge(tb_zero, 16 * DEPTH)
            sp.wait_ge(tb_out, 16 * TT * TOPK * DEPTH)
            all_of(sp, y_out, DEPTH - 1, MT, 16)
            sp.wait_ge(fin_out, 16 * TT)

        @block.gpsimd
        def _(pool):
            steps = [0]

            def seq(ins):
                steps[0] += 1
                ins.then_inc(pool_step, 1)
                pool.wait_ge(pool_step, steps[0])

            nc.gpsimd.memset(wft[:], 0.0).then_inc(zero_done, 1)
            nc.gpsimd.memset(s_init[:], 0.0).then_inc(zero_done, 1)
            nc.gpsimd.memset(eps_t[:], EPS).then_inc(zero_done, 1)
            nc.gpsimd.memset(zeros_i[:], 0).then_inc(zero_done, 1)
            pool.wait_ge(zero_done, 4)
            for l in range(DEPTH):
                for g in range(4):
                    h = 64 * (g % 2)
                    pool.dma_start(wft[h:h + 64, l, g // 2, h:h + 64], A["w_ft"][l, g]).then_inc(late_in, 16)
                    for d, name in enumerate(("state_fwd", "state_bwd")):
                        pool.dma_start(s_init[h:h + 64, l, d, g // 2, h:h + 64], A[name][0, l, g]).then_inc(late_in, 16)
                pool.dma_start(wr[:, l, :, 0:NEG], A["w_gr"][l].rearrange("(k p) g -> p k g", p=P)).then_inc(late_in, 16)
                pool.dma_start(wr[:, l, :, NEG:], A["w_er"][l].rearrange("(k p) g -> p k g", p=P)).then_inc(late_in, 16)
                pool.dma_start(br[0:1, l, 0:NEG], A["b_gr"][l:l + 1]).then_inc(late_in, 16)
                pool.dma_start(br[0:1, l, NEG:], A["b_er"][l:l + 1]).then_inc(late_in, 16)
            pool.wait_ge(consts_in, 16 * N_CONST)

            for l in range(DEPTH):
                for c in range(5):
                    n = l * 5 + c
                    pool.wait_ge(qnorm, n + 1)
                    if n >= 2:
                        pool.wait_ge(qk_ok, n - 1)
                    nc.gpsimd.tensor_tensor(scr[:, 2 + c % 2, 0:NS], pT[:, c, NP:], K["cosT"][:], ALU.mult).then_inc(qcos, 1)
                for p in range(2):
                    for d in range(2):
                        u = (l * 2 + p) * 2 + d
                        if p == 0 and d == 0:
                            pool.wait_ge(gt_ok, 4 * l + 4)
                        b = pT[:, C_HF + 2 * d + p, :]
                        for i, m in enumerate(HALVES):
                            n = u * 6 + i
                            if n >= 2:
                                pool.wait_ge(lv_ok, 2 * (n - 1))
                            bv = b.rearrange("p (n m) -> p n m", m=2 * m)
                            dv = scr[:, 2 + i % 2, :].rearrange("p (n m) -> p n m", m=2 * m)
                            nb = TOK // (2 * m)
                            if d == 0:
                                ref = bv[:, :, m - 1:m].to_broadcast([P, nb, m])
                                q, k = slice(m, 2 * m), slice(0, m)
                            else:
                                ref = bv[:, :, m:m + 1].to_broadcast([P, nb, m])
                                q, k = slice(0, m), slice(m, 2 * m)
                            nc.gpsimd.tensor_tensor(dv[:, :, q], bv[:, :, q], ref, ALU.subtract).then_inc(lv_d, 1)
                            nc.gpsimd.tensor_tensor(dv[:, :, k], ref, bv[:, :, k], ALU.subtract).then_inc(lv_d, 1)
                if l > 0:
                    pool.wait_ge(tb_in, 16 * l)
                pool.dma_start(table.rearrange("(p j) o -> p (j o)", p=P), zeros_i[:]).then_inc(tb_zero, 16)
                pool.wait_ge(tb_zero, 16 * (l + 1))
                pool.wait_ge(rt_ok, l + 1)
                for t in range(TT):
                    for c in range(TOPK):
                        pool.indirect_dma_start(table, bass.IndirectOffsetOnAxis(ap=slot_i[:, t, c:c + 1], axis=0),
                                                tokid[:, t:t + 1], None).then_inc(tb_out, 16)
                pool.wait_ge(tb_out, 16 * TT * TOPK * (l + 1))
                pool.dma_start(slot_tok[:], table.rearrange("(j p) o -> p (j o)", p=P), allow_slow_non_contiguous=True).then_inc(tb_in, 16)
                pool.wait_ge(tb_in, 16 * (l + 1))
                all_of(pool, hr_out, l, TT, 16)
                for j in range(MT):
                    n = l * MT + j
                    if n >= 2:
                        pool.wait_ge(xg_ps, n - 1)
                    if j == 0:
                        pool.wait_ge(x_mid, 2 * KC * (l + 1))
                    pool.indirect_dma_start(xg[:, j % 2, :], None, h_dram,
                                            bass.IndirectOffsetOnAxis(ap=slot_tok[:, j:j + 1], axis=0)).then_inc(xg_in[j % 2], 16)
                all_of(pool, y_out, l, MT, 16)
                for t in range(TT):
                    n = l * TT + t
                    if n >= 2:
                        pool.wait_ge(y_sum, n - 1)
                    for c, dst in enumerate((y1, y2)):
                        if t >= 2 and c == 1:
                            pool.wait_ge(yt_ps, n - 1)
                        pool.indirect_dma_start(dst[:, t % 2, :], None, y_dram,
                                                bass.IndirectOffsetOnAxis(ap=slot_i[:, t, c:c + 1], axis=0)).then_inc(y_in[t % 2], 16)

        @block.scalar
        def _(act):
            steps = [0]

            def seq(ins):
                steps[0] += 1
                ins.then_inc(act_step, 1)
                act.wait_ge(act_step, steps[0])

            def A_(out, in_, f, **kw):
                return nc.scalar.activation(out, in_, f, **kw)

            r0 = rows[:, 0, :]
            n_par = 0
            for src, at, cnt in (("c_ctx", PA_COND, 8), ("c", PA_COND + 8, 8)):
                v = A[src] if src == "c_ctx" else A[src][0]
                act.dma_start(r0[at:at + cnt, :], v.rearrange("(k p) -> k p", p=P)).then_inc(params_in, 16)
                n_par += 1
            for src, at in (("norm1_w", PA_N1), ("norm2_w", PA_N2)):
                act.dma_start(r0[at:at + 16, :], A[src].rearrange("l (k p) -> (l k) p", p=P)).then_inc(params_in, 16)
                n_par += 1
            for src, at in (("q_norm_w", PA_QN), ("k_norm_w", PA_KN), ("hg_norm_w", PA_HN)):
                for b in range(2):
                    act.dma_start(r0[at:at + 2, 64 * b:64 * b + 64], A[src]).then_inc(params_in, 16)
                    n_par += 1
            act.dma_start(r0[PA_LB:PA_LB + 8, :], A["hg_lb"].rearrange("l d (k p) -> (l d k) p", p=P)).then_inc(params_in, 16)
            act.dma_start(rows[0:96, 1, :], A["b_ada"].rearrange("l (k p) -> (l k) p", p=P)).then_inc(params_in, 16)
            n_par += 2
            assert n_par == N_PARAM_DMAS
            for l in range(DEPTH):
                act.dma_start(ck_row[:, l, :], A["cache_k"][0, l].rearrange("t h d -> t (h d)")).then_inc(params_in, 16)
                act.dma_start(cv_tok[:, l, :], A["cache_v"][0, l].rearrange("t h d -> t (h d)")).then_inc(params_in, 16)

            act.wait_ge(par_sb, 1)
            A_(csc[:, 0, :], par[:, PA_COND:PA_COND + 16], ACT.Exp, scale=-1.0).then_inc(cond_e, 1)
            act.wait_ge(lb_d, 1)
            A_(lbt[:, 1, :], lbt[:, 0, :], ACT.Exp).then_inc(lb_e, 1)
            A_(lbt[:, 3, :], lbt[:, 2, :], ACT.Exp).then_inc(lb_e, 1)
            for t in range(TT):
                if t % 2 == 0:
                    act.wait_ge(xt_ps, t + 1)
                    A_(xT[:, :, t * P:(t + 1) * P], ps[:, 0:1024].rearrange("p (k t) -> p k t", k=KC), ACT.Copy).then_inc(xt_act, 1)

            def norm(l, which):
                n0 = (l * 2 + which) * KC
                for k in range(KC):
                    if n0 + k >= 2:
                        act.wait_ge(nsum, n0 + k - 1)
                    if which == 0:
                        x_whole(act, l)
                    else:
                        act.wait_ge(x_mid, l * 2 * KC + 2 * (k + 1))
                    A_(scr[:, k % 2, :], xT[:, k, :], ACT.Square).then_inc(nsq, 1)
                act.wait_ge(nsum, n0 + KC)
                rs = scr[:, 2, :]
                seq(A_(rs[:, 0:NS], bank(5), ACT.Ln, scale=1.0 / D, bias=eps_t[:, 0:1]))
                seq(A_(rs[:, NS:], bank(6, NP), ACT.Ln, scale=1.0 / D, bias=eps_t[:, 0:1]))
                A_(rs, rs, ACT.Exp, scale=-0.5).then_inc(nrs, 1)
                for k in range(KC):
                    act.wait_ge(nscaled, 2 * (n0 + k + 1))
                    for g, a, b in GROUPS:
                        A_(hT[:, k, a:b], hT[:, k, a:b], ACT.Identity,
                           bias=mods[:, l, 3 * which, k, g:g + 1]).then_inc(h_ok, 1)

            act.wait_ge(zero_done, 4)
            for l in range(DEPTH):
                act.wait_ge(mods_ok, l + 1)
                norm(l, 0)

                for u in range(0, 18, 2):
                    act.wait_ge(proj_ps, 18 * l + u + 1)
                    dst, src = PROJ_EVAC[u](pT, v_tok, i_tok, ps)
                    A_(dst, src, ACT.Copy).then_inc(proj_act, 1)
                act.wait_ge(proj_act, 9 * (l + 1))
                act.wait_ge(proj_dve, 9 * (l + 1))
                act.dma_start(o_cv[0, l].rearrange("t h d -> t (h d)"), v_tok[:, 0, :]).then_inc(cache_out, 16)

                for c in range(5):
                    n = l * 5 + c
                    r = scr[:, c % 2, :]
                    if n >= 2:
                        act.wait_ge(qnorm, n - 1)
                    A_(r, pT[:, c, :], ACT.Square).then_inc(qsq, 1)
                    act.wait_ge(qsum, n + 1)
                    seq(A_(r, ps[:, 1024 * (c % 2):1024 * (c % 2) + TOK], ACT.Ln, scale=1.0 / HD, bias=eps_t[:, 0:1]))
                    A_(r, r, ACT.Exp, scale=-0.5).then_inc(qrs, 1)
                act.wait_ge(ck_ps, l + 1)
                if l > 0:
                    act.wait_ge(cache_out, 16 * 2 * l)
                A_(kout[:], bank(6, P), ACT.Copy).then_inc(ko_sb, 1)
                act.wait_ge(ko_sb, l + 1)
                act.dma_start(o_ck[0, l].rearrange("t h d -> t (h d)"), kout[:]).then_inc(cache_out, 16)

                for i in range(NU + 1):
                    if i < NU:
                        n = l * NU + i
                        w = P if i % TT == 0 else TOK
                        act.wait_ge(sc_max, n + 1)
                        if n >= 2:
                            act.wait_ge(pt_ps, n - 1)
                        A_(scr[:, 4 + i % 2, 0:w], ps[:, 1024 * (i % 2):1024 * (i % 2) + w], ACT.Exp,
                           scale=HD ** -0.5, bias=st[:, i % 2, 1:2], accum_out=st[:, i % 2, 2:3]).then_inc(sc_exp, 1)
                    if i >= 1:
                        n = l * NU + i - 1
                        w = P if (i - 1) % TT == 0 else TOK
                        act.wait_ge(pt_ps, n + 1)
                        if n >= 2:
                            act.wait_ge(av_ps, n - 1)
                        A_(scr[:, 6 + (i - 1) % 2, 0:w], ps[:, 2048:2048 + w], ACT.Copy).then_inc(pt_sb, 1)

                for i, c in enumerate((C_HQ, C_HQ + 1, C_HG, C_HG + 1)):
                    n = 4 * l + i
                    if n >= 2:
                        act.wait_ge(sl_ok, n - 1)
                    A_(scr[:, i % 2, :], pT[:, c, :], ACT.Exp, scale=-1.0).then_inc(sl_e, 1)
                for i in range(4):
                    n = 4 * l + i
                    act.wait_ge(gt_in, 2 * (n + 1))
                    for j in range(2):
                        A_(scr[:, 2 + j, :], scr[:, 4 + j, :], ACT.Exp).then_inc(gt_e, 1)
                    act.wait_ge(gt_den, n + 1)
                    A_(scr[:, 6, :], scr[:, 7, :], ACT.Ln).then_inc(gt_ln, 1)
                    if l > 0:
                        A_(scr[:, 8, :], scr[:, 9, :], ACT.Ln).then_inc(gt_ln, 1)
                for p in range(2):
                    for d in range(2):
                        u = (l * 2 + p) * 2 + d
                        act.wait_ge(gt_ok, 4 * l + 4)
                        if u >= 1:
                            act.wait_ge(inter_ps, u)
                            act.wait_ge(s_ok, u)
                        A_(scr[:, 8, :], pT[:, C_HF + 2 * d + p, :], ACT.Exp).then_inc(dk_e, 1)
                        act.wait_ge(dk_d, u + 1)
                        A_(scr[:, 10, :], scr[:, 10, :], ACT.Exp).then_inc(dk_e, 1)
                        for i in range(6):
                            n = u * 6 + i
                            act.wait_ge(lv_d, 2 * (n + 1))
                            A_(scr[:, 2 + i % 2, :], scr[:, 2 + i % 2, :], ACT.Exp).then_inc(lv_e, 1)
                        act.wait_ge(s_ok, u + 1)
                        for h in range(2):
                            hs = slice(64 * h, 64 * h + 64)
                            act.dma_start((o_sf, o_sb)[d][0, l, 2 * p + h], S[hs, 1, hs]).then_inc(state_out, 16)
                    n = 2 * l + p
                    act.wait_ge(intra_ps, 2 * n + 2)
                    r = scr[:, 0, :]
                    A_(r, ps[:, 3072:3072 + TOK], ACT.Square).then_inc(on_sq, 1)
                    act.wait_ge(on_sum, n + 1)
                    seq(A_(r, ps[:, 0:TOK], ACT.Ln, scale=1.0 / HD, bias=eps_t[:, 0:1]))
                    A_(r, r, ACT.Exp, scale=-0.5).then_inc(on_rs, 1)
                for p in range(2):
                    n = 2 * l + p
                    act.wait_ge(f_o, n + 1)
                    A_(pT[:, C_FT + p, NP:], bank(6), ACT.Copy).then_inc(f_os, 1)
                    A_(pT[:, C_FT + p, 0:NP], bank(7, NP), ACT.Copy).then_inc(f_os, 1)

                norm(l, 1)
                for t in range(TT):
                    n = l * TT + t
                    act.wait_ge(hr_ps, n + 1)
                    if nth(l, TT, t) > 1:
                        act.wait_ge(hr_out[t % 2], 16 * (nth(l, TT, t) - 1))
                    A_(hrow[:, t % 2, :], ps[:, 1024 * (t % 2):1024 * (t % 2) + D], ACT.Copy).then_inc(hr_sb, 1)
                    act.wait_ge(hr_sb, n + 1)
                    act.dma_start(h_dram[t * P:(t + 1) * P, :], hrow[:, t % 2, :]).then_inc(hr_out[t % 2], 16)

                act.wait_ge(rt_m, 2 * l + 1)
                A_(rt[:, 130:150], rt[:, 130:150], ACT.Exp).then_inc(rt_e, 1)
                A_(rt[:, 360:365], rt[:, 360:365], ACT.Exp).then_inc(rt_e, 1)

                for i in range(MT + 2):
                    if i < MT:
                        n = l * MT + i
                        act.wait_ge(xg_ps, n + 1)
                        if n >= 2:
                            act.wait_ge(gu_ps, n - 1)
                        A_(xgT[:, i % 2], ps[:, 0:1024].rearrange("p (k t) -> p k t", k=KC), ACT.Copy).then_inc(xg_sb, 1)
                    if 1 <= i <= MT:
                        n = l * MT + i - 1
                        j = (i - 1) % 2
                        act.wait_ge(gu_ps, n + 1)
                        if n >= 2:
                            act.wait_ge(hid_ok, n - 1)
                        A_(sg[:, j, :], bank(2 + j, DE), ACT.Silu).then_inc(gu_s, 1)
                    if i >= 2:
                        n = l * MT + i - 2
                        j = (i - 2) % 2
                        act.wait_ge(dn_sb, n + 1)
                        act.dma_start(y_dram[(i - 2) * P:(i - 1) * P, :], yb[:, j, :]).then_inc(y_out[j], 16)

            for t in range(TT):
                act.wait_ge(fin_ps, t + 1)
                A_(xrow[:, t, :], ps[:, 1024 * (t % 2):1024 * (t % 2) + D], ACT.Copy).then_inc(fin_sb, 1)
                act.wait_ge(fin_sb, t + 1)
                dst = y_prompt[0] if t == 0 else y_sample[0, (t - 1) * P:t * P, :]
                act.dma_start(dst, xrow[:, t, :]).then_inc(fin_out, 16)

        @block.vector
        def _(dve):
            steps = [0]
            V = nc.vector

            def seq(ins):
                steps[0] += 1
                ins.then_inc(dve_step, 1)
                dve.wait_ge(dve_step, steps[0])

            dve.wait_ge(par_ps, 3)
            V.tensor_copy(ckT[:], bank(5, 2 * P).rearrange("p (l t) -> p l t", l=2)).then_inc(ck_sb, 1)
            seq(V.tensor_copy(par[:, PB0:PB0 + 96], bank(4, 96, PB0)))
            V.tensor_copy(par[:, 0:PA_ROWS], bank(4, PA_ROWS)).then_inc(par_sb, 1)
            dve.wait_ge(cond_e, 1)
            dve.wait_ge(par_sb, 1)
            seq(V.tensor_scalar(csc[:, 0, :], csc[:, 0, :], 1.0, None, ALU.add))
            seq(V.reciprocal(csc[:, 1, :], csc[:, 0, :]))
            V.tensor_tensor(cond[:].rearrange("p g k -> p (g k)"), par[:, PA_COND:PA_COND + 16], csc[:, 1, :],
                            ALU.mult).then_inc(cond_ok, 1)
            l0, l1 = par[:, PA_LB:PA_LB + 4], par[:, PA_LB + 4:PA_LB + 8]
            seq(V.tensor_tensor(lb[:, 0, :], l0, l1, ALU.max))
            seq(V.tensor_tensor(lbt[:, 0, :], l0, lb[:, 0, :], ALU.subtract))
            V.tensor_tensor(lbt[:, 2, :], l1, lb[:, 0, :], ALU.subtract).then_inc(lb_d, 1)
            dve.wait_ge(lb_e, 2)
            seq(V.tensor_tensor(lbt[:, 0, :], lbt[:, 1, :], lbt[:, 3, :], ALU.add))
            seq(V.reciprocal(lbt[:, 2, :], lbt[:, 0, :]))
            seq(V.tensor_tensor(lb[:, 1, :], lbt[:, 3, :], lbt[:, 2, :], ALU.mult))
            seq(V.memset(lb[:, 0, :], 0.0))
            seq(V.tensor_scalar(omlb[:], lb[:], -1.0, 1.0, ALU.mult, ALU.add))
            for t in range(TT):
                if t % 2 == 1:
                    dve.wait_ge(xt_ps, t + 1)
                    V.tensor_copy(xT[:, :, t * P:(t + 1) * P], ps[:, 1024:2048].rearrange("p (k t) -> p k t", k=KC)).then_inc(xt_dve, 1)
            dve.wait_ge(consts_in, 16 * N_CONST)
            seq(V.tensor_copy(tokid[:], K["tileno"][:, 40:40 + TT]))
            seq(V.tensor_copy(K["lvl"][:], lvl_f))

            def norm(l, which):
                n0 = (l * 2 + which) * KC
                dve.wait_ge(nrs, 2 * l + which + 1)
                rs = scr[:, 2, :]
                for k in range(KC):
                    for g, a, b in GROUPS:
                        r = rs[:, NS:] if g == 0 else rs[:, 0:NS]
                        V.scalar_tensor_tensor(hT[:, k, a:b], xT[:, k, a:b], amul[:, l, which, k, g:g + 1], r,
                                               ALU.mult, ALU.mult).then_inc(nscaled, 1)

            for l in range(DEPTH):
                dve.wait_ge(ada_ps, (l + 1) * ADA_ITEMS)
                bias = par[:, PB0 + 48 * l:PB0 + 48 * l + 48].unsqueeze(2).to_broadcast([P, 48, 2])
                seq(V.tensor_tensor(mods[:, l].rearrange("p s k g -> p (s k) g"),
                                    bank(7, 96).rearrange("p (n g) -> p n g", g=2), bias, ALU.add))
                for which, at in ((0, PA_N1), (1, PA_N2)):
                    w = par[:, at + 8 * l:at + 8 * l + 8].unsqueeze(2).to_broadcast([P, KC, 2])
                    ins = V.scalar_tensor_tensor(amul[:, l, which], mods[:, l, 3 * which + 1], 1.0, w, ALU.add, ALU.mult)
                    if which == 0:
                        seq(ins)
                    else:
                        ins.then_inc(mods_ok, 1)
                        dve.wait_ge(mods_ok, l + 1)
                x_whole(dve, l)
                norm(l, 0)

                for u in range(1, 18, 2):
                    dve.wait_ge(proj_ps, 18 * l + u + 1)
                    dst, src = PROJ_EVAC[u](pT, v_tok, i_tok, ps)
                    V.tensor_copy(dst, src).then_inc(proj_dve, 1)
                dve.wait_ge(proj_act, 9 * (l + 1))
                dve.wait_ge(proj_dve, 9 * (l + 1))

                for c in range(5):
                    n = l * 5 + c
                    w = par[:, (PA_QN if c < 4 else PA_KN) + l:(PA_QN if c < 4 else PA_KN) + l + 1]
                    dve.wait_ge(qrs, n + 1)
                    V.scalar_tensor_tensor(pT[:, c, :], pT[:, c, :], w, scr[:, c % 2, :], ALU.mult, ALU.mult).then_inc(qnorm, 1)
                    dve.wait_ge(qrot, n + 1)
                    seq(V.tensor_tensor(scr[:, 4, 0:NS], bank(4 + c % 2), K["sinT"][:], ALU.mult))
                    dve.wait_ge(qcos, n + 1)
                    V.tensor_tensor(pT[:, c, NP:], scr[:, 4, 0:NS], scr[:, 2 + c % 2, 0:NS], ALU.add).then_inc(qk_ok, 1)

                for i in range(NU + 2):
                    if i < NU:
                        n = l * NU + i
                        w = P if i % TT == 0 else TOK
                        dve.wait_ge(sc_ps, n + 1)
                        if n >= 2:
                            dve.wait_ge(sc_exp, n - 1)
                        seq(V.tensor_reduce(st[:, i % 2, 0:1], ps[:, 1024 * (i % 2):1024 * (i % 2) + w], AX_X, ALU.max))
                        V.tensor_scalar(st[:, i % 2, 1:2], st[:, i % 2, 0:1], -HD ** -0.5, None, ALU.mult).then_inc(sc_max, 1)
                    if 1 <= i <= NU:
                        n = l * NU + i - 1
                        j = (i - 1) % 2
                        w = P if (i - 1) % TT == 0 else TOK
                        dve.wait_ge(sc_exp, n + 1)
                        seq(V.reciprocal(st[:, j, 3:4], st[:, j, 2:3]))
                        V.tensor_scalar(scr[:, 4 + j, 0:w], scr[:, 4 + j, 0:w], st[:, j, 3:4], None, ALU.mult).then_inc(sc_norm, 1)
                    if i >= 2:
                        n = l * NU + i - 2
                        h, t = (i - 2) // TT, (i - 2) % TT
                        c, b = h // 2, h % 2
                        dve.wait_ge(av_ps, n + 1)
                        V.tensor_copy(pT[64 * b:64 * b + 64, c, t * P:(t + 1) * P],
                                      bank(6 + (i - 2) % 2, P)[64 * b:64 * b + 64, :]).then_inc(av_sb, 1)

                for i, c in enumerate((C_HQ, C_HQ + 1, C_HG, C_HG + 1)):
                    n = 4 * l + i
                    e = scr[:, i % 2, :]
                    dve.wait_ge(sl_e, n + 1)
                    seq(V.tensor_scalar(e, e, 1.0, None, ALU.add))
                    seq(V.reciprocal(e, e))
                    V.tensor_tensor(pT[:, c, :], pT[:, c, :], e, ALU.mult).then_inc(sl_ok, 1)
                dve.wait_ge(sl_ok, 4 * (l + 1))
                for i in range(4):
                    d, p = i // 2, i % 2
                    n = 4 * l + i
                    z = pT[:, C_HF + i, :]
                    ep, en, tp, tn = (scr[:, j, :] for j in (2, 3, 4, 5))
                    lnden, den = scr[:, 6, :], scr[:, 7, :]
                    lnnum, num = scr[:, 8, :], scr[:, 9, :]
                    V.tensor_scalar(tp, z, 0.0, None, ALU.min).then_inc(gt_in, 1)
                    V.tensor_scalar(tn, z, -1.0, 0.0, ALU.mult, ALU.min).then_inc(gt_in, 1)
                    dve.wait_ge(gt_e, 2 * (n + 1))
                    if l > 0:
                        seq(V.scalar_tensor_tensor(num, en, lb[:, l, i:i + 1], ep, ALU.mult, ALU.add))
                    V.tensor_tensor(den, ep, en, ALU.add).then_inc(gt_den, 1)
                    dve.wait_ge(gt_den, n + 1)
                    rden = scr[:, 10, :]
                    seq(V.reciprocal(rden, den))
                    seq(V.scalar_tensor_tensor(decayed[:, i, :], en, omlb[:, l, i:i + 1], rden, ALU.mult, ALU.mult))
                    dve.wait_ge(gt_ln, n + 1 if l == 0 else 4 + 2 * (n + 1 - 4))
                    if l == 0:
                        seq(V.tensor_tensor(tn, tp, lnden, ALU.subtract))
                    else:
                        seq(V.tensor_scalar(tp, z, 80.0, 0.0, ALU.add, ALU.min))
                        seq(V.tensor_tensor(tn, lnnum, lnden, ALU.subtract))
                        seq(V.tensor_tensor(tn, tn, tp, ALU.add))
                    if d == 0:
                        V.tensor_tensor_scan(out=z, data0=K["restart"][:], data1=tn, initial=0.0,
                                             op0=ALU.mult, op1=ALU.add).then_inc(gt_ok, 1)
                    else:
                        V.tensor_tensor_scan(out=z[:, ::-1], data0=K["restart"][:], data1=tn[:, ::-1], initial=0.0,
                                             op0=ALU.mult, op1=ALU.add).then_inc(gt_ok, 1)
                    dve.wait_ge(gt_ok, n + 1)

                for p in range(2):
                    for d in range(2):
                        u = (l * 2 + p) * 2 + d
                        b = pT[:, C_HF + 2 * d + p, :]
                        bv = b.rearrange("p (n m) -> p n m", m=CH)
                        q, k = pT[:, C_HQ + p, :], decayed[:, 2 * d + p, :]
                        eb, qd, kd = scr[:, 8, :], scr[:, 9, :], scr[:, 10, :]
                        end = CH - 1 if d == 0 else 0
                        if u >= 1:
                            dve.wait_ge(inter_ps, u)
                        V.tensor_tensor(kd.rearrange("p (n m) -> p n m", m=CH),
                                        bv[:, :, end:end + 1].to_broadcast([P, NCH, CH]), bv, ALU.subtract).then_inc(dk_d, 1)
                        dve.wait_ge(dk_e, 2 * (u + 1))
                        V.tensor_tensor(kd, kd, k, ALU.mult).then_inc(dk_ok, 1)
                        V.tensor_tensor(qd, q, eb, ALU.mult).then_inc(dk_ok, 1)
                        g0 = u * 9
                        dve.wait_ge(g_ps, g0 + 1)
                        V.tensor_copy(scr[:, 11, :], ps[:, 1536 * ((g0) % 2):1536 * ((g0) % 2) + TOK]).then_inc(g_used, 1)
                        dve.wait_ge(g_ps, g0 + 2)
                        o = 1536 * ((g0 + 1) % 2)
                        if u >= 1:
                            dve.wait_ge(state_out, 32 * u)
                        for i, cnt in ((1, 4), (0, 5)):
                            ins = V.tensor_tensor(S[:, i::2, :], ps[:, o + 1024 * i:o + 1024 * i + cnt * P].rearrange("p (n v) -> p n v", v=P),
                                                  blockones[:].unsqueeze(1).to_broadcast([P, cnt, P]), ALU.mult)
                            if i == 1:
                                seq(ins)
                        ins.then_inc(g_used, 1)
                        dve.wait_ge(g_used, g0 + 2)
                        order = list(range(NCH)) if d == 0 else list(range(PROMPT_CH))[::-1] + list(range(PROMPT_CH, NCH))[::-1]
                        seq(V.scalar_tensor_tensor(S[:, 1, :], S[:, 0, :], eb[:, order[1] * CH + end:order[1] * CH + end + 1],
                                                   S[:, 1, :], ALU.mult, ALU.add))
                        for i in range(7):
                            ch = order[PROMPT_CH + i]
                            prev = s_init[:, l, d, p, :] if i == 0 else S[:, 1 + i, :]
                            ins = V.scalar_tensor_tensor(S[:, 2 + i, :], prev, eb[:, ch * CH + end:ch * CH + end + 1],
                                                         S[:, 2 + i, :], ALU.mult, ALU.add)
                            if i < 6:
                                seq(ins)
                            else:
                                ins.then_inc(s_ok, 1)
                        for i in range(7):
                            if i < 6:
                                m = HALVES[i]
                                n = u * 6 + i
                                dve.wait_ge(lv_e, n + 1)
                                if n >= 2:
                                    dve.wait_ge(g_ps, (n - 2) // 6 * 9 + (n - 2) % 6 + 4)
                                ev, qv, kv, ov = (x.rearrange("p (n m) -> p n m", m=2 * m) for x in
                                                  (scr[:, 2 + i % 2, :], q, k, scr[:, 6 + i % 2, :]))
                                qs, ks = (slice(m, 2 * m), slice(0, m)) if d == 0 else (slice(0, m), slice(m, 2 * m))
                                V.tensor_tensor(ov[:, :, qs], qv[:, :, qs], ev[:, :, qs], ALU.mult).then_inc(lv_ok, 1)
                                V.tensor_tensor(ov[:, :, ks], kv[:, :, ks], ev[:, :, ks], ALU.mult).then_inc(lv_ok, 1)
                            g = g0 + 2 + i
                            o = 1536 * (g % 2)
                            scores = ps[:, o:o + 1280].rearrange("p (n t) -> p n t", t=P)
                            dve.wait_ge(g_ps, g + 1)
                            if i == 0:
                                if u >= 1:
                                    dve.wait_ge(intra_ps, u)
                                V.tensor_tensor(aT, scores, ident[:].unsqueeze(1).to_broadcast([P, 10, P]), ALU.mult).then_inc(g_used, 1)
                            else:
                                mask = K["lvl"][:, d, i - 1, :].unsqueeze(1).to_broadcast([P, 10, P])
                                dve.wait_ge(g_used, g)
                                V.copy_predicated(aT, mask, scores).then_inc(g_used, 1)
                    n = 2 * l + p
                    dve.wait_ge(on_rs, n + 1)
                    seq(V.scalar_tensor_tensor(scr[:, 1, :], ps[:, 3072:3072 + TOK], par[:, PA_HN + l:PA_HN + l + 1],
                                               scr[:, 0, :], ALU.mult, ALU.mult))
                    V.tensor_tensor(pT[:, C_HG + p, :], pT[:, C_HG + p, :], scr[:, 1, :], ALU.mult).then_inc(on_ok, 1)

                dve.wait_ge(f_ab, l + 1)
                V.tensor_copy(scr_flat[:, 0:512], bank(6)).then_inc(f_abs, 1)
                for p in range(2):
                    n = 2 * l + p
                    dve.wait_ge(f_z, n + 1)
                    V.tensor_copy(scr_flat[:, 1280 * (1 + p):1280 * (2 + p)], ps[:, 1536 * p:1536 * p + 1280]).then_inc(f_zs, 1)

                for c in range(KC):
                    n = l * KC + c
                    dve.wait_ge(op_ps, n + 1)
                    for g, a, b in GROUPS:
                        V.scalar_tensor_tensor(xT[:, c, a:b], ps[:, 1024 * (c % 3) + a:1024 * (c % 3) + b],
                                               mods[:, l, 2, c, g:g + 1], xT[:, c, a:b], ALU.mult, ALU.add).then_inc(x_mid, 1)
                dve.wait_ge(x_mid, 2 * KC * (l + 1))
                dve.wait_ge(state_out, 16 * 8 * (l + 1))
                norm(l, 1)

                dve.wait_ge(lg_ps, l + 1)
                R = lambda at, n: rt[:, at:at + n]
                lg = R(0, 100).rearrange("p (t e) -> p t e", t=TT)
                seq(V.tensor_copy(lg, bank(7, 100).rearrange("p (t e) -> p t e", t=TT)))
                lgg, lge = lg[:, :, 0:NEG], lg[:, :, NEG:]
                gmax = R(100, 5).unsqueeze(2)
                t4 = R(110, 20).rearrange("p (t e) -> p t e", t=TT)
                u4 = R(130, 20).rearrange("p (t e) -> p t e", t=TT)
                s5 = R(150, 5).unsqueeze(2)
                ohg = R(160, 20).rearrange("p (t e) -> p t e", t=TT)
                gw = R(180, 5).unsqueeze(2)
                iota4 = K["tileno"][:, 32:36].unsqueeze(1).to_broadcast([P, TT, 4])

                def first_max(vals, mx, onehot):
                    seq(V.tensor_reduce(mx, vals, AX_X, ALU.max))
                    seq(V.tensor_tensor(t4, vals, mx.to_broadcast([P, TT, 4]), ALU.is_lt))
                    seq(V.scalar_tensor_tensor(t4, t4, 8.0, iota4, ALU.mult, ALU.add))
                    seq(V.tensor_reduce(s5, t4, AX_X, ALU.min))
                    seq(V.tensor_tensor(onehot, iota4, s5.to_broadcast([P, TT, 4]), ALU.is_equal))

                first_max(lgg, gmax, ohg)
                seq(V.tensor_tensor(u4, lgg, gmax.to_broadcast([P, TT, 4]), ALU.subtract))
                les = R(190, 20).rearrange("p (t e) -> p t e", t=TT)
                big = R(210, 80).rearrange("p (t e g) -> p t e g", t=TT, e=4)
                for t in range(TT):
                    seq(V.tensor_tensor(big[:, t], lge[:, t].rearrange("p (g e) -> p e g", g=4),
                                        ohg[:, t:t + 1, :].to_broadcast([P, 4, 4]), ALU.mult))
                seq(V.tensor_reduce(les, big, AX_X, ALU.add))
                m1, m2 = R(290, 5).unsqueeze(2), R(295, 5).unsqueeze(2)
                oh1 = R(300, 20).rearrange("p (t e) -> p t e", t=TT)
                oh2 = R(320, 20).rearrange("p (t e) -> p t e", t=TT)
                le2 = R(340, 20).rearrange("p (t e) -> p t e", t=TT)
                first_max(les, m1, oh1)
                seq(V.tensor_scalar(le2, oh1, -1.0, 1.0, ALU.mult, ALU.add))
                seq(V.tensor_tensor(le2, le2, les, ALU.mult))
                seq(V.scalar_tensor_tensor(le2, oh1, -BIG, le2, ALU.mult, ALU.add))
                first_max(le2, m2, oh2)
                V.tensor_tensor(R(360, 5).unsqueeze(2), m2, m1, ALU.subtract).then_inc(rt_m, 1)
                o1 = R(400, 80).rearrange("p (t e) -> p t e", t=TT)
                o2 = R(480, 80).rearrange("p (t e) -> p t e", t=TT)
                both = R(560, 80)
                for t in range(TT):
                    for o, oh in ((o1, oh1), (o2, oh2)):
                        seq(V.tensor_tensor(o[:, t].rearrange("p (g e) -> p g e", g=4),
                                            ohg[:, t, :].unsqueeze(2).to_broadcast([P, 4, 4]),
                                            oh[:, t:t + 1, :].to_broadcast([P, 4, 4]), ALU.mult))
                V.tensor_tensor(both, R(400, 80), R(480, 80), ALU.add).then_inc(rt_m, 1)
                dve.wait_ge(rt_e, 2 * (l + 1))
                e4 = R(130, 20).rearrange("p (t e) -> p t e", t=TT)
                seq(V.tensor_reduce(gw, e4, AX_X, ALU.add))
                e21 = R(360, 5).unsqueeze(2)
                seq(V.tensor_scalar(R(365, 5), R(360, 5), 1.0, None, ALU.add))
                seq(V.tensor_tensor(R(370, 5), R(365, 5), R(180, 5), ALU.mult))
                seq(V.reciprocal(R(375, 5), R(370, 5)))
                seq(V.tensor_copy(wgt[:, :, 0], R(375, 5)))
                seq(V.tensor_tensor(wgt[:, :, 1], R(375, 5), R(360, 5), ALU.mult))
                dve.wait_ge(rk_ps, l + 1)
                cnt, ntl, inc, exc = R(640, 16), R(656, 16), R(672, 16), R(100, 16)
                seq(V.tensor_copy(cnt, bank(6, 16, 80)))
                seq(V.tensor_scalar(ntl, cnt, 0.0, None, ALU.is_gt))
                for j in range(1, TT):
                    seq(V.scalar_tensor_tensor(ntl, cnt, float(P * j), ntl, ALU.is_gt, ALU.add))
                seq(V.tensor_tensor_scan(out=inc, data0=ones[:, 0:16], data1=ntl, initial=0.0, op0=ALU.mult, op1=ALU.add))
                seq(V.tensor_tensor(exc, inc, ntl, ALU.subtract))
                pos = R(210, 80)
                seq(V.scalar_tensor_tensor(pos.rearrange("p (t e) -> p t e", t=TT),
                                           exc.unsqueeze(1).to_broadcast([P, TT, 16]), float(P),
                                           bank(6, 80).rearrange("p (t e) -> p t e", t=TT), ALU.mult, ALU.add))
                for c, o in enumerate((R(400, 80), R(480, 80))):
                    seq(V.tensor_tensor(o, o, pos, ALU.mult))
                    seq(V.tensor_reduce(R(380 + 5 * c, 5), o.rearrange("p (t e) -> p t e", t=TT), AX_X, ALU.add))
                    if l > 0 and c == 0:
                        all_of(dve, y_in, l - 1, TT, 32)
                    seq(V.tensor_copy(slot_i[:, :, c], R(380 + 5 * c, 5)))
                cmp = scr_flat[:, 7000:7000 + MT * 16].rearrange("p (j e) -> p j e", e=16)
                seq(V.tensor_tensor(cmp, inc.unsqueeze(1).to_broadcast([P, MT, 16]),
                                    K["tileno"][:, 0:MT].unsqueeze(2).to_broadcast([P, MT, 16]), ALU.is_le))
                seq(V.tensor_reduce(R(110, MT), cmp, AX_X, ALU.add))
                seq(V.tensor_scalar(R(110, MT), R(110, MT), float(NE - 1), None, ALU.min))
                V.tensor_copy(tile_e[:, 0:MT], R(110, MT)).then_inc(rt_ok, 1)

                for i in range(MT + 1):
                    if i < MT:
                        n = l * MT + i
                        j = i % 2
                        dve.wait_ge(gu_s, n + 1)
                        if n >= 2:
                            dve.wait_ge(hid_ps, n - 1)
                        V.tensor_tensor(hid[:, j, :], bank(2 + j, DE, DE), sg[:, j, :], ALU.mult).then_inc(hid_ok, 1)
                        dve.wait_ge(hid_ps, n + 1)
                        if n >= 2:
                            dve.wait_ge(dn_ps, n - 1)
                        V.tensor_copy(hidT[:, j], bank(4, 256).rearrange("p (k t) -> p k t", k=2)).then_inc(hid_sb, 1)
                    if i >= 1:
                        n = l * MT + i - 1
                        j = (i - 1) % 2
                        dve.wait_ge(dn_ps, n + 1)
                        if nth(l, MT, i - 1) > 1:
                            dve.wait_ge(y_out[j], 16 * (nth(l, MT, i - 1) - 1))
                        V.tensor_copy(yb[:, j, :], ps[:, 2560:2560 + D]).then_inc(dn_sb, 1)
                for t in range(TT):
                    n = l * TT + t
                    j = t % 2
                    dve.wait_ge(y_in[j], 32 * nth(l, TT, t))
                    seq(V.tensor_scalar(y1[:, j, :], y1[:, j, :], wgt[:, t, 0:1], None, ALU.mult))
                    V.scalar_tensor_tensor(y2[:, j, :], y2[:, j, :], wgt[:, t, 1:2], y1[:, j, :], ALU.mult, ALU.add).then_inc(y_sum, 1)
                    dve.wait_ge(yt_ps, n + 1)
                    g = 0 if t == 0 else 1
                    for k in range(KC):
                        V.scalar_tensor_tensor(xT[:, k, t * P:(t + 1) * P],
                                               ps[:, 1024 * j + k * P:1024 * j + (k + 1) * P],
                                               mods[:, l, 5, k, g:g + 1], xT[:, k, t * P:(t + 1) * P],
                                               ALU.mult, ALU.add).then_inc(x_new, 1)

        @block.tensor
        def _(pe):
            mm = nc.tensor.matmul

            def item(n):
                pe.wait_ge(slot_in[n % RING], landed[n])
                return slot(n)

            def columns(out, lhs, rhs, parts, start, stop, **kw):
                for a, b in parts:
                    ins = mm(out[:, a:b], lhs, rhs[:, a:b], start=start, stop=stop, **kw)
                return ins

            WIDE = ((0, 512), (512, TOK))

            pe.wait_ge(x_in, 48)
            pe.wait_ge(params_in, 16 * (N_PARAM_DMAS + 4))
            nc.tensor.transpose(bank(4, PA_ROWS), rows[0:PA_ROWS, 0, :], ident[0:PA_ROWS, 0:PA_ROWS]).then_inc(par_ps, 1)
            nc.tensor.transpose(bank(4, 96, PB0), rows[0:96, 1, :], ident[0:96, 0:96]).then_inc(par_ps, 1)
            for l in range(DEPTH):
                last = nc.tensor.transpose(bank(5, P, P * l), ck_row[:, l, :], ident[:])
            last.then_inc(par_ps, 1)
            for t in range(TT):
                if t >= 2:
                    pe.wait_ge(xt_act if t % 2 == 0 else xt_dve, t // 2)
                for k in range(KC):
                    last = nc.tensor.transpose(ps[:, 1024 * (t % 2) + k * P:1024 * (t % 2) + (k + 1) * P],
                                               xrow[:, t, k * P:(k + 1) * P], ident[:])
                last.then_inc(xt_ps, 1)
            pe.wait_ge(cond_ok, 1)
            pe.wait_ge(consts_in, 16 * N_CONST)
            pe.wait_ge(late_in, 16 * 16 * DEPTH)
            pe.wait_ge(ck_sb, 1)

            def norm(l, which):
                n0 = (l * 2 + which) * KC
                for k in range(KC):
                    pe.wait_ge(nsq, n0 + k + 1)
                    sq = scr[:, k % 2, :]
                    mm(bank(5), ones[:], sq[:, NP:], start=(k == 0), stop=(k == KC - 1))
                    mm(bank(6, NP), ones[:], sq[:, 0:NP], start=(k == 0), stop=(k == KC - 1)).then_inc(nsum, 1)

            for l in range(DEPTH):
                base = l * PER_LAYER
                if l > 0:
                    pe.wait_ge(rt_ok, l)
                for i in range(ADA_ITEMS):
                    w = item(base + i).rearrange("p (k n) -> p k n", k=KC)
                    for j in range(2):
                        for k in range(KC):
                            last = mm(bank(7, 2, 2 * (2 * i + j)), w[:, k, j * P:(j + 1) * P], cond[:, :, k],
                                      start=(k == 0), stop=(k == KC - 1))
                    last.then_inc(ada_ps, 1)
                norm(l, 0)
                pe.wait_ge(h_ok, 2 * KC * (2 * l + 1))

                def unit(u):
                    n = 18 * l + u
                    v = u - 3
                    if v >= 0:
                        pe.wait_ge(proj_act if v % 2 == 0 else proj_dve, 9 * l + v // 2 + 1)
                    return ps[:, 1024 * (u % 3):1024 * (u % 3) + 1024]

                pe.wait_ge(nrs, 2 * l + 1)
                u = 0
                for i in range(IN_ITEMS):
                    n = base + ADA_ITEMS + i
                    w = item(n).rearrange("p (k n) -> p k n", k=KC)
                    for j in range(2):
                        token_major = i == 6 or (i == 2 and j == 1)
                        out = unit(u)
                        if not token_major:
                            for k in range(KC):
                                last = columns(out, w[:, k, j * P:(j + 1) * P], hT[:, k, :], WIDE, k == 0, k == KC - 1)
                        else:
                            if i == 2:
                                tiles, a, width = range(TT), P, P
                            else:
                                tiles, a, width = (range(4) if j == 0 else range(4, 5)), 0, 256
                            for s, t in enumerate(tiles):
                                for k in range(KC):
                                    last = mm(out[:, s * width:(s + 1) * width], hT[:, k, t * P:(t + 1) * P],
                                              w[:, k, a:a + width], start=(k == 0), stop=(k == KC - 1))
                        last.then_inc(proj_ps, 1)
                        u += 1
                pe.wait_ge(proj_act, 9 * (l + 1))
                pe.wait_ge(proj_dve, 9 * (l + 1))
                for i in range(6):
                    if i < 5:
                        n = l * 5 + i
                        pe.wait_ge(qsq, n + 1)
                        if i >= 2:
                            pe.wait_ge(qrs, n - 1)
                        out = ps[:, 1024 * (i % 2):1024 * (i % 2) + 1024]
                        columns(out, blockones[:], scr[:, i % 2, :], WIDE, True, True).then_inc(qsum, 1)
                    if i >= 1:
                        c = i - 1
                        n = l * 5 + c
                        pe.wait_ge(qnorm, n + 1)
                        if c >= 2:
                            pe.wait_ge(qk_ok, n - 1)
                        mm(bank(4 + c % 2), rot[:], pT[:, c, NP:], start=True, stop=True).then_inc(qrot, 1)
                nc.tensor.transpose(bank(6, P), pT[:, C_K, 0:NP], ident[:]).then_inc(ck_ps, 1)
                pe.wait_ge(qk_ok, 5 * (l + 1))
                pe.wait_ge(qrs, 5 * (l + 1))

                for i in range(NU + 2):
                    if i < NU:
                        n = l * NU + i
                        h, t = i // TT, i % TT
                        c, b = h // 2, slice(64 * (h % 2), 64 * (h % 2) + 64)
                        if i >= 2:
                            pe.wait_ge(sc_exp, n - 1)
                        out = ps[:, 1024 * (i % 2):1024 * (i % 2) + 1024]
                        q = pT[b, c, t * P:(t + 1) * P]
                        if t == 0:
                            last = mm(out[:, 0:P], q, pT[b, C_K, 0:NP], start=True, stop=True)
                        else:
                            mm(out[:, 0:NS], q, pT[b, C_K, NP:], start=True, stop=True)
                            last = mm(out[:, NS:NS + P], q, ckT[b, l, :], start=True, stop=True)
                        last.then_inc(sc_ps, 1)
                    if 1 <= i <= NU:
                        n = l * NU + i - 1
                        pe.wait_ge(sc_norm, n + 1)
                        if i >= 2:
                            pe.wait_ge(pt_sb, n)
                        for s in range(1 if (i - 1) % TT == 0 else 5):
                            last = nc.tensor.transpose(ps[:, 2048 + s * P:2048 + (s + 1) * P],
                                                       scr[:, 4 + (i - 1) % 2, s * P:(s + 1) * P], ident[:])
                        last.then_inc(pt_ps, 1)
                    if i >= 2:
                        n = l * NU + i - 2
                        h, t = (i - 2) // TT, (i - 2) % TT
                        b = slice(64 * (h % 2), 64 * (h % 2) + 64)
                        pe.wait_ge(pt_sb, n + 1)
                        if i >= 4:
                            pe.wait_ge(av_sb, n - 1)
                        elif i == 2:
                            pe.wait_ge(ko_sb, l + 1)
                        keys = [v_tok[:, 0, b]] if t == 0 else [v_tok[:, 1 + s, b] for s in range(4)] + [cv_tok[:, l, b]]
                        for s, v in enumerate(keys):
                            last = mm(bank(6 + i % 2, P)[b, :], v, scr[:, 6 + i % 2, s * P:(s + 1) * P],
                                      start=(s == 0), stop=(s == len(keys) - 1))
                        last.then_inc(av_ps, 1)

                pe.wait_ge(av_sb, NU * (l + 1))
                pe.wait_ge(sl_ok, 4 * (l + 1))
                for p in range(2):
                    for d in range(2):
                        u = (l * 2 + p) * 2 + d
                        q, k = pT[:, C_HQ + p, :], decayed[:, 2 * d + p, :]
                        g0 = u * 9
                        pe.wait_ge(gt_ok, 4 * (l + 1))

                        def buffer(g):
                            if g >= 2:
                                pe.wait_ge(g_used, g - 1)
                            return ps[:, 1536 * (g % 2):1536 * (g % 2) + 1536]
                        if d == 0 and u > 0:
                            pe.wait_ge(on_ok, 2 * l + p)
                        out = buffer(g0)
                        pe.wait_ge(dk_ok, 2 * u + 1)
                        for t in range(TT):
                            last = nc.tensor.transpose(out[:, t * P:(t + 1) * P], scr[:, 10, t * P:(t + 1) * P], ident[:])
                        last.then_inc(g_ps, 1)
                        out = buffer(g0 + 1)
                        pe.wait_ge(g_used, g0 + 1)
                        order = list(range(NCH)) if d == 0 else list(range(PROMPT_CH))[::-1] + list(range(PROMPT_CH, NCH))[::-1]
                        for i in range(9):
                            t, h = order[i] // 2, slice(64 * (order[i] % 2), 64 * (order[i] % 2) + 64)
                            at = 1024 * (i % 2) + (i // 2) * P
                            last = mm(out[:, at:at + P], scr[h, 11, t * P:(t + 1) * P],
                                      i_tok[h, t, p * P:(p + 1) * P], start=True, stop=True)
                        last.then_inc(g_ps, 1)
                        for i in range(7):
                            g = g0 + 2 + i
                            out = buffer(g)
                            if i > 0:
                                pe.wait_ge(lv_ok, 2 * (u * 6 + i))
                            kk, qq = (k, q) if i == 0 else (scr[:, 6 + (i - 1) % 2, :],) * 2
                            for s, (h, t) in enumerate(((0, 4), (0, 0), (0, 1), (0, 2), (0, 3), (1, 3), (1, 4), (1, 0), (1, 1), (1, 2))):
                                hs = slice(64 * h, 64 * h + 64)
                                if s == 7:
                                    pe.wait_ge(mid_ps, u * 7 + i + 1)
                                last = mm(out[:, (h * TT + t) * P:(h * TT + t + 1) * P],
                                          kk[hs, t * P:(t + 1) * P], qq[hs, t * P:(t + 1) * P], start=True, stop=True)
                                if s == 0:
                                    last.then_inc(mid_ps, 1)
                            last.then_inc(g_ps, 1)
                            if i == 1:
                                pe.wait_ge(s_ok, u + 1)
                                pe.wait_ge(dk_ok, 2 * u + 2)
                                for j, ch in enumerate(order):
                                    if j == 0:
                                        continue
                                    state = (S[:, 0, :] if j == 1 else s_init[:, l, d, p, :] if j == PROMPT_CH
                                             else S[:, j - 1, :])
                                    last = mm(ps[:, 3072 + ch * CH:3072 + (ch + 1) * CH], state,
                                              scr[:, 9, ch * CH:(ch + 1) * CH], start=(d == 0 and ch in (1, 8)),
                                              stop=False, skip_group_check=True)
                                last.then_inc(inter_ps, 1)
                        pe.wait_ge(g_used, g0 + 9)
                        for h in range(2):
                            for t in range(TT):
                                last = mm(ps[64 * h:64 * h + 64, 3072 + t * P:3072 + (t + 1) * P],
                                          i_tok[:, t, p * P + 64 * h:p * P + 64 * h + 64], aT[:, h * TT + t, :],
                                          start=False, stop=(d == 1), skip_group_check=True)
                        last.then_inc(intra_ps, 1)
                    n = 2 * l + p
                    pe.wait_ge(on_sq, n + 1)
                    pe.wait_ge(g_used, (u + 1) * 9)
                    columns(ps[:, 0:1024], blockones[:], scr[:, 0, :], WIDE, True, True).then_inc(on_sum, 1)

                pe.wait_ge(on_ok, 2 * (l + 1))
                for p in range(2):
                    for s in range(2):
                        last = mm(bank(6, P, (2 * p + s) * P), K["dft64"][:, s, :], wft[:, l, p, :], start=True, stop=True)
                last.then_inc(f_ab, 1)
                pe.wait_ge(f_abs, l + 1)
                for p in range(2):
                    for t in range(TT):
                        last = mm(ps[:, 1536 * p + 256 * t:1536 * p + 256 * t + 256], pT[:, C_FT + p, t * P:(t + 1) * P],
                                  scr_flat[:, 256 * p:256 * p + 256], start=True, stop=True)
                    last.then_inc(f_z, 1)
                for p in range(2):
                    n = 2 * l + p
                    pe.wait_ge(f_zs, n + 1)
                    if p == 1:
                        pe.wait_ge(f_os, 2 * n)
                    z = scr_flat[:, 1280 * (1 + p):1280 * (2 + p)].rearrange("p (t s e) -> p t s e", t=TT, s=2)
                    for i, (t, s) in enumerate((t, s) for t in range(4) for s in range(2)):
                        mm(bank(6), z[:, 1 + t, s, :], K["dft_s"][:, s, t, :], start=(i == 0), stop=(i == 7))
                    for s in range(2):
                        last = mm(bank(7, NP), z[:, 0, s, :], K["dft_p"][:, s, 0, :], start=(s == 0), stop=(s == 1))
                    last.then_inc(f_o, 1)
                pe.wait_ge(f_os, 4 * (l + 1))

                for i in range(OUT_ITEMS):
                    n = base + ADA_ITEMS + IN_ITEMS + i
                    w = item(n).rearrange("p (k n) -> p k n", k=KC)
                    for j in range(2):
                        c = 2 * i + j
                        if c >= 3:
                            pe.wait_ge(x_mid, l * 2 * KC + 2 * (c - 2))
                        out = ps[:, 1024 * (c % 3):1024 * (c % 3) + 1024]
                        for k in range(KC):
                            last = columns(out, w[:, k, j * P:(j + 1) * P], pT[:, MIX[k], :], WIDE, k == 0, k == KC - 1)
                        last.then_inc(op_ps, 1)
                pe.wait_ge(x_mid, 2 * KC * (l + 1))
                norm(l, 1)
                pe.wait_ge(h_ok, 2 * KC * (2 * l + 2))
                for t in range(TT):
                    for k in range(KC):
                        mm(bank(7, 20, 20 * t), hT[:, k, t * P:(t + 1) * P], wr[:, l, k, :], start=(k == 0), stop=False)
                    last = mm(bank(7, 20, 20 * t), ones[0:1, :], br[0:1, l, :], start=False, stop=True)
                last.then_inc(lg_ps, 1)
                for t in range(TT):
                    n = l * TT + t
                    if t >= 2:
                        pe.wait_ge(hr_sb, n - 1)
                    for k in range(KC):
                        last = nc.tensor.transpose(ps[:, 1024 * (t % 2) + k * P:1024 * (t % 2) + (k + 1) * P],
                                                   hT[:, k, t * P:(t + 1) * P], ident[:])
                    last.then_inc(hr_ps, 1)
                pe.wait_ge(rt_m, 2 * (l + 1))
                pe.wait_ge(nrs, 2 * l + 2)
                both = rt[:, 560:640].rearrange("p (t e) -> p t e", t=TT)
                for t in range(TT + 1):
                    out = bank(6, 16, 16 * t)
                    for s in range(t):
                        last = mm(out, ones[:], both[:, s, :], start=(s == 0), stop=(t == TT and s == TT - 1))
                    if t < TT:
                        mm(out, tri[:], both[:, t, :], start=(t == 0), stop=True)
                last.then_inc(rk_ps, 1)

                pe.wait_ge(hr_sb, TT * (l + 1))
                pe.wait_ge(rt_ok, l + 1)
                for i in range(MT + 2):
                    if i < MT:
                        n = l * MT + i
                        pe.wait_ge(xg_in[i % 2], 16 * nth(l, MT, i))
                        if i >= 1:
                            pe.wait_ge(xg_sb, n)
                        for k in range(KC):
                            last = nc.tensor.transpose(ps[:, k * P:(k + 1) * P], xg[:, i % 2, k * P:(k + 1) * P], ident[:])
                        last.then_inc(xg_ps, 1)
                    if i >= 1 and i <= MT:
                        n = l * MT + i - 1
                        j = (i - 1) % 2
                        pe.wait_ge(xg_sb, n + 1)
                        if i >= 3:
                            pe.wait_ge(hid_ok, n - 1)
                        for w_, half in ((0, 0), (1, DE)):
                            m = base + PRE + 3 * (i - 1) + w_
                            w = item(m).rearrange("p (k n) -> p k n", k=KC)
                            for k in range(KC):
                                last = mm(bank(2 + j, DE, half), xgT[:, j, k, :], w[:, k, :], start=(k == 0), stop=(k == KC - 1))
                            last.then_inc(gu_ps if w_ else gate_ps, 1)
                    if i >= 2:
                        n = l * MT + i - 2
                        j = (i - 2) % 2
                        pe.wait_ge(hid_ok, n + 1)
                        if i >= 3:
                            pe.wait_ge(hid_sb, n)
                        for k in range(2):
                            last = nc.tensor.transpose(bank(4, P, k * P), hid[:, j, k * P:(k + 1) * P], ident[:])
                        last.then_inc(hid_ps, 1)
                        pe.wait_ge(hid_sb, n + 1)
                        if i >= 3:
                            pe.wait_ge(dn_sb, n)
                        m = base + PRE + 3 * (i - 2) + 2
                        w = item(m).rearrange("p (k n) -> p k n", k=2)
                        for half in range(2):
                            for k in range(2):
                                last = mm(bank(5 + half), hidT[:, j, k, :], w[:, k, 512 * half:512 * half + 512],
                                          start=(k == 0), stop=(k == 1))
                        last.then_inc(dn_ps, 1)
                for t in range(TT):
                    n = l * TT + t
                    pe.wait_ge(y_sum, n + 1)
                    if t >= 2:
                        pe.wait_ge(x_new, 8 * (n - 1))
                    for k in range(KC):
                        last = nc.tensor.transpose(ps[:, 1024 * (t % 2) + k * P:1024 * (t % 2) + (k + 1) * P],
                                                   y2[:, t % 2, k * P:(k + 1) * P], ident[:])
                    last.then_inc(yt_ps, 1)

            pe.wait_ge(x_new, 8 * TT * DEPTH)
            for t in range(TT):
                if t >= 2:
                    pe.wait_ge(fin_sb, t - 1)
                for k in range(KC):
                    last = nc.tensor.transpose(ps[:, 1024 * (t % 2) + k * P:1024 * (t % 2) + (k + 1) * P],
                                               xT[:, k, t * P:(t + 1) * P], ident[:])
                last.then_inc(fin_ps, 1)


_INS = ["x_prompt", "x_sample", "cache_k", "cache_v", "state_fwd", "state_bwd", "c", "c_ctx", "w_ada", "b_ada",
        "norm1_w", "norm2_w", "w_in", "q_norm_w", "k_norm_w", "hg_lb", "hg_norm_w", "w_ft", "w_out",
        "w_gr", "b_gr", "w_er", "b_er", "w_gate", "w_up", "w_down"]
_OUTS = [(1, NP, D), (1, NS, D), (1, DEPTH, NP, 2, HD), (1, DEPTH, NP, 2, HD), (1, DEPTH, 4, HD, HD), (1, DEPTH, 4, HD, HD)]


def kernel(**inputs):
    import numpy as _np
    import concourse.bacc as _bacc
    from concourse import mybir as _mybir
    from concourse.bass_utils import run_bass_kernel_spmd as _run

    nc = _bacc.Bacc("TRN2", target_bir_lowering=False, num_devices=1)
    arrays, A, C = {}, {}, {}
    for name in _INS:
        a = _np.ascontiguousarray(inputs[name])
        arrays[f"in_{name}_dram"] = a
        A[name] = nc.dram_tensor(f"in_{name}_dram", a.shape, _mybir.dt.from_np(a.dtype), kind="ExternalInput").ap()
    for name, a in shape_constants().items():
        arrays[f"const_{name}_dram"] = a
        C[name] = nc.dram_tensor(f"const_{name}_dram", a.shape, _mybir.dt.from_np(a.dtype), kind="ExternalInput").ap()
    outs = [nc.dram_tensor(f"out_{i}_dram", s, _mybir.dt.float32, kind="ExternalOutput").ap() for i, s in enumerate(_OUTS)]
    build_program(nc, A, C, outs)
    r = _run(nc, [arrays], core_ids=[0])
    return tuple(r.results[0][f"out_{i}_dram"] for i in range(len(_OUTS)))
```

```python
from contextlib import ExitStack

import concourse.bass as bass
from concourse import mybir

ALU = mybir.AluOpType
ACT = mybir.ActivationFunctionType
AX_X = mybir.AxisListType.X
F32 = mybir.dt.float32
I32 = mybir.dt.int32
U8 = mybir.dt.uint8

P = 128
D = 1024
KC = D // P
DEPTH = 2
NP, NS = 128, 512
TOK = NP + NS
TT = TOK // P
GROUPS = ((0, 0, NP), (1, NP, TOK))
HD = 64
CH = 64
NCH = TOK // CH
PROMPT_CH = NP // CH
HALVES = (32, 16, 8, 4, 2, 1)
NE, TOPK = 16, 2
NEG, EPG = 4, 4
DE = 256
MT = (TOPK * TOK + NE * (P - 1)) // P
SLOTS = MT * P
EPS = 1e-6
IN_W = 2304
BIG = 3.0e38

C_Q, C_K, C_HQ, C_HF, C_HG, C_FT = 0, 4, 5, 7, 11, 13
MIX = (0, 1, 2, 3, 11, 12, 13, 14)

RING = 5
ADA_HALF, IN_ITEMS, OUT_ITEMS = 12, 9, 4
IN_ORDER = (4, 5, 3, 7, 2, 0, 1, 8, 6)


def weight_stream():
    s = []
    for l in range(DEPTH):
        if l == 0:
            s += [("ada", l, i) for i in range(ADA_HALF)]
        s += [("ada", l, ADA_HALF + i) for i in range(ADA_HALF)] if l == 0 else []
        s += [("in", l, i) for i in range(IN_ITEMS)]
        s += [("out", l, i) for i in range(OUT_ITEMS)]
        if l + 1 < DEPTH:
            s += [("ada", l + 1, i) for i in range(ADA_HALF)]
        s += [(k, l, j) for j in range(MT) for k in ("gate", "up", "down")]
        if l + 1 < DEPTH:
            s += [("ada", l + 1, ADA_HALF + i) for i in range(ADA_HALF)]
    return s


STREAM = weight_stream()
ITEM = {item: n for n, item in enumerate(STREAM)}

PA_COND, PA_N1, PA_N2, PA_QN, PA_KN, PA_HN, PA_LB, PA_ROWS = 0, 16, 32, 48, 50, 52, 54, 62
PB0 = 64

NU = 8 * TT
N_PARAM_DMAS = 12

CONSTS = ("ident", "blockones", "ones", "rot", "tri", "dft64", "cosT", "sinT",
          "dft_s", "dft_p", "lvl", "restart", "tileno")


def shape_constants():
    import numpy as np
    c = {}
    c["ident"] = np.eye(P, dtype=np.float32)
    bo = np.zeros((P, P), np.float32)
    bo[:64, :64] = 1
    bo[64:, 64:] = 1
    c["blockones"] = bo
    c["ones"] = np.ones((P, P), np.float32)
    rot = np.zeros((P, P), np.float32)
    for m in range(P):
        if m % 32 < 16:
            rot[m + 16, m] = -1.0
        else:
            rot[m - 16, m] = 1.0
    c["rot"] = rot
    c["tri"] = np.triu(np.ones((P, P), np.float32), 1)
    k = np.arange(64)
    th = 2 * np.pi * ((k[:, None] * k[None, :]) % 64) / 64
    d64 = np.zeros((P, 2, P), np.float32)
    for b in range(2):
        d64[64 * b:64 * b + 64, 0, 64 * b:64 * b + 64] = np.cos(th)
        d64[64 * b:64 * b + 64, 1, 64 * b:64 * b + 64] = -np.sin(th)
    c["dft64"] = d64
    half = 32
    inv = (1.0 / (np.float32(10000.0) ** (np.arange(0, half, 2, dtype=np.float32) / np.float32(half)))).astype(np.float32)
    t = np.arange(NS)
    row, col = (t // 64).astype(np.float32), (t % 64).astype(np.float32)
    cosT, sinT = np.zeros((P, NS), np.float32), np.zeros((P, NS), np.float32)
    for p in range(P):
        d = p % 64
        ang = ((row if d < 32 else col) * inv[d % 16]).astype(np.float32)
        cosT[p], sinT[p] = np.cos(ang), np.sin(ang)
    c["cosT"], c["sinT"] = cosT, sinT

    def dft(n):
        i = np.arange(n)
        a = 2 * np.pi * ((i[:, None] * i[None, :]) % n) / n
        s = 1.0 / np.sqrt(n * 64.0)
        both = np.stack([np.cos(a) * s, np.sin(a) * s], 0)
        return both.reshape(2, n // P, P, n).transpose(2, 0, 1, 3).astype(np.float32).copy()
    c["dft_s"], c["dft_p"] = dft(NS), dft(NP)
    lvl = np.zeros((P, 2, len(HALVES), P), np.float32)
    s, q = np.arange(P)[:, None], np.arange(P)[None, :]
    for i, m in enumerate(HALVES):
        same = (s // (2 * m)) == (q // (2 * m))
        lvl[:, 0, i] = same & (s % (2 * m) < m) & (q % (2 * m) >= m)
        lvl[:, 1, i] = same & (s % (2 * m) >= m) & (q % (2 * m) < m)
    c["lvl"] = lvl
    c["restart"] = np.broadcast_to((np.arange(TOK) % CH != 0).astype(np.float32), (P, TOK)).copy()
    tn = np.zeros((P, 64), np.float32)
    tn[:, 0:MT] = np.arange(MT)
    tn[:, 32:36] = np.arange(4)
    tn[:, 40:40 + TT] = np.arange(TT)[None] * P + np.arange(P)[:, None]
    c["tileno"] = tn
    return c


def nth(l, n, i):
    return l * ((n + 1 - i % 2) // 2) + i // 2 + 1


def all_of(eng, sems, l, n, each):
    for i in range(2):
        eng.wait_ge(sems[i], each * nth(l, n, n - 1 if (n - 1) % 2 == i else n - 2))


def _proj_unit(u):
    i, j = IN_ORDER[u // 2], u % 2

    def pair(ps):
        return ps[:, 1024 * (u % 2):1024 * (u % 2) + 1024]
    if (i, j) == (2, 1):
        return lambda pT, v, t, ps: (v[:, :, :], pair(ps)[:, 0:TOK].rearrange("p (t e) -> p t e", t=TT))
    if (i, j) == (6, 0):
        return lambda pT, v, t, ps: (t[:, 0:4, :], pair(ps).rearrange("p (t e) -> p t e", t=4))
    if (i, j) == (6, 1):
        return lambda pT, v, t, ps: (t[:, 4, :], pair(ps)[:, 0:256])
    c = 2 * i + j - (0 if i < 3 else 1 if i < 6 else 3)
    return lambda pT, v, t, ps: (pT[:, c, :], pair(ps)[:, 0:TOK])


PROJ_EVAC = [_proj_unit(u) for u in range(18)]
AFTER = {1: ("gate", 0), 2: ("gate", 1), 3: ("gate", 2), 4: ("gate", 3), 6: ("silu", 0), 7: ("silu", 1),
         8: ("silu", 2), 9: ("silu", 3), 10: ("qk", 0), 12: ("qk", 1), 13: ("qk", 2), 14: ("qk", 3), 15: ("qk", 4),
         16: ("qk", 5)}
QK_CHUNKS = (4, 0, 1, 2, 3)
GATE_CHUNKS = (5, 6, 11, 12)
PBUF = (4, 5, 8)


def build_program(nc, A, C, outs):
    y_prompt, y_sample, o_ck, o_cv, o_sf, o_sb = outs
    ctx = ExitStack()
    with ctx:
        def sb(name, shape, dt=F32):
            return ctx.enter_context(nc.sbuf_tensor(name, shape, dt))

        def sem(name):
            return ctx.enter_context(nc.semaphore(name))

        K = {n: sb("c_" + n, list(C[n].shape), U8 if n == "lvl" else F32) for n in CONSTS}
        ident, blockones, ones, rot, tri = (K[n] for n in ("ident", "blockones", "ones", "rot", "tri"))

        xT = sb("xT", [P, KC, TOK])
        hT = sb("hT", [P, KC, TOK])
        hT_flat = hT[:, :, :].rearrange("p k t -> p (k t)")
        xrow = hT_flat.rearrange("p (t d) -> p t d", t=TT)
        pT = sb("pT", [P, 15, TOK])
        pT_flat = pT[:, :, :].rearrange("p k t -> p (k t)")
        v_tok = sb("v_tok", [P, TT, P])
        i_tok = sb("i_tok", [P, TT, 256])
        ring = sb("ring", [P, RING, 2048])
        par = sb("par", [P, 160])
        cond = sb("cond", [P, 2, KC])
        csc = sb("csc", [P, 2, 16])
        lbt = sb("lbt", [P, 4, 4])
        lb = sb("lb", [P, DEPTH, 4])
        omlb = sb("omlb", [P, DEPTH, 4])
        eps_t = sb("eps_t", [P, 1])
        ckT = sb("ckT", [P, DEPTH, P])
        cv_tok = sb("cv_tok", [P, DEPTH, P])
        wr = sb("wr", [P, DEPTH, KC, NEG + NE])
        br = sb("br", [1, DEPTH, NEG + NE])
        wft = sb("wft", [P, DEPTH, 2, P])
        s_init = sb("s_init", [P, DEPTH, 2, 2, P])
        decayed = sb("decayed", [P, 4, TOK])
        mrow = sb("mrow", [2, 2, 256])
        mods = sb("mods", [P, DEPTH, 6, KC, 2])
        amul = sb("amul", [P, DEPTH, 2, KC, 2])
        scr = sb("scr", [P, 12, TOK])
        scr_flat = scr[:, :, :].rearrange("p k t -> p (k t)")
        st = sb("st", [P, 3, 8])
        kout = scr[:, 11, 0:P]
        rt = scr_flat[:, 6144:6844]
        slot_i = sb("slot_i", [P, TT, TOPK], I32)
        slot_tok = sb("slot_tok", [P, MT], I32)
        tokid = sb("tokid", [P, TT], I32)
        zeros_i = sb("zeros_i", [P, MT], I32)
        tile_e = sb("tile_e", [P, 32], I32)
        wgt = sb("wgt", [P, TT, TOPK])

        S = hT_flat[:, 0:9 * P].rearrange("p (n v) -> p n v", v=P)
        aT = hT_flat[:, 1280:2560].rearrange("p (n v) -> p n v", v=P)
        lvl_f = pT_flat[:, 0:2 * len(HALVES) * P].rearrange("p (d i t) -> p d i t", d=2, t=P)
        rows = pT_flat[:, 2048:2304].rearrange("p (a b) -> p a b", a=2)
        ck_row = pT_flat[:, 2304:2304 + DEPTH * P].rearrange("p (l t) -> p l t", l=DEPTH)
        xg = pT_flat[:, 0:2048].rearrange("p (b d) -> p b d", b=2)
        xgT = pT_flat[:, 2048:4096].rearrange("p (b k t) -> p b k t", b=2, k=KC)
        sg = pT_flat[:, 4096:4608].rearrange("p (b f) -> p b f", b=2)
        hid = pT_flat[:, 4608:5120].rearrange("p (b f) -> p b f", b=2)
        hidT = pT_flat[:, 5120:5632].rearrange("p (b k t) -> p b k t", b=2, k=2)
        yb = pT_flat[:, 5632:7680].rearrange("p (b d) -> p b d", b=2)
        hrow = scr_flat[:, 0:2048].rearrange("p (b d) -> p b d", b=2)
        y1 = scr_flat[:, 2048:4096].rearrange("p (b d) -> p b d", b=2)
        y2 = scr_flat[:, 4096:6144].rearrange("p (b d) -> p b d", b=2)

        ps = ctx.enter_context(nc.psum_tensor("ps", [P, 8 * 512], F32))

        def bank(b, n=512, off=0):
            return ps[:, b * 512 + off:b * 512 + off + n]

        h_dram = nc.dram_tensor("h_rows", (TOK, D), F32).ap()
        table = nc.dram_tensor("slot_table", (SLOTS, 1), I32).ap()
        y_dram = nc.dram_tensor("y_rows", (SLOTS, D), F32).ap()

        consts_in = sem("consts_in"); params_in = sem("params_in"); x_in = sem("x_in")
        late_in = sem("late_in")
        slot_in = [sem(f"slot_in{i}") for i in range(RING)]
        ada_ps = sem("ada_ps"); ada_sb = sem("ada_sb"); ada_tr = sem("ada_tr"); gate_ps = sem("gate_ps")
        zero_done = sem("zero_done")
        xt_ps = sem("xt_ps"); xt_act = sem("xt_act"); xt_dve = sem("xt_dve")
        par_ps = sem("par_ps"); par_sb = sem("par_sb")
        cond_e = sem("cond_e"); cond_ok = sem("cond_ok"); lb_d = sem("lb_d"); lb_e = sem("lb_e")
        mods_ok = sem("mods_ok")
        nsq = sem("nsq"); nsum = sem("nsum"); nrs = sem("nrs"); nscaled = sem("nscaled"); h_ok = sem("h_ok")
        proj_ps = sem("proj_ps"); proj_act = sem("proj_act"); proj_dve = sem("proj_dve")
        qsq = sem("qsq"); qsum = sem("qsum"); qrs = sem("qrs"); qnorm = sem("qnorm")
        qrot = sem("qrot"); qcos = sem("qcos"); qk_ok = sem("qk_ok")
        ck_ps = sem("ck_ps"); ck_sb = sem("ck_sb"); cache_out = sem("cache_out"); ko_sb = sem("ko_sb"); rt_e = sem("rt_e")
        sc_ps = sem("sc_ps"); sc_max = sem("sc_max"); sc_exp = sem("sc_exp"); sc_norm = sem("sc_norm")
        pt_ps = sem("pt_ps"); pt_sb = sem("pt_sb"); av_ps = sem("av_ps"); av_sb = sem("av_sb")
        sl_e = sem("sl_e"); sl_ok = sem("sl_ok")
        gt_in = sem("gt_in"); gt_e = sem("gt_e"); gt_den = sem("gt_den"); gt_ln = sem("gt_ln"); gt_ok = sem("gt_ok")
        dk_d = sem("dk_d"); dk_e = sem("dk_e"); dk_ok = sem("dk_ok")
        lv_d = sem("lv_d"); lv_e = sem("lv_e"); lv_ok = sem("lv_ok")
        g_ps = sem("g_ps"); mid_ps = sem("mid_ps"); g_used = sem("g_used"); s_ok = sem("s_ok")
        inter_ps = sem("inter_ps"); intra_ps = sem("intra_ps")
        on_sq = sem("on_sq"); on_sum = sem("on_sum"); on_rs = sem("on_rs"); on_ok = sem("on_ok")
        state_out = sem("state_out")
        f_ab = sem("f_ab"); f_abs = sem("f_abs"); f_z = sem("f_z"); f_zs = sem("f_zs"); f_o = sem("f_o"); f_os = sem("f_os")
        op_ps = sem("op_ps"); x_mid = sem("x_mid")
        lg_ps = sem("lg_ps"); lg_sb = sem("lg_sb"); rt_m = sem("rt_m"); rk_ps = sem("rk_ps"); rt_ok = sem("rt_ok")
        hr_ps = sem("hr_ps"); hr_sb = sem("hr_sb"); hr_out = [sem(f"hr_out{i}") for i in range(2)]
        tb_zero = sem("tb_zero"); tb_out = sem("tb_out"); tb_in = sem("tb_in")
        xg_in = [sem(f"xg_in{i}") for i in range(2)]; xg_ps = sem("xg_ps"); xg_sb = sem("xg_sb")
        gu_ps = sem("gu_ps"); gu_s = sem("gu_s"); hid_ok = sem("hid_ok"); hid_ps = sem("hid_ps"); hid_sb = sem("hid_sb")
        dn_ps = sem("dn_ps"); dn_sb = sem("dn_sb"); y_out = [sem(f"y_out{i}") for i in range(2)]
        y_in = [sem(f"y_in{i}") for i in range(2)]; y_sum = sem("y_sum"); yt_ps = sem("yt_ps"); x_new = sem("x_new")
        fin_ps = sem("fin_ps"); fin_sb = sem("fin_sb"); fin_out = sem("fin_out")
        dve_step = sem("dve_step"); act_step = sem("act_step"); pool_step = sem("pool_step")

        N_CONST = len(CONSTS) - 1

        def item_dmas(n):
            kind, l, i = STREAM[n]
            return 4 if kind == "in" and IN_ORDER[i] < 2 else 3 if kind == "out" else 1

        landed, slot_total = [], [0] * RING
        for n in range(len(STREAM)):
            slot_total[n % RING] += 16 * item_dmas(n)
            landed.append(slot_total[n % RING])

        def multiplied(n):
            kind, l, i = STREAM[n]
            if kind == "ada":
                return ada_ps, l * 2 * ADA_HALF + i + 1
            if kind == "in":
                return proj_ps, 2 * (l * IN_ITEMS + i + 1)
            if kind == "out":
                return op_ps, 2 * (l * OUT_ITEMS + i + 1)
            return {"gate": gate_ps, "up": gu_ps, "down": dn_ps}[kind], l * MT + i + 1

        def slot(n):
            return ring[:, n % RING, :]

        def x_whole(eng, l):
            if l == 0:
                eng.wait_ge(xt_act, 3)
                eng.wait_ge(xt_dve, 2)
            else:
                eng.wait_ge(x_new, KC * TT * l)

        block = ctx.enter_context(nc.Block())

        @block.sync
        def _(sp):
            sp.dma_start(K["ident"][:], C["ident"]).then_inc(x_in, 16)
            sp.dma_start(xrow[:, 0, :], A["x_prompt"][0]).then_inc(x_in, 16)
            sp.dma_start(xrow[:, 1:TT, :], A["x_sample"][0].rearrange("(t p) d -> p t d", p=P)).then_inc(x_in, 16)
            for n in CONSTS[1:]:
                sp.dma_start(lvl_f if n == "lvl" else K[n][:], C[n]).then_inc(consts_in, 16)

            def next_item(n):
                if n >= RING:
                    sp.wait_ge(*multiplied(n - RING))
                return slot(n), slot_in[n % RING]

            for n, (kind, l, i) in enumerate(STREAM):
                dst, s = next_item(n)
                cols = dst.rearrange("p (k n) -> p k n", k=KC)
                if kind == "ada":
                    sp.dma_start(cols, A["w_ada"][l].rearrange("(k p) n -> p k n", p=P)[:, :, 256 * i:256 * i + 256]).then_inc(s, 16)
                elif kind == "in":
                    w_in = A["w_in"][l].rearrange("(k p) n -> p k n", p=P)
                    c0 = IN_ORDER[i]
                    if c0 < 2:
                        view = dst.rearrange("p (k c b j) -> p k c b j", k=KC, c=2, b=2)
                        for b in range(2):
                            for c in range(2):
                                at = 256 * b + 128 * c0 + 64 * c
                                sp.dma_start(view[:, :, c, b, :], w_in[:, :, at:at + 64]).then_inc(s, 16)
                    else:
                        sp.dma_start(cols, w_in[:, :, 256 * c0:256 * c0 + 256]).then_inc(s, 16)
                elif kind == "out":
                    w_out = A["w_out"][l]
                    for b in range(2):
                        sp.dma_start(cols[64 * b:64 * b + 64, 0:4, :],
                                     w_out[256 * b:256 * b + 256, 256 * i:256 * i + 256]
                                     .rearrange("(c p) n -> p c n", p=64)).then_inc(s, 16)
                    sp.dma_start(cols[:, 4:8, :], w_out[512:1024, 256 * i:256 * i + 256]
                                 .rearrange("(c p) n -> p c n", p=P)).then_inc(s, 16)
                else:
                    if kind == "gate":
                        if i == 0:
                            sp.wait_ge(rt_ok, l + 1)
                        e = sp.value_load(tile_e[0:1, i:i + 1], min_val=0, max_val=NE - 1)
                    name = {"gate": "w_gate", "up": "w_up", "down": "w_down"}[kind]
                    sp.dma_start(dst.rearrange("p (k n) -> p k n", k=2 if kind == "down" else KC),
                                 A[name][l, bass.ds(e, 1)].rearrange("e (k p) n -> p (e k) n", p=P)).then_inc(s, 16)
            sp.wait_ge(cache_out, 16 * 2 * DEPTH)
            sp.wait_ge(state_out, 16 * 8 * DEPTH)
            all_of(sp, hr_out, DEPTH - 1, TT, 16)
            sp.wait_ge(tb_zero, 16 * DEPTH)
            sp.wait_ge(tb_out, 16 * TT * TOPK * DEPTH)
            all_of(sp, y_out, DEPTH - 1, MT, 16)
            sp.wait_ge(fin_out, 16 * TT)

        @block.gpsimd
        def _(pool):
            steps = [0]

            def seq(ins):
                steps[0] += 1
                ins.then_inc(pool_step, 1)
                pool.wait_ge(pool_step, steps[0])

            nc.gpsimd.memset(wft[:], 0.0).then_inc(zero_done, 1)
            nc.gpsimd.memset(s_init[:], 0.0).then_inc(zero_done, 1)
            nc.gpsimd.memset(eps_t[:], EPS).then_inc(zero_done, 1)
            nc.gpsimd.memset(zeros_i[:], 0).then_inc(zero_done, 1)
            pool.wait_ge(zero_done, 4)
            for l in range(DEPTH):
                for g in range(4):
                    h = 64 * (g % 2)
                    pool.dma_start(wft[h:h + 64, l, g // 2, h:h + 64], A["w_ft"][l, g]).then_inc(late_in, 16)
                    for d, name in enumerate(("state_fwd", "state_bwd")):
                        pool.dma_start(s_init[h:h + 64, l, d, g // 2, h:h + 64], A[name][0, l, g]).then_inc(late_in, 16)
                pool.dma_start(wr[:, l, :, 0:NEG], A["w_gr"][l].rearrange("(k p) g -> p k g", p=P)).then_inc(late_in, 16)
                pool.dma_start(wr[:, l, :, NEG:], A["w_er"][l].rearrange("(k p) g -> p k g", p=P)).then_inc(late_in, 16)
                pool.dma_start(br[0:1, l, 0:NEG], A["b_gr"][l:l + 1]).then_inc(late_in, 16)
                pool.dma_start(br[0:1, l, NEG:], A["b_er"][l:l + 1]).then_inc(late_in, 16)
            pool.wait_ge(consts_in, 16 * N_CONST)

            for l in range(DEPTH):
                for i, c in enumerate(QK_CHUNKS):
                    n = l * 5 + i
                    pool.wait_ge(qnorm, n + 1)
                    if n >= 2:
                        pool.wait_ge(qk_ok, n - 1)
                    nc.gpsimd.tensor_tensor(scr[:, 2 + i % 2, 0:NS], pT[:, c, NP:], K["cosT"][:], ALU.mult).then_inc(qcos, 1)
                for p in range(2):
                    for d in range(2):
                        u = (l * 2 + p) * 2 + d
                        if p == 0 and d == 0:
                            pool.wait_ge(gt_ok, 4 * l + 4)
                            pool.wait_ge(qk_ok, 5 * (l + 1))
                        b = pT[:, C_HF + 2 * d + p, :]
                        for i, m in enumerate(HALVES):
                            n = u * 6 + i
                            if n >= 2:
                                pool.wait_ge(lv_ok, 2 * (n - 1))
                            bv = b.rearrange("p (n m) -> p n m", m=2 * m)
                            dv = scr[:, 2 + i % 2, :].rearrange("p (n m) -> p n m", m=2 * m)
                            nb = TOK // (2 * m)
                            if d == 0:
                                ref = bv[:, :, m - 1:m].to_broadcast([P, nb, m])
                                q, k = slice(m, 2 * m), slice(0, m)
                            else:
                                ref = bv[:, :, m:m + 1].to_broadcast([P, nb, m])
                                q, k = slice(0, m), slice(m, 2 * m)
                            nc.gpsimd.tensor_tensor(dv[:, :, q], bv[:, :, q], ref, ALU.subtract).then_inc(lv_d, 1)
                            nc.gpsimd.tensor_tensor(dv[:, :, k], ref, bv[:, :, k], ALU.subtract).then_inc(lv_d, 1)
                if l > 0:
                    pool.wait_ge(tb_in, 16 * l)
                pool.dma_start(table.rearrange("(p j) o -> p (j o)", p=P), zeros_i[:]).then_inc(tb_zero, 16)
                pool.wait_ge(tb_zero, 16 * (l + 1))
                pool.wait_ge(rt_ok, l + 1)
                for t in range(TT):
                    for c in range(TOPK):
                        pool.indirect_dma_start(table, bass.IndirectOffsetOnAxis(ap=slot_i[:, t, c:c + 1], axis=0),
                                                tokid[:, t:t + 1], None).then_inc(tb_out, 16)
                pool.wait_ge(tb_out, 16 * TT * TOPK * (l + 1))
                pool.dma_start(slot_tok[:], table.rearrange("(j p) o -> p (j o)", p=P), allow_slow_non_contiguous=True).then_inc(tb_in, 16)
                pool.wait_ge(tb_in, 16 * (l + 1))
                all_of(pool, hr_out, l, TT, 16)
                for j in range(MT):
                    n = l * MT + j
                    if n >= 2:
                        pool.wait_ge(xg_ps, n - 1)
                    if j == 0:
                        pool.wait_ge(x_mid, 2 * KC * (l + 1))
                    pool.indirect_dma_start(xg[:, j % 2, :], None, h_dram,
                                            bass.IndirectOffsetOnAxis(ap=slot_tok[:, j:j + 1], axis=0)).then_inc(xg_in[j % 2], 16)
                all_of(pool, y_out, l, MT, 16)
                for t in range(TT):
                    n = l * TT + t
                    if n >= 2:
                        pool.wait_ge(y_sum, n - 1)
                    for c, dst in enumerate((y1, y2)):
                        if t >= 2 and c == 1:
                            pool.wait_ge(yt_ps, n - 1)
                        pool.indirect_dma_start(dst[:, t % 2, :], None, y_dram,
                                                bass.IndirectOffsetOnAxis(ap=slot_i[:, t, c:c + 1], axis=0)).then_inc(y_in[t % 2], 16)

        @block.scalar
        def _(act):
            steps = [0]

            def seq(ins):
                steps[0] += 1
                ins.then_inc(act_step, 1)
                act.wait_ge(act_step, steps[0])

            def A_(out, in_, f, **kw):
                return nc.scalar.activation(out, in_, f, **kw)

            r0 = rows[:, 0, :]
            n_par = 0
            for src, at, cnt in (("c_ctx", PA_COND, 8), ("c", PA_COND + 8, 8)):
                v = A[src] if src == "c_ctx" else A[src][0]
                act.dma_start(r0[at:at + cnt, :], v.rearrange("(k p) -> k p", p=P)).then_inc(params_in, 16)
                n_par += 1
            for src, at in (("norm1_w", PA_N1), ("norm2_w", PA_N2)):
                act.dma_start(r0[at:at + 16, :], A[src].rearrange("l (k p) -> (l k) p", p=P)).then_inc(params_in, 16)
                n_par += 1
            for src, at in (("q_norm_w", PA_QN), ("k_norm_w", PA_KN), ("hg_norm_w", PA_HN)):
                for b in range(2):
                    act.dma_start(r0[at:at + 2, 64 * b:64 * b + 64], A[src]).then_inc(params_in, 16)
                    n_par += 1
            act.dma_start(r0[PA_LB:PA_LB + 8, :], A["hg_lb"].rearrange("l d (k p) -> (l d k) p", p=P)).then_inc(params_in, 16)
            act.dma_start(rows[0:96, 1, :], A["b_ada"].rearrange("l (k p) -> (l k) p", p=P)).then_inc(params_in, 16)
            n_par += 2
            assert n_par == N_PARAM_DMAS
            for l in range(DEPTH):
                act.dma_start(ck_row[:, l, :], A["cache_k"][0, l].rearrange("t h d -> t (h d)")).then_inc(params_in, 16)
                act.dma_start(cv_tok[:, l, :], A["cache_v"][0, l].rearrange("t h d -> t (h d)")).then_inc(params_in, 16)

            act.wait_ge(par_sb, 1)
            A_(csc[:, 0, :], par[:, PA_COND:PA_COND + 16], ACT.Exp, scale=-1.0).then_inc(cond_e, 1)
            act.wait_ge(lb_d, 1)
            A_(lbt[:, 1, :], lbt[:, 0, :], ACT.Exp).then_inc(lb_e, 1)
            A_(lbt[:, 3, :], lbt[:, 2, :], ACT.Exp).then_inc(lb_e, 1)
            for t in range(TT):
                if t % 2 == 0:
                    act.wait_ge(xt_ps, t + 1)
                    A_(xT[:, :, t * P:(t + 1) * P], ps[:, 0:1024].rearrange("p (k t) -> p k t", k=KC), ACT.Copy).then_inc(xt_act, 1)

            def norm(l, which):
                n0 = (l * 2 + which) * KC
                for k in range(KC):
                    if n0 + k >= 2:
                        act.wait_ge(nsum, n0 + k - 1)
                    if which == 0:
                        x_whole(act, l)
                    else:
                        act.wait_ge(x_mid, l * 2 * KC + 2 * (k + 1))
                    A_(scr[:, k % 2, :], xT[:, k, :], ACT.Square).then_inc(nsq, 1)
                act.wait_ge(nsum, n0 + KC)
                rs = scr[:, 2, :]
                seq(A_(rs[:, 0:NS], bank(5), ACT.Ln, scale=1.0 / D, bias=eps_t[:, 0:1]))
                seq(A_(rs[:, NS:], bank(6, NP), ACT.Ln, scale=1.0 / D, bias=eps_t[:, 0:1]))
                A_(rs, rs, ACT.Exp, scale=-0.5).then_inc(nrs, 1)
                for k in range(KC):
                    act.wait_ge(nscaled, 2 * (n0 + k + 1))
                    for g, a, b in GROUPS:
                        A_(hT[:, k, a:b], hT[:, k, a:b], ACT.Identity,
                           bias=mods[:, l, 3 * which, k, g:g + 1]).then_inc(h_ok, 1)

            def ada(l, half):
                for i in range(ADA_HALF):
                    n = (2 * l + half) * ADA_HALF + i
                    act.wait_ge(ada_ps, n + 1)
                    if n >= 2:
                        act.wait_ge(ada_tr, n - 1)
                    A_(mrow[:, i % 2, :], bank(4 + i % 2, 256)[0:2, :], ACT.Copy).then_inc(ada_sb, 1)

            def evacuated(l, u):
                act.wait_ge(proj_act if u % 2 == 0 else proj_dve, 9 * l + u // 2 + 1)

            def gate(l, i):
                n = 4 * l + i
                act.wait_ge(gt_in, 2 * (n + 1))
                for j in range(2):
                    A_(scr[:, 2 + j, :], scr[:, 4 + j, :], ACT.Exp).then_inc(gt_e, 1)
                act.wait_ge(gt_den, n + 1)
                A_(scr[:, 6, :], scr[:, 7, :], ACT.Ln).then_inc(gt_ln, 1)
                if l > 0:
                    A_(scr[:, 8, :], scr[:, 9, :], ACT.Ln).then_inc(gt_ln, 1)

            def silu(l, i):
                n = 4 * l + i
                if n >= 2:
                    act.wait_ge(sl_ok, n - 1)
                evacuated(l, 4 + i)
                A_(scr[:, i % 2, :], pT[:, GATE_CHUNKS[i], :], ACT.Exp, scale=-1.0).then_inc(sl_e, 1)

            def qk(l, i):
                if i == 5:
                    return
                n, c = l * 5 + i, QK_CHUNKS[i]
                r = scr[:, i % 2, :]
                if n >= 2:
                    act.wait_ge(qnorm, n - 1)
                evacuated(l, 8 if c == 4 else 10 + c)
                act.wait_ge(sl_ok, 4 * (l + 1))
                A_(r, pT[:, c, :], ACT.Square).then_inc(qsq, 1)
                act.wait_ge(qsum, n + 1)
                seq(A_(r, ps[:, 3072:3072 + TOK], ACT.Ln, scale=1.0 / HD, bias=eps_t[:, 0:1]))
                A_(r, r, ACT.Exp, scale=-0.5).then_inc(qrs, 1)

            act.wait_ge(zero_done, 4)
            ada(0, 0)
            for l in range(DEPTH):
                act.wait_ge(mods_ok, 2 * l + 1)
                norm(l, 0)
                if l == 0:
                    ada(0, 1)

                for u in range(18):
                    if u % 2 == 0:
                        act.wait_ge(proj_ps, 18 * l + u + 1)
                        dst, src = PROJ_EVAC[u](pT, v_tok, i_tok, ps)
                        A_(dst, src, ACT.Copy).then_inc(proj_act, 1)
                    if u in AFTER:
                        kind, i = AFTER[u]
                        {"gate": gate, "silu": silu, "qk": qk}[kind](l, i)
                act.wait_ge(proj_act, 9 * (l + 1))
                act.wait_ge(proj_dve, 9 * (l + 1))
                act.dma_start(o_cv[0, l].rearrange("t h d -> t (h d)"), v_tok[:, 0, :]).then_inc(cache_out, 16)
                act.wait_ge(ck_ps, l + 1)
                if l > 0:
                    act.wait_ge(cache_out, 16 * 2 * l)
                A_(kout, bank(5, P), ACT.Copy).then_inc(ko_sb, 1)
                act.wait_ge(ko_sb, l + 1)
                act.dma_start(o_ck[0, l].rearrange("t h d -> t (h d)"), kout).then_inc(cache_out, 16)

                for i in range(NU + 2):
                    if i < NU:
                        n = l * NU + i
                        w = P if i % TT == 0 else TOK
                        act.wait_ge(sc_max, n + 1)
                        if i >= 3:
                            act.wait_ge(pt_ps, n - 2)
                        A_(scr[:, PBUF[i % 3], 0:w], ps[:, 1024 * (i % 2):1024 * (i % 2) + w], ACT.Exp,
                           scale=HD ** -0.5, bias=st[:, i % 3, 1:2], accum_out=st[:, i % 3, 2:3]).then_inc(sc_exp, 1)
                    if i >= 2:
                        n = l * NU + i - 2
                        w = P if (i - 2) % TT == 0 else TOK
                        act.wait_ge(pt_ps, n + 1)
                        if i >= 4:
                            act.wait_ge(av_ps, n - 1)
                        A_(scr[:, 6 + i % 2, 0:w], ps[:, 2048:2048 + w], ACT.Copy).then_inc(pt_sb, 1)

                for p in range(2):
                    for d in range(2):
                        u = (l * 2 + p) * 2 + d
                        act.wait_ge(gt_ok, 4 * l + 4)
                        if u >= 1:
                            act.wait_ge(inter_ps, u)
                            act.wait_ge(s_ok, u)
                        A_(scr[:, 8, :], pT[:, C_HF + 2 * d + p, :], ACT.Exp).then_inc(dk_e, 1)
                        act.wait_ge(dk_d, u + 1)
                        A_(scr[:, 10, :], scr[:, 10, :], ACT.Exp).then_inc(dk_e, 1)
                        for i in range(6):
                            n = u * 6 + i
                            act.wait_ge(lv_d, 2 * (n + 1))
                            A_(scr[:, 2 + i % 2, :], scr[:, 2 + i % 2, :], ACT.Exp).then_inc(lv_e, 1)
                        act.wait_ge(s_ok, u + 1)
                        for h in range(2):
                            hs = slice(64 * h, 64 * h + 64)
                            act.dma_start((o_sf, o_sb)[d][0, l, 2 * p + h], S[hs, 1, hs]).then_inc(state_out, 16)
                    n = 2 * l + p
                    act.wait_ge(intra_ps, 2 * n + 2)
                    r = scr[:, 0, :]
                    A_(r, ps[:, 3072:3072 + TOK], ACT.Square).then_inc(on_sq, 1)
                    act.wait_ge(on_sum, n + 1)
                    seq(A_(r, ps[:, 0:TOK], ACT.Ln, scale=1.0 / HD, bias=eps_t[:, 0:1]))
                    A_(r, r, ACT.Exp, scale=-0.5).then_inc(on_rs, 1)
                for p in range(2):
                    n = 2 * l + p
                    act.wait_ge(f_o, n + 1)
                    A_(pT[:, C_FT + p, NP:], bank(6), ACT.Copy).then_inc(f_os, 1)
                    A_(pT[:, C_FT + p, 0:NP], bank(7, NP), ACT.Copy).then_inc(f_os, 1)

                norm(l, 1)
                for t in range(TT):
                    n = l * TT + t
                    act.wait_ge(hr_ps, n + 1)
                    if nth(l, TT, t) > 1:
                        act.wait_ge(hr_out[t % 2], 16 * (nth(l, TT, t) - 1))
                    A_(hrow[:, t % 2, :], ps[:, 1024 * (t % 2):1024 * (t % 2) + D], ACT.Copy).then_inc(hr_sb, 1)
                    act.wait_ge(hr_sb, n + 1)
                    act.dma_start(h_dram[t * P:(t + 1) * P, :], hrow[:, t % 2, :]).then_inc(hr_out[t % 2], 16)

                if l + 1 < DEPTH:
                    ada(l + 1, 0)
                act.wait_ge(rt_m, 2 * l + 1)
                A_(rt[:, 130:150], rt[:, 130:150], ACT.Exp).then_inc(rt_e, 1)
                A_(rt[:, 360:365], rt[:, 360:365], ACT.Exp).then_inc(rt_e, 1)

                for i in range(MT + 2):
                    if i < MT:
                        n = l * MT + i
                        act.wait_ge(xg_ps, n + 1)
                        if n >= 2:
                            act.wait_ge(gu_ps, n - 1)
                        A_(xgT[:, i % 2], ps[:, 0:1024].rearrange("p (k t) -> p k t", k=KC), ACT.Copy).then_inc(xg_sb, 1)
                    if 1 <= i <= MT:
                        n = l * MT + i - 1
                        j = (i - 1) % 2
                        act.wait_ge(gu_ps, n + 1)
                        if n >= 2:
                            act.wait_ge(hid_ok, n - 1)
                        A_(sg[:, j, :], bank(2 + j, DE), ACT.Silu).then_inc(gu_s, 1)
                    if i >= 2:
                        n = l * MT + i - 2
                        j = (i - 2) % 2
                        act.wait_ge(dn_sb, n + 1)
                        act.dma_start(y_dram[(i - 2) * P:(i - 1) * P, :], yb[:, j, :]).then_inc(y_out[j], 16)
                if l + 1 < DEPTH:
                    ada(l + 1, 1)

            for t in range(TT):
                act.wait_ge(fin_ps, t + 1)
                A_(xrow[:, t, :], ps[:, 1024 * (t % 2):1024 * (t % 2) + D], ACT.Copy).then_inc(fin_sb, 1)
                act.wait_ge(fin_sb, t + 1)
                dst = y_prompt[0] if t == 0 else y_sample[0, (t - 1) * P:t * P, :]
                act.dma_start(dst, xrow[:, t, :]).then_inc(fin_out, 16)

        @block.vector
        def _(dve):
            steps = [0]
            V = nc.vector

            def seq(ins):
                steps[0] += 1
                ins.then_inc(dve_step, 1)
                dve.wait_ge(dve_step, steps[0])

            dve.wait_ge(par_ps, 3)
            V.tensor_copy(ckT[:], bank(5, 2 * P).rearrange("p (l t) -> p l t", l=2)).then_inc(ck_sb, 1)
            seq(V.tensor_copy(par[:, PB0:PB0 + 96], bank(4, 96, PB0)))
            V.tensor_copy(par[:, 0:PA_ROWS], bank(4, PA_ROWS)).then_inc(par_sb, 1)
            dve.wait_ge(cond_e, 1)
            dve.wait_ge(par_sb, 1)
            seq(V.tensor_scalar(csc[:, 0, :], csc[:, 0, :], 1.0, None, ALU.add))
            seq(V.reciprocal(csc[:, 1, :], csc[:, 0, :]))
            V.tensor_tensor(cond[:].rearrange("p g k -> p (g k)"), par[:, PA_COND:PA_COND + 16], csc[:, 1, :],
                            ALU.mult).then_inc(cond_ok, 1)
            l0, l1 = par[:, PA_LB:PA_LB + 4], par[:, PA_LB + 4:PA_LB + 8]
            seq(V.tensor_tensor(lb[:, 0, :], l0, l1, ALU.max))
            seq(V.tensor_tensor(lbt[:, 0, :], l0, lb[:, 0, :], ALU.subtract))
            V.tensor_tensor(lbt[:, 2, :], l1, lb[:, 0, :], ALU.subtract).then_inc(lb_d, 1)
            dve.wait_ge(lb_e, 2)
            seq(V.tensor_tensor(lbt[:, 0, :], lbt[:, 1, :], lbt[:, 3, :], ALU.add))
            seq(V.reciprocal(lbt[:, 2, :], lbt[:, 0, :]))
            seq(V.tensor_tensor(lb[:, 1, :], lbt[:, 3, :], lbt[:, 2, :], ALU.mult))
            seq(V.memset(lb[:, 0, :], 0.0))
            seq(V.tensor_scalar(omlb[:], lb[:], -1.0, 1.0, ALU.mult, ALU.add))
            for t in range(TT):
                if t % 2 == 1:
                    dve.wait_ge(xt_ps, t + 1)
                    V.tensor_copy(xT[:, :, t * P:(t + 1) * P], ps[:, 1024:2048].rearrange("p (k t) -> p k t", k=KC)).then_inc(xt_dve, 1)
            dve.wait_ge(consts_in, 16 * N_CONST)
            seq(V.tensor_copy(tokid[:], K["tileno"][:, 40:40 + TT]))
            seq(V.tensor_copy(K["lvl"][:], lvl_f))

            def norm(l, which):
                n0 = (l * 2 + which) * KC
                dve.wait_ge(nrs, 2 * l + which + 1)
                rs = scr[:, 2, :]
                for k in range(KC):
                    for g, a, b in GROUPS:
                        r = rs[:, NS:] if g == 0 else rs[:, 0:NS]
                        V.scalar_tensor_tensor(hT[:, k, a:b], xT[:, k, a:b], amul[:, l, which, k, g:g + 1], r,
                                               ALU.mult, ALU.mult).then_inc(nscaled, 1)

            def modulations(l, half):
                dve.wait_ge(ada_tr, (2 * l + half + 1) * ADA_HALF)
                at = PB0 + 48 * l + 24 * half
                bias = par[:, at:at + 24].unsqueeze(2).to_broadcast([P, 24, 2])
                seq(V.tensor_tensor(mods[:, l, 3 * half:3 * half + 3].rearrange("p s k g -> p (s k) g"),
                                    bank(7, 48).rearrange("p (n g) -> p n g", g=2), bias, ALU.add))
                at = (PA_N1, PA_N2)[half] + 8 * l
                w = par[:, at:at + 8].unsqueeze(2).to_broadcast([P, KC, 2])
                V.scalar_tensor_tensor(amul[:, l, half], mods[:, l, 3 * half + 1], 1.0, w, ALU.add, ALU.mult).then_inc(mods_ok, 1)
                dve.wait_ge(mods_ok, 2 * l + half + 1)

            def evacuated(l, u):
                dve.wait_ge(proj_act if u % 2 == 0 else proj_dve, 9 * l + u // 2 + 1)

            def silu(l, i):
                c, n, e = GATE_CHUNKS[i], 4 * l + i, scr[:, i % 2, :]
                dve.wait_ge(sl_e, n + 1)
                seq(V.tensor_scalar(e, e, 1.0, None, ALU.add))
                seq(V.reciprocal(e, e))
                V.tensor_tensor(pT[:, c, :], pT[:, c, :], e, ALU.mult).then_inc(sl_ok, 1)

            def gate(l, i):
                d, n = i // 2, 4 * l + i
                z = pT[:, C_HF + i, :]
                ep, en, tp, tn = (scr[:, j, :] for j in (2, 3, 4, 5))
                lnden, den, lnnum, num, rden = (scr[:, j, :] for j in (6, 7, 8, 9, 10))
                evacuated(l, i)
                V.tensor_scalar(tp, z, 0.0, None, ALU.min).then_inc(gt_in, 1)
                V.tensor_scalar(tn, z, -1.0, 0.0, ALU.mult, ALU.min).then_inc(gt_in, 1)
                dve.wait_ge(gt_e, 2 * (n + 1))
                if l > 0:
                    seq(V.scalar_tensor_tensor(num, en, lb[:, l, i:i + 1], ep, ALU.mult, ALU.add))
                V.tensor_tensor(den, ep, en, ALU.add).then_inc(gt_den, 1)
                dve.wait_ge(gt_den, n + 1)
                seq(V.reciprocal(rden, den))
                seq(V.scalar_tensor_tensor(decayed[:, i, :], en, omlb[:, l, i:i + 1], rden, ALU.mult, ALU.mult))
                dve.wait_ge(gt_ln, n + 1 if l == 0 else 4 + 2 * (n + 1 - 4))
                if l == 0:
                    seq(V.tensor_tensor(tn, tp, lnden, ALU.subtract))
                else:
                    seq(V.tensor_scalar(tp, z, 80.0, 0.0, ALU.add, ALU.min))
                    seq(V.tensor_tensor(tn, lnnum, lnden, ALU.subtract))
                    seq(V.tensor_tensor(tn, tn, tp, ALU.add))
                way = slice(None, None, 1 if d == 0 else -1)
                V.tensor_tensor_scan(out=z[:, way], data0=K["restart"][:], data1=tn[:, way], initial=0.0,
                                     op0=ALU.mult, op1=ALU.add).then_inc(gt_ok, 1)
                dve.wait_ge(gt_ok, n + 1)

            def qk(l, i):
                if i < 5:
                    n, c = l * 5 + i, QK_CHUNKS[i]
                    at = (PA_QN if c < 4 else PA_KN) + l
                    dve.wait_ge(qrs, n + 1)
                    V.scalar_tensor_tensor(pT[:, c, :], pT[:, c, :], par[:, at:at + 1], scr[:, i % 2, :],
                                           ALU.mult, ALU.mult).then_inc(qnorm, 1)
                if i >= 1:
                    n, c = l * 5 + i - 1, QK_CHUNKS[i - 1]
                    dve.wait_ge(qrot, n + 1)
                    if n >= 1:
                        dve.wait_ge(qk_ok, n)
                    seq(V.tensor_tensor(scr[:, 4, 0:NS], bank(4 + (i - 1) % 2), K["sinT"][:], ALU.mult))
                    dve.wait_ge(qcos, n + 1)
                    V.tensor_tensor(pT[:, c, NP:], scr[:, 4, 0:NS], scr[:, 2 + (i - 1) % 2, 0:NS], ALU.add).then_inc(qk_ok, 1)

            modulations(0, 0)
            for l in range(DEPTH):
                x_whole(dve, l)
                norm(l, 0)
                if l == 0:
                    modulations(0, 1)

                for u in range(18):
                    if u % 2 == 1:
                        dve.wait_ge(proj_ps, 18 * l + u + 1)
                        dst, src = PROJ_EVAC[u](pT, v_tok, i_tok, ps)
                        V.tensor_copy(dst, src).then_inc(proj_dve, 1)
                    if u in AFTER:
                        kind, i = AFTER[u]
                        {"gate": gate, "silu": silu, "qk": qk}[kind](l, i)

                for i in range(NU + 3):
                    if i < NU:
                        n = l * NU + i
                        w = P if i % TT == 0 else TOK
                        dve.wait_ge(sc_ps, n + 1)
                        if i >= 3:
                            dve.wait_ge(sc_exp, n - 2)
                        seq(V.tensor_reduce(st[:, i % 3, 0:1], ps[:, 1024 * (i % 2):1024 * (i % 2) + w], AX_X, ALU.max))
                        V.tensor_scalar(st[:, i % 3, 1:2], st[:, i % 3, 0:1], -HD ** -0.5, None, ALU.mult).then_inc(sc_max, 1)
                    if 1 <= i <= NU:
                        n = l * NU + i - 1
                        j = (i - 1) % 3
                        w = P if (i - 1) % TT == 0 else TOK
                        dve.wait_ge(sc_exp, n + 1)
                        seq(V.reciprocal(st[:, j, 3:4], st[:, j, 2:3]))
                        V.tensor_scalar(scr[:, PBUF[j], 0:w], scr[:, PBUF[j], 0:w], st[:, j, 3:4], None, ALU.mult).then_inc(sc_norm, 1)
                    if i >= 3:
                        n = l * NU + i - 3
                        h, t = (i - 3) // TT, (i - 3) % TT
                        c, b = h // 2, h % 2
                        dve.wait_ge(av_ps, n + 1)
                        V.tensor_copy(pT[64 * b:64 * b + 64, c, t * P:(t + 1) * P],
                                      bank(6 + (i - 3) % 2, P)[64 * b:64 * b + 64, :]).then_inc(av_sb, 1)

                for p in range(2):
                    for d in range(2):
                        u = (l * 2 + p) * 2 + d
                        b = pT[:, C_HF + 2 * d + p, :]
                        bv = b.rearrange("p (n m) -> p n m", m=CH)
                        q, k = pT[:, C_HQ + p, :], decayed[:, 2 * d + p, :]
                        eb, qd, kd = scr[:, 8, :], scr[:, 9, :], scr[:, 10, :]
                        end = CH - 1 if d == 0 else 0
                        if u >= 1:
                            dve.wait_ge(inter_ps, u)
                        V.tensor_tensor(kd.rearrange("p (n m) -> p n m", m=CH),
                                        bv[:, :, end:end + 1].to_broadcast([P, NCH, CH]), bv, ALU.subtract).then_inc(dk_d, 1)
                        dve.wait_ge(dk_e, 2 * (u + 1))
                        V.tensor_tensor(kd, kd, k, ALU.mult).then_inc(dk_ok, 1)
                        V.tensor_tensor(qd, q, eb, ALU.mult).then_inc(dk_ok, 1)
                        g0 = u * 9
                        dve.wait_ge(g_ps, g0 + 1)
                        if p == 0 and d == 0:
                            dve.wait_ge(cache_out, 16 * 2 * (l + 1))
                        V.tensor_copy(scr[:, 11, :], ps[:, 1536 * ((g0) % 2):1536 * ((g0) % 2) + TOK]).then_inc(g_used, 1)
                        dve.wait_ge(g_ps, g0 + 2)
                        o = 1536 * ((g0 + 1) % 2)
                        if u >= 1:
                            dve.wait_ge(state_out, 32 * u)
                        for i, cnt in ((1, 4), (0, 5)):
                            ins = V.tensor_tensor(S[:, i::2, :], ps[:, o + 1024 * i:o + 1024 * i + cnt * P].rearrange("p (n v) -> p n v", v=P),
                                                  blockones[:].unsqueeze(1).to_broadcast([P, cnt, P]), ALU.mult)
                            if i == 1:
                                seq(ins)
                        ins.then_inc(g_used, 1)
                        dve.wait_ge(g_used, g0 + 2)
                        order = list(range(NCH)) if d == 0 else list(range(PROMPT_CH))[::-1] + list(range(PROMPT_CH, NCH))[::-1]
                        seq(V.scalar_tensor_tensor(S[:, 1, :], S[:, 0, :], eb[:, order[1] * CH + end:order[1] * CH + end + 1],
                                                   S[:, 1, :], ALU.mult, ALU.add))
                        for i in range(7):
                            ch = order[PROMPT_CH + i]
                            prev = s_init[:, l, d, p, :] if i == 0 else S[:, 1 + i, :]
                            ins = V.scalar_tensor_tensor(S[:, 2 + i, :], prev, eb[:, ch * CH + end:ch * CH + end + 1],
                                                         S[:, 2 + i, :], ALU.mult, ALU.add)
                            if i < 6:
                                seq(ins)
                            else:
                                ins.then_inc(s_ok, 1)
                        for i in range(7):
                            if i < 6:
                                m = HALVES[i]
                                n = u * 6 + i
                                dve.wait_ge(lv_e, n + 1)
                                if n >= 2:
                                    dve.wait_ge(g_ps, (n - 2) // 6 * 9 + (n - 2) % 6 + 4)
                                ev, qv, kv, ov = (x.rearrange("p (n m) -> p n m", m=2 * m) for x in
                                                  (scr[:, 2 + i % 2, :], q, k, scr[:, 6 + i % 2, :]))
                                qs, ks = (slice(m, 2 * m), slice(0, m)) if d == 0 else (slice(0, m), slice(m, 2 * m))
                                V.tensor_tensor(ov[:, :, qs], qv[:, :, qs], ev[:, :, qs], ALU.mult).then_inc(lv_ok, 1)
                                V.tensor_tensor(ov[:, :, ks], kv[:, :, ks], ev[:, :, ks], ALU.mult).then_inc(lv_ok, 1)
                            g = g0 + 2 + i
                            o = 1536 * (g % 2)
                            scores = ps[:, o:o + 1280].rearrange("p (n t) -> p n t", t=P)
                            dve.wait_ge(g_ps, g + 1)
                            if i == 0:
                                if u >= 1:
                                    dve.wait_ge(intra_ps, u)
                                V.tensor_tensor(aT, scores, ident[:].unsqueeze(1).to_broadcast([P, 10, P]), ALU.mult).then_inc(g_used, 1)
                            else:
                                mask = K["lvl"][:, d, i - 1, :].unsqueeze(1).to_broadcast([P, 10, P])
                                dve.wait_ge(g_used, g)
                                V.copy_predicated(aT, mask, scores).then_inc(g_used, 1)
                    n = 2 * l + p
                    dve.wait_ge(on_rs, n + 1)
                    seq(V.scalar_tensor_tensor(scr[:, 1, :], ps[:, 3072:3072 + TOK], par[:, PA_HN + l:PA_HN + l + 1],
                                               scr[:, 0, :], ALU.mult, ALU.mult))
                    V.tensor_tensor(pT[:, C_HG + p, :], pT[:, C_HG + p, :], scr[:, 1, :], ALU.mult).then_inc(on_ok, 1)

                dve.wait_ge(f_ab, l + 1)
                V.tensor_copy(scr_flat[:, 0:512], bank(6)).then_inc(f_abs, 1)
                for p in range(2):
                    n = 2 * l + p
                    dve.wait_ge(f_z, n + 1)
                    V.tensor_copy(scr_flat[:, 1280 * (1 + p):1280 * (2 + p)], ps[:, 1536 * p:1536 * p + 1280]).then_inc(f_zs, 1)

                for c in range(KC):
                    n = l * KC + c
                    dve.wait_ge(op_ps, n + 1)
                    for g, a, b in GROUPS:
                        V.scalar_tensor_tensor(xT[:, c, a:b], ps[:, 1024 * (c % 3) + a:1024 * (c % 3) + b],
                                               mods[:, l, 2, c, g:g + 1], xT[:, c, a:b], ALU.mult, ALU.add).then_inc(x_mid, 1)
                dve.wait_ge(x_mid, 2 * KC * (l + 1))
                dve.wait_ge(state_out, 16 * 8 * (l + 1))
                norm(l, 1)

                dve.wait_ge(lg_ps, l + 1)
                R = lambda at, n: rt[:, at:at + n]
                lg = R(0, 100).rearrange("p (t e) -> p t e", t=TT)
                V.tensor_copy(lg, bank(7, 100).rearrange("p (t e) -> p t e", t=TT)).then_inc(lg_sb, 1)
                dve.wait_ge(lg_sb, l + 1)
                lgg, lge = lg[:, :, 0:NEG], lg[:, :, NEG:]
                gmax = R(100, 5).unsqueeze(2)
                t4 = R(110, 20).rearrange("p (t e) -> p t e", t=TT)
                u4 = R(130, 20).rearrange("p (t e) -> p t e", t=TT)
                s5 = R(150, 5).unsqueeze(2)
                ohg = R(160, 20).rearrange("p (t e) -> p t e", t=TT)
                gw = R(180, 5).unsqueeze(2)
                iota4 = K["tileno"][:, 32:36].unsqueeze(1).to_broadcast([P, TT, 4])

                def first_max(vals, mx, onehot):
                    seq(V.tensor_reduce(mx, vals, AX_X, ALU.max))
                    seq(V.tensor_tensor(t4, vals, mx.to_broadcast([P, TT, 4]), ALU.is_lt))
                    seq(V.scalar_tensor_tensor(t4, t4, 8.0, iota4, ALU.mult, ALU.add))
                    seq(V.tensor_reduce(s5, t4, AX_X, ALU.min))
                    seq(V.tensor_tensor(onehot, iota4, s5.to_broadcast([P, TT, 4]), ALU.is_equal))

                first_max(lgg, gmax, ohg)
                seq(V.tensor_tensor(u4, lgg, gmax.to_broadcast([P, TT, 4]), ALU.subtract))
                les = R(190, 20).rearrange("p (t e) -> p t e", t=TT)
                big = R(210, 80).rearrange("p (t e g) -> p t e g", t=TT, e=4)
                for t in range(TT):
                    seq(V.tensor_tensor(big[:, t], lge[:, t].rearrange("p (g e) -> p e g", g=4),
                                        ohg[:, t:t + 1, :].to_broadcast([P, 4, 4]), ALU.mult))
                seq(V.tensor_reduce(les, big, AX_X, ALU.add))
                m1, m2 = R(290, 5).unsqueeze(2), R(295, 5).unsqueeze(2)
                oh1 = R(300, 20).rearrange("p (t e) -> p t e", t=TT)
                oh2 = R(320, 20).rearrange("p (t e) -> p t e", t=TT)
                le2 = R(340, 20).rearrange("p (t e) -> p t e", t=TT)
                first_max(les, m1, oh1)
                seq(V.tensor_scalar(le2, oh1, -1.0, 1.0, ALU.mult, ALU.add))
                seq(V.tensor_tensor(le2, le2, les, ALU.mult))
                seq(V.scalar_tensor_tensor(le2, oh1, -BIG, le2, ALU.mult, ALU.add))
                first_max(le2, m2, oh2)
                V.tensor_tensor(R(360, 5).unsqueeze(2), m2, m1, ALU.subtract).then_inc(rt_m, 1)
                o1 = R(400, 80).rearrange("p (t e) -> p t e", t=TT)
                o2 = R(480, 80).rearrange("p (t e) -> p t e", t=TT)
                both = R(560, 80)
                for t in range(TT):
                    for o, oh in ((o1, oh1), (o2, oh2)):
                        seq(V.tensor_tensor(o[:, t].rearrange("p (g e) -> p g e", g=4),
                                            ohg[:, t, :].unsqueeze(2).to_broadcast([P, 4, 4]),
                                            oh[:, t:t + 1, :].to_broadcast([P, 4, 4]), ALU.mult))
                V.tensor_tensor(both, R(400, 80), R(480, 80), ALU.add).then_inc(rt_m, 1)
                dve.wait_ge(rt_e, 2 * (l + 1))
                e4 = R(130, 20).rearrange("p (t e) -> p t e", t=TT)
                seq(V.tensor_reduce(gw, e4, AX_X, ALU.add))
                e21 = R(360, 5).unsqueeze(2)
                seq(V.tensor_scalar(R(365, 5), R(360, 5), 1.0, None, ALU.add))
                seq(V.tensor_tensor(R(370, 5), R(365, 5), R(180, 5), ALU.mult))
                seq(V.reciprocal(R(375, 5), R(370, 5)))
                seq(V.tensor_copy(wgt[:, :, 0], R(375, 5)))
                seq(V.tensor_tensor(wgt[:, :, 1], R(375, 5), R(360, 5), ALU.mult))
                dve.wait_ge(rk_ps, l + 1)
                cnt, ntl, inc, exc = R(640, 16), R(656, 16), R(672, 16), R(100, 16)
                seq(V.tensor_copy(cnt, bank(6, 16, 80)))
                seq(V.tensor_scalar(ntl, cnt, 0.0, None, ALU.is_gt))
                for j in range(1, TT):
                    seq(V.scalar_tensor_tensor(ntl, cnt, float(P * j), ntl, ALU.is_gt, ALU.add))
                seq(V.tensor_tensor_scan(out=inc, data0=ones[:, 0:16], data1=ntl, initial=0.0, op0=ALU.mult, op1=ALU.add))
                seq(V.tensor_tensor(exc, inc, ntl, ALU.subtract))
                pos = R(210, 80)
                seq(V.scalar_tensor_tensor(pos.rearrange("p (t e) -> p t e", t=TT),
                                           exc.unsqueeze(1).to_broadcast([P, TT, 16]), float(P),
                                           bank(6, 80).rearrange("p (t e) -> p t e", t=TT), ALU.mult, ALU.add))
                for c, o in enumerate((R(400, 80), R(480, 80))):
                    seq(V.tensor_tensor(o, o, pos, ALU.mult))
                    seq(V.tensor_reduce(R(380 + 5 * c, 5), o.rearrange("p (t e) -> p t e", t=TT), AX_X, ALU.add))
                    if l > 0 and c == 0:
                        all_of(dve, y_in, l - 1, TT, 32)
                    seq(V.tensor_copy(slot_i[:, :, c], R(380 + 5 * c, 5)))
                cmp = scr_flat[:, 7000:7000 + MT * 16].rearrange("p (j e) -> p j e", e=16)
                seq(V.tensor_tensor(cmp, inc.unsqueeze(1).to_broadcast([P, MT, 16]),
                                    K["tileno"][:, 0:MT].unsqueeze(2).to_broadcast([P, MT, 16]), ALU.is_le))
                seq(V.tensor_reduce(R(110, MT), cmp, AX_X, ALU.add))
                seq(V.tensor_scalar(R(110, MT), R(110, MT), float(NE - 1), None, ALU.min))
                V.tensor_copy(tile_e[:, 0:MT], R(110, MT)).then_inc(rt_ok, 1)

                if l + 1 < DEPTH:
                    modulations(l + 1, 0)
                for i in range(MT + 1):
                    if i < MT:
                        n = l * MT + i
                        j = i % 2
                        dve.wait_ge(gu_s, n + 1)
                        if n >= 2:
                            dve.wait_ge(hid_ps, n - 1)
                        V.tensor_tensor(hid[:, j, :], bank(2 + j, DE, DE), sg[:, j, :], ALU.mult).then_inc(hid_ok, 1)
                        dve.wait_ge(hid_ps, n + 1)
                        if n >= 2:
                            dve.wait_ge(dn_ps, n - 1)
                        V.tensor_copy(hidT[:, j], bank(4, 256).rearrange("p (k t) -> p k t", k=2)).then_inc(hid_sb, 1)
                    if i >= 1:
                        n = l * MT + i - 1
                        j = (i - 1) % 2
                        dve.wait_ge(dn_ps, n + 1)
                        if nth(l, MT, i - 1) > 1:
                            dve.wait_ge(y_out[j], 16 * (nth(l, MT, i - 1) - 1))
                        V.tensor_copy(yb[:, j, :], ps[:, 2560:2560 + D]).then_inc(dn_sb, 1)
                for t in range(TT):
                    n = l * TT + t
                    j = t % 2
                    dve.wait_ge(y_in[j], 32 * nth(l, TT, t))
                    seq(V.tensor_scalar(y1[:, j, :], y1[:, j, :], wgt[:, t, 0:1], None, ALU.mult))
                    V.scalar_tensor_tensor(y2[:, j, :], y2[:, j, :], wgt[:, t, 1:2], y1[:, j, :], ALU.mult, ALU.add).then_inc(y_sum, 1)
                    dve.wait_ge(yt_ps, n + 1)
                    g = 0 if t == 0 else 1
                    for k in range(KC):
                        V.scalar_tensor_tensor(xT[:, k, t * P:(t + 1) * P],
                                               ps[:, 1024 * j + k * P:1024 * j + (k + 1) * P],
                                               mods[:, l, 5, k, g:g + 1], xT[:, k, t * P:(t + 1) * P],
                                               ALU.mult, ALU.add).then_inc(x_new, 1)
                if l + 1 < DEPTH:
                    modulations(l + 1, 1)

        @block.tensor
        def _(pe):
            mm = nc.tensor.matmul

            def item(n):
                pe.wait_ge(slot_in[n % RING], landed[n])
                return slot(n)

            def columns(out, lhs, rhs, parts, start, stop, **kw):
                for a, b in parts:
                    ins = mm(out[:, a:b], lhs, rhs[:, a:b], start=start, stop=stop, **kw)
                return ins

            WIDE = ((0, 512), (512, TOK))

            pe.wait_ge(x_in, 48)
            pe.wait_ge(params_in, 16 * (N_PARAM_DMAS + 4))
            nc.tensor.transpose(bank(4, PA_ROWS), rows[0:PA_ROWS, 0, :], ident[0:PA_ROWS, 0:PA_ROWS]).then_inc(par_ps, 1)
            nc.tensor.transpose(bank(4, 96, PB0), rows[0:96, 1, :], ident[0:96, 0:96]).then_inc(par_ps, 1)
            for l in range(DEPTH):
                last = nc.tensor.transpose(bank(5, P, P * l), ck_row[:, l, :], ident[:])
            last.then_inc(par_ps, 1)
            for t in range(TT):
                if t >= 2:
                    pe.wait_ge(xt_act if t % 2 == 0 else xt_dve, t // 2)
                for k in range(KC):
                    last = nc.tensor.transpose(ps[:, 1024 * (t % 2) + k * P:1024 * (t % 2) + (k + 1) * P],
                                               xrow[:, t, k * P:(k + 1) * P], ident[:])
                last.then_inc(xt_ps, 1)
            pe.wait_ge(cond_ok, 1)
            pe.wait_ge(consts_in, 16 * N_CONST)
            pe.wait_ge(late_in, 16 * 16 * DEPTH)
            pe.wait_ge(ck_sb, 1)

            def norm(l, which):
                n0 = (l * 2 + which) * KC
                for k in range(KC):
                    pe.wait_ge(nsq, n0 + k + 1)
                    sq = scr[:, k % 2, :]
                    mm(bank(5), ones[:], sq[:, NP:], start=(k == 0), stop=(k == KC - 1))
                    mm(bank(6, NP), ones[:], sq[:, 0:NP], start=(k == 0), stop=(k == KC - 1)).then_inc(nsum, 1)

            def ada(l, half, first, end):
                for i in range(first, end + (end == ADA_HALF)):
                    n = (2 * l + half) * ADA_HALF + i
                    if i < ADA_HALF:
                        w = item(ITEM["ada", l, ADA_HALF * half + i]).rearrange("p (k n) -> p k n", k=KC)
                        if n >= 2:
                            pe.wait_ge(ada_sb, n - 1)
                        for k in range(KC):
                            last = mm(bank(4 + i % 2, 256)[0:2, :], cond[:, :, k], w[:, k, :], start=(k == 0), stop=(k == KC - 1))
                        last.then_inc(ada_ps, 1)
                    if i >= 1:
                        pe.wait_ge(ada_sb, n)
                        for j in range(2):
                            last = nc.tensor.transpose(bank(7, 2, 4 * (i - 1) + 2 * j), mrow[:, (i - 1) % 2, j * P:(j + 1) * P],
                                                       ident[0:2, 0:2])
                        last.then_inc(ada_tr, 1)

            ada(0, 0, 0, ADA_HALF)
            for l in range(DEPTH):
                norm(l, 0)
                if l == 0:
                    pe.wait_ge(mods_ok, 1)
                    pe.wait_ge(nrs, 1)
                    ada(0, 1, 0, ADA_HALF)
                pe.wait_ge(h_ok, 2 * KC * (2 * l + 1))

                def unit(u):
                    if u >= 2:
                        pe.wait_ge(proj_act if u % 2 == 0 else proj_dve, 9 * l + (u - 2) // 2 + 1)
                    return ps[:, 1024 * (u % 2):1024 * (u % 2) + 1024]

                def qk(i):
                    if i < 5:
                        n = l * 5 + i
                        pe.wait_ge(qsq, n + 1)
                        if i >= 1:
                            pe.wait_ge(qrs, n)
                        columns(ps[:, 3072:4096], blockones[:], scr[:, i % 2, :], WIDE, True, True).then_inc(qsum, 1)
                    if i >= 1:
                        n, c = l * 5 + i - 1, QK_CHUNKS[i - 1]
                        pe.wait_ge(qnorm, n + 1)
                        if i >= 3:
                            pe.wait_ge(qk_ok, n - 1)
                        mm(bank(4 + (i - 1) % 2), rot[:], pT[:, c, NP:], start=True, stop=True).then_inc(qrot, 1)

                for i, c0 in enumerate(IN_ORDER):
                    w = item(ITEM["in", l, i]).rearrange("p (k n) -> p k n", k=KC)
                    for j in range(2):
                        u = 2 * i + j
                        out = unit(u)
                        if c0 != 6 and (c0, j) != (2, 1):
                            for k in range(KC):
                                last = columns(out, w[:, k, j * P:(j + 1) * P], hT[:, k, :], WIDE, k == 0, k == KC - 1)
                        else:
                            if c0 == 2:
                                tiles, a, width = range(TT), P, P
                            else:
                                tiles, a, width = (range(4) if j == 0 else range(4, 5)), 0, 256
                            for s, t in enumerate(tiles):
                                for k in range(KC):
                                    last = mm(out[:, s * width:(s + 1) * width], hT[:, k, t * P:(t + 1) * P],
                                              w[:, k, a:a + width], start=(k == 0), stop=(k == KC - 1))
                        last.then_inc(proj_ps, 1)
                        if u in AFTER and AFTER[u][0] == "qk":
                            qk(AFTER[u][1])
                pe.wait_ge(qk_ok, 5 * (l + 1))
                nc.tensor.transpose(bank(5, P), pT[:, C_K, 0:NP], ident[:]).then_inc(ck_ps, 1)
                pe.wait_ge(proj_act, 9 * (l + 1))
                pe.wait_ge(proj_dve, 9 * (l + 1))

                for i in range(NU + 3):
                    if i < NU:
                        n = l * NU + i
                        h, t = i // TT, i % TT
                        c, b = h // 2, slice(64 * (h % 2), 64 * (h % 2) + 64)
                        if i >= 2:
                            pe.wait_ge(sc_exp, n - 1)
                        out = ps[:, 1024 * (i % 2):1024 * (i % 2) + 1024]
                        q = pT[b, c, t * P:(t + 1) * P]
                        if t == 0:
                            last = mm(out[:, 0:P], q, pT[b, C_K, 0:NP], start=True, stop=True)
                        else:
                            mm(out[:, 0:NS], q, pT[b, C_K, NP:], start=True, stop=True)
                            last = mm(out[:, NS:NS + P], q, ckT[b, l, :], start=True, stop=True)
                        last.then_inc(sc_ps, 1)
                    if 2 <= i <= NU + 1:
                        n = l * NU + i - 2
                        if i == 2:
                            pe.wait_ge(ko_sb, l + 1)
                        pe.wait_ge(sc_norm, n + 1)
                        if i >= 3:
                            pe.wait_ge(pt_sb, n)
                        for s in range(1 if (i - 2) % TT == 0 else 5):
                            last = nc.tensor.transpose(ps[:, 2048 + s * P:2048 + (s + 1) * P],
                                                       scr[:, PBUF[(i - 2) % 3], s * P:(s + 1) * P], ident[:])
                        last.then_inc(pt_ps, 1)
                    if i >= 3:
                        n = l * NU + i - 3
                        h, t = (i - 3) // TT, (i - 3) % TT
                        b = slice(64 * (h % 2), 64 * (h % 2) + 64)
                        pe.wait_ge(pt_sb, n + 1)
                        if i >= 5:
                            pe.wait_ge(av_sb, n - 1)
                        keys = [v_tok[:, 0, b]] if t == 0 else [v_tok[:, 1 + s, b] for s in range(4)] + [cv_tok[:, l, b]]
                        for s, v in enumerate(keys):
                            last = mm(bank(6 + (i - 3) % 2, P)[b, :], v, scr[:, 6 + (i - 3) % 2, s * P:(s + 1) * P],
                                      start=(s == 0), stop=(s == len(keys) - 1))
                        last.then_inc(av_ps, 1)

                pe.wait_ge(av_sb, NU * (l + 1))
                pe.wait_ge(sl_ok, 4 * (l + 1))
                for p in range(2):
                    for d in range(2):
                        u = (l * 2 + p) * 2 + d
                        q, k = pT[:, C_HQ + p, :], decayed[:, 2 * d + p, :]
                        g0 = u * 9
                        pe.wait_ge(gt_ok, 4 * (l + 1))

                        def buffer(g):
                            if g >= 2:
                                pe.wait_ge(g_used, g - 1)
                            return ps[:, 1536 * (g % 2):1536 * (g % 2) + 1536]
                        if d == 0 and u > 0:
                            pe.wait_ge(on_ok, 2 * l + p)
                        out = buffer(g0)
                        pe.wait_ge(dk_ok, 2 * u + 1)
                        for t in range(TT):
                            last = nc.tensor.transpose(out[:, t * P:(t + 1) * P], scr[:, 10, t * P:(t + 1) * P], ident[:])
                        last.then_inc(g_ps, 1)
                        out = buffer(g0 + 1)
                        pe.wait_ge(g_used, g0 + 1)
                        order = list(range(NCH)) if d == 0 else list(range(PROMPT_CH))[::-1] + list(range(PROMPT_CH, NCH))[::-1]
                        for i in range(9):
                            t, h = order[i] // 2, slice(64 * (order[i] % 2), 64 * (order[i] % 2) + 64)
                            at = 1024 * (i % 2) + (i // 2) * P
                            last = mm(out[:, at:at + P], scr[h, 11, t * P:(t + 1) * P],
                                      i_tok[h, t, p * P:(p + 1) * P], start=True, stop=True)
                        last.then_inc(g_ps, 1)
                        for i in range(7):
                            g = g0 + 2 + i
                            out = buffer(g)
                            if i > 0:
                                pe.wait_ge(lv_ok, 2 * (u * 6 + i))
                            kk, qq = (k, q) if i == 0 else (scr[:, 6 + (i - 1) % 2, :],) * 2
                            for s, (h, t) in enumerate(((0, 4), (0, 0), (0, 1), (0, 2), (0, 3), (1, 3), (1, 4), (1, 0), (1, 1), (1, 2))):
                                hs = slice(64 * h, 64 * h + 64)
                                if s == 7:
                                    pe.wait_ge(mid_ps, u * 7 + i + 1)
                                last = mm(out[:, (h * TT + t) * P:(h * TT + t + 1) * P],
                                          kk[hs, t * P:(t + 1) * P], qq[hs, t * P:(t + 1) * P], start=True, stop=True)
                                if s == 0:
                                    last.then_inc(mid_ps, 1)
                            last.then_inc(g_ps, 1)
                            if i == 1:
                                pe.wait_ge(s_ok, u + 1)
                                pe.wait_ge(dk_ok, 2 * u + 2)
                                for j, ch in enumerate(order):
                                    if j == 0:
                                        continue
                                    state = (S[:, 0, :] if j == 1 else s_init[:, l, d, p, :] if j == PROMPT_CH
                                             else S[:, j - 1, :])
                                    last = mm(ps[:, 3072 + ch * CH:3072 + (ch + 1) * CH], state,
                                              scr[:, 9, ch * CH:(ch + 1) * CH], start=(d == 0 and ch in (1, 8)),
                                              stop=False, skip_group_check=True)
                                last.then_inc(inter_ps, 1)
                        pe.wait_ge(g_used, g0 + 9)
                        for h in range(2):
                            for t in range(TT):
                                last = mm(ps[64 * h:64 * h + 64, 3072 + t * P:3072 + (t + 1) * P],
                                          i_tok[:, t, p * P + 64 * h:p * P + 64 * h + 64], aT[:, h * TT + t, :],
                                          start=False, stop=(d == 1), skip_group_check=True)
                        last.then_inc(intra_ps, 1)
                    n = 2 * l + p
                    pe.wait_ge(on_sq, n + 1)
                    pe.wait_ge(g_used, (u + 1) * 9)
                    columns(ps[:, 0:1024], blockones[:], scr[:, 0, :], WIDE, True, True).then_inc(on_sum, 1)

                pe.wait_ge(on_ok, 2 * (l + 1))
                for p in range(2):
                    for s in range(2):
                        last = mm(bank(6, P, (2 * p + s) * P), K["dft64"][:, s, :], wft[:, l, p, :], start=True, stop=True)
                last.then_inc(f_ab, 1)
                pe.wait_ge(f_abs, l + 1)
                for p in range(2):
                    for t in range(TT):
                        last = mm(ps[:, 1536 * p + 256 * t:1536 * p + 256 * t + 256], pT[:, C_FT + p, t * P:(t + 1) * P],
                                  scr_flat[:, 256 * p:256 * p + 256], start=True, stop=True)
                    last.then_inc(f_z, 1)
                for p in range(2):
                    n = 2 * l + p
                    pe.wait_ge(f_zs, n + 1)
                    if p == 1:
                        pe.wait_ge(f_os, 2 * n)
                    z = scr_flat[:, 1280 * (1 + p):1280 * (2 + p)].rearrange("p (t s e) -> p t s e", t=TT, s=2)
                    for i, (t, s) in enumerate((t, s) for t in range(4) for s in range(2)):
                        mm(bank(6), z[:, 1 + t, s, :], K["dft_s"][:, s, t, :], start=(i == 0), stop=(i == 7))
                    for s in range(2):
                        last = mm(bank(7, NP), z[:, 0, s, :], K["dft_p"][:, s, 0, :], start=(s == 0), stop=(s == 1))
                    last.then_inc(f_o, 1)
                pe.wait_ge(f_os, 4 * (l + 1))

                for i in range(OUT_ITEMS):
                    w = item(ITEM["out", l, i]).rearrange("p (k n) -> p k n", k=KC)
                    for j in range(2):
                        c = 2 * i + j
                        if c >= 3:
                            pe.wait_ge(x_mid, l * 2 * KC + 2 * (c - 2))
                        out = ps[:, 1024 * (c % 3):1024 * (c % 3) + 1024]
                        for k in range(KC):
                            last = columns(out, w[:, k, j * P:(j + 1) * P], pT[:, MIX[k], :], WIDE, k == 0, k == KC - 1)
                        last.then_inc(op_ps, 1)
                pe.wait_ge(x_mid, 2 * KC * (l + 1))
                norm(l, 1)
                pe.wait_ge(h_ok, 2 * KC * (2 * l + 2))
                for t in range(TT):
                    for k in range(KC):
                        mm(bank(7, 20, 20 * t), hT[:, k, t * P:(t + 1) * P], wr[:, l, k, :], start=(k == 0), stop=False)
                    last = mm(bank(7, 20, 20 * t), ones[0:1, :], br[0:1, l, :], start=False, stop=True)
                last.then_inc(lg_ps, 1)
                for t in range(TT):
                    n = l * TT + t
                    if t >= 2:
                        pe.wait_ge(hr_sb, n - 1)
                    for k in range(KC):
                        last = nc.tensor.transpose(ps[:, 1024 * (t % 2) + k * P:1024 * (t % 2) + (k + 1) * P],
                                                   hT[:, k, t * P:(t + 1) * P], ident[:])
                    last.then_inc(hr_ps, 1)
                if l + 1 < DEPTH:
                    pe.wait_ge(lg_sb, l + 1)
                    ada(l + 1, 0, 0, 5)
                pe.wait_ge(rt_m, 2 * (l + 1))
                pe.wait_ge(nrs, 2 * l + 2)
                both = rt[:, 560:640].rearrange("p (t e) -> p t e", t=TT)
                for t in range(TT + 1):
                    out = bank(6, 16, 16 * t)
                    for s in range(t):
                        last = mm(out, ones[:], both[:, s, :], start=(s == 0), stop=(t == TT and s == TT - 1))
                    if t < TT:
                        mm(out, tri[:], both[:, t, :], start=(t == 0), stop=True)
                last.then_inc(rk_ps, 1)
                if l + 1 < DEPTH:
                    ada(l + 1, 0, 5, ADA_HALF)
                    pe.wait_ge(mods_ok, 2 * l + 3)

                pe.wait_ge(hr_sb, TT * (l + 1))
                pe.wait_ge(rt_ok, l + 1)
                for i in range(MT + 2):
                    if i < MT:
                        n = l * MT + i
                        pe.wait_ge(xg_in[i % 2], 16 * nth(l, MT, i))
                        if i >= 1:
                            pe.wait_ge(xg_sb, n)
                        for k in range(KC):
                            last = nc.tensor.transpose(ps[:, k * P:(k + 1) * P], xg[:, i % 2, k * P:(k + 1) * P], ident[:])
                        last.then_inc(xg_ps, 1)
                    if i >= 1 and i <= MT:
                        n = l * MT + i - 1
                        j = (i - 1) % 2
                        pe.wait_ge(xg_sb, n + 1)
                        if i >= 3:
                            pe.wait_ge(hid_ok, n - 1)
                        for w_, half in ((0, 0), (1, DE)):
                            w = item(ITEM["up" if w_ else "gate", l, i - 1]).rearrange("p (k n) -> p k n", k=KC)
                            for k in range(KC):
                                last = mm(bank(2 + j, DE, half), xgT[:, j, k, :], w[:, k, :], start=(k == 0), stop=(k == KC - 1))
                            last.then_inc(gu_ps if w_ else gate_ps, 1)
                    if i >= 2:
                        n = l * MT + i - 2
                        j = (i - 2) % 2
                        pe.wait_ge(hid_ok, n + 1)
                        if i >= 3:
                            pe.wait_ge(hid_sb, n)
                        for k in range(2):
                            last = nc.tensor.transpose(bank(4, P, k * P), hid[:, j, k * P:(k + 1) * P], ident[:])
                        last.then_inc(hid_ps, 1)
                        pe.wait_ge(hid_sb, n + 1)
                        if i >= 3:
                            pe.wait_ge(dn_sb, n)
                        w = item(ITEM["down", l, i - 2]).rearrange("p (k n) -> p k n", k=2)
                        for half in range(2):
                            for k in range(2):
                                last = mm(bank(5 + half), hidT[:, j, k, :], w[:, k, 512 * half:512 * half + 512],
                                          start=(k == 0), stop=(k == 1))
                        last.then_inc(dn_ps, 1)
                if l + 1 < DEPTH:
                    pe.wait_ge(dn_sb, MT * (l + 1))
                    ada(l + 1, 1, 0, ADA_HALF)
                for t in range(TT):
                    n = l * TT + t
                    pe.wait_ge(y_sum, n + 1)
                    if t >= 2:
                        pe.wait_ge(x_new, 8 * (n - 1))
                    for k in range(KC):
                        last = nc.tensor.transpose(ps[:, 1024 * (t % 2) + k * P:1024 * (t % 2) + (k + 1) * P],
                                                   y2[:, t % 2, k * P:(k + 1) * P], ident[:])
                    last.then_inc(yt_ps, 1)

            pe.wait_ge(x_new, 8 * TT * DEPTH)
            for t in range(TT):
                if t >= 2:
                    pe.wait_ge(fin_sb, t - 1)
                for k in range(KC):
                    last = nc.tensor.transpose(ps[:, 1024 * (t % 2) + k * P:1024 * (t % 2) + (k + 1) * P],
                                               xT[:, k, t * P:(t + 1) * P], ident[:])
                last.then_inc(fin_ps, 1)


_INS = ["x_prompt", "x_sample", "cache_k", "cache_v", "state_fwd", "state_bwd", "c", "c_ctx", "w_ada", "b_ada",
        "norm1_w", "norm2_w", "w_in", "q_norm_w", "k_norm_w", "hg_lb", "hg_norm_w", "w_ft", "w_out",
        "w_gr", "b_gr", "w_er", "b_er", "w_gate", "w_up", "w_down"]
_OUTS = [(1, NP, D), (1, NS, D), (1, DEPTH, NP, 2, HD), (1, DEPTH, NP, 2, HD), (1, DEPTH, 4, HD, HD), (1, DEPTH, 4, HD, HD)]


def kernel(**inputs):
    import numpy as _np
    import concourse.bacc as _bacc
    from concourse import mybir as _mybir
    from concourse.bass_utils import run_bass_kernel_spmd as _run

    nc = _bacc.Bacc("TRN2", target_bir_lowering=False, num_devices=1)
    arrays, A, C = {}, {}, {}
    for name in _INS:
        a = _np.ascontiguousarray(inputs[name])
        arrays[f"in_{name}_dram"] = a
        A[name] = nc.dram_tensor(f"in_{name}_dram", a.shape, _mybir.dt.from_np(a.dtype), kind="ExternalInput").ap()
    for name, a in shape_constants().items():
        arrays[f"const_{name}_dram"] = a
        C[name] = nc.dram_tensor(f"const_{name}_dram", a.shape, _mybir.dt.from_np(a.dtype), kind="ExternalInput").ap()
    outs = [nc.dram_tensor(f"out_{i}_dram", s, _mybir.dt.float32, kind="ExternalOutput").ap() for i, s in enumerate(_OUTS)]
    build_program(nc, A, C, outs)
    r = _run(nc, [arrays], core_ids=[0])
    return tuple(r.results[0][f"out_{i}_dram"] for i in range(len(_OUTS)))
```

```python
from contextlib import ExitStack

import concourse.bass as bass
from concourse import mybir

ALU = mybir.AluOpType
ACT = mybir.ActivationFunctionType
AX_X = mybir.AxisListType.X
F32 = mybir.dt.float32
F32R = mybir.dt.float32r
I32 = mybir.dt.int32
U8 = mybir.dt.uint8

P = 128
D = 1024
KC = D // P
DEPTH = 2
NP, NS = 128, 512
TOK = NP + NS
TT = TOK // P
GROUPS = ((0, 0, NP), (1, NP, TOK))
HD = 64
CH = 64
NCH = TOK // CH
PROMPT_CH = NP // CH
HALVES = (32, 16, 8, 4, 2, 1)
NE, TOPK = 16, 2
NEG, EPG = 4, 4
DE = 256
MT = (TOPK * TOK + NE * (P - 1)) // P
SLOTS = MT * P
EPS = 1e-6
IN_W = 2304
BIG = 3.0e38

C_Q, C_K, C_HQ, C_HF, C_HG, C_FT = 0, 4, 5, 7, 11, 13
MIX = (0, 1, 2, 3, 11, 12, 13, 14)

RING = 5
ADA_HALF, IN_ITEMS, OUT_ITEMS = 12, 9, 4
IN_ORDER = (4, 5, 3, 7, 2, 0, 1, 8, 6)


def expert_items(l):
    s = []
    for i in range(MT + 1):
        s += [("gate", l, i), ("up", l, i)] if i < MT else []
        s += [("down", l, i - 1)] if i >= 1 else []
    return s


def weight_stream():
    s = []
    for l in range(DEPTH):
        if l == 0:
            s += [("ada", l, i) for i in range(2 * ADA_HALF)]
        s += [("in", l, i) for i in range(IN_ITEMS)]
        s += [("out", l, i) for i in range(OUT_ITEMS)]
        if l + 1 < DEPTH:
            s += [("ada", l + 1, i) for i in range(ADA_HALF)]
        s += expert_items(l)
        if l + 1 < DEPTH:
            s += [("ada", l + 1, ADA_HALF + i) for i in range(ADA_HALF)]
    return s


STREAM = weight_stream()
ITEM = {item: n for n, item in enumerate(STREAM)}

WB = 4
XB = 4
REST_BY = {("gate", 0): "dve", ("gate", 1): "pool", ("up", 0): "dve", ("up", 1): "dve", ("down", 0): "pool", ("down", 1): "dve"}
UNITS = [(k, l, j, h) for l in range(DEPTH) for k, _, j in expert_items(l) for h in range(2)]
UNIT = {u: n for n, u in enumerate(UNITS)}
REST_COUNT = {}
for _n, _u in enumerate(UNITS):
    REST_COUNT[_u] = 1 + sum(REST_BY[v[0], v[3]] == REST_BY[_u[0], _u[3]] for v in UNITS[:_n])

ADA_AT = (5, 7, 9, 10, 11, ADA_HALF)

PA_COND, PA_N1, PA_N2, PA_QN, PA_KN, PA_HN, PA_LB, PA_ROWS = 0, 16, 32, 48, 50, 52, 54, 62
PB0 = 64

NU = 8 * TT
N_PARAM_DMAS = 12

CONSTS = ("ident", "blockones", "ones", "rot", "tri", "dft64", "cosT", "sinT",
          "dft_s", "dft_p", "lvl", "restart", "tileno")


def shape_constants():
    import numpy as np
    c = {}
    c["ident"] = np.eye(P, dtype=np.float32)
    bo = np.zeros((P, P), np.float32)
    bo[:64, :64] = 1
    bo[64:, 64:] = 1
    c["blockones"] = bo
    c["ones"] = np.ones((P, P), np.float32)
    rot = np.zeros((P, P), np.float32)
    for m in range(P):
        if m % 32 < 16:
            rot[m + 16, m] = -1.0
        else:
            rot[m - 16, m] = 1.0
    c["rot"] = rot
    c["tri"] = np.triu(np.ones((P, P), np.float32), 1)
    k = np.arange(64)
    th = 2 * np.pi * ((k[:, None] * k[None, :]) % 64) / 64
    d64 = np.zeros((P, 2, P), np.float32)
    for b in range(2):
        d64[64 * b:64 * b + 64, 0, 64 * b:64 * b + 64] = np.cos(th)
        d64[64 * b:64 * b + 64, 1, 64 * b:64 * b + 64] = -np.sin(th)
    c["dft64"] = d64
    half = 32
    inv = (1.0 / (np.float32(10000.0) ** (np.arange(0, half, 2, dtype=np.float32) / np.float32(half)))).astype(np.float32)
    t = np.arange(NS)
    row, col = (t // 64).astype(np.float32), (t % 64).astype(np.float32)
    cosT, sinT = np.zeros((P, NS), np.float32), np.zeros((P, NS), np.float32)
    for p in range(P):
        d = p % 64
        ang = ((row if d < 32 else col) * inv[d % 16]).astype(np.float32)
        cosT[p], sinT[p] = np.cos(ang), np.sin(ang)
    c["cosT"], c["sinT"] = cosT, sinT

    def dft(n):
        i = np.arange(n)
        a = 2 * np.pi * ((i[:, None] * i[None, :]) % n) / n
        s = 1.0 / np.sqrt(n * 64.0)
        both = np.stack([np.cos(a) * s, np.sin(a) * s], 0)
        return both.reshape(2, n // P, P, n).transpose(2, 0, 1, 3).astype(np.float32).copy()
    c["dft_s"], c["dft_p"] = dft(NS), dft(NP)
    lvl = np.zeros((P, 2, len(HALVES), P), np.float32)
    s, q = np.arange(P)[:, None], np.arange(P)[None, :]
    for i, m in enumerate(HALVES):
        same = (s // (2 * m)) == (q // (2 * m))
        lvl[:, 0, i] = same & (s % (2 * m) < m) & (q % (2 * m) >= m)
        lvl[:, 1, i] = same & (s % (2 * m) >= m) & (q % (2 * m) < m)
    c["lvl"] = lvl
    c["restart"] = np.broadcast_to((np.arange(TOK) % CH != 0).astype(np.float32), (P, TOK)).copy()
    tn = np.zeros((P, 64), np.float32)
    tn[:, 0:MT] = np.arange(MT)
    tn[:, 32:36] = np.arange(4)
    tn[:, 40:40 + TT] = np.arange(TT)[None] * P + np.arange(P)[:, None]
    c["tileno"] = tn
    return c


def chunk_order(d):
    way = 1 if d == 0 else -1
    return list(range(PROMPT_CH))[::way] + list(range(PROMPT_CH, NCH))[::way]


def nth(l, n, i, ways=2):
    return l * ((n + ways - 1 - i % ways) // ways) + i // ways + 1


def all_of(eng, sems, l, n, each):
    for i in range(2):
        eng.wait_ge(sems[i], each * nth(l, n, n - 1 if (n - 1) % 2 == i else n - 2))


def _proj_unit(u):
    i, j = IN_ORDER[u // 2], u % 2

    def pair(ps):
        return ps[:, 1024 * (u % 2):1024 * (u % 2) + 1024]
    if (i, j) == (2, 1):
        return lambda pT, v, t, ps: (v[:, :, :], pair(ps)[:, 0:TOK].rearrange("p (t e) -> p t e", t=TT))
    if (i, j) == (6, 0):
        return lambda pT, v, t, ps: (t[:, 0:4, :], pair(ps).rearrange("p (t e) -> p t e", t=4))
    if (i, j) == (6, 1):
        return lambda pT, v, t, ps: (t[:, 4, :], pair(ps)[:, 0:256])
    c = 2 * i + j - (0 if i < 3 else 1 if i < 6 else 3)
    return lambda pT, v, t, ps: (pT[:, c, :], pair(ps)[:, 0:TOK])


PROJ_EVAC = [_proj_unit(u) for u in range(18)]
AFTER = {1: ("gate", 0), 2: ("gate", 1), 3: ("gate", 2), 4: ("gate", 3), 6: ("silu", 0), 7: ("silu", 1),
         8: ("silu", 2), 9: ("silu", 3), 10: ("qk", 0), 12: ("qk", 1), 13: ("qk", 2), 14: ("qk", 3), 15: ("qk", 4),
         16: ("qk", 5)}
QK_CHUNKS = (4, 0, 1, 2, 3)
GATE_CHUNKS = (5, 6, 11, 12)
PBUF = (4, 5, 8)


def build_program(nc, A, C, outs):
    y_prompt, y_sample, o_ck, o_cv, o_sf, o_sb = outs
    ctx = ExitStack()
    with ctx:
        def sb(name, shape, dt=F32):
            return ctx.enter_context(nc.sbuf_tensor(name, shape, dt))

        def sem(name):
            return ctx.enter_context(nc.semaphore(name))

        K = {n: sb("c_" + n, list(C[n].shape), U8 if n == "lvl" else F32) for n in CONSTS}
        ident, blockones, ones, rot, tri = (K[n] for n in ("ident", "blockones", "ones", "rot", "tri"))

        xT = sb("xT", [P, KC, TOK])
        hT_at = nc.sbuf_base
        hT = sb("hT", [P, KC, TOK])
        hT_flat = hT[:, :, :].rearrange("p k t -> p (k t)")
        xrow = hT_flat.rearrange("p (t d) -> p t d", t=TT)
        pT = sb("pT", [P, 15, TOK])
        pT_flat = pT[:, :, :].rearrange("p k t -> p (k t)")
        v_tok = sb("v_tok", [P, TT, P])
        i_tok = sb("i_tok", [P, TT, 256])
        ring = sb("ring", [P, RING, 2048])
        par = sb("par", [P, 160])
        cond = sb("cond", [P, 2, KC])
        csc = sb("csc", [P, 2, 16])
        lbt = sb("lbt", [P, 4, 4])
        lb = sb("lb", [P, DEPTH, 4])
        omlb = sb("omlb", [P, DEPTH, 4])
        eps_t = sb("eps_t", [P, 1])
        ckT = sb("ckT", [P, DEPTH, P])
        cv_tok = sb("cv_tok", [P, DEPTH, P])
        wr = sb("wr", [P, DEPTH, KC, NEG + NE])
        br = sb("br", [1, DEPTH, NEG + NE])
        wft = sb("wft", [P, DEPTH, 2, P])
        s_init = sb("s_init", [P, DEPTH, 2, 2, P])
        decayed_at = nc.sbuf_base
        decayed = sb("decayed", [P, 4, TOK])
        mrow = sb("mrow", [2, 2, 256])
        mods = sb("mods", [P, DEPTH, 6, KC, 2])
        amul = sb("amul", [P, DEPTH, 2, KC, 2])
        scr_at = nc.sbuf_base
        scr = sb("scr", [P, 12, TOK])
        scr_flat = scr[:, :, :].rearrange("p k t -> p (k t)")
        st = sb("st", [P, 3, 8])
        kout = scr[:, 11, 0:P]
        lgt = scr[0:NEG + NE, 5, :]
        rt = scr_flat[:, 6144:6844]
        slot_i = sb("slot_i", [P, TT, TOPK], I32)
        slot_tok = sb("slot_tok", [P, MT], I32)
        tile_e = sb("tile_e", [P, 32], I32)
        wgt = sb("wgt", [P, TT, TOPK])

        S = hT_flat[:, 0:9 * P].rearrange("p (n v) -> p n v", v=P)
        aT = hT_flat[:, 1280:2560].rearrange("p (n v) -> p n v", v=P)
        kz = hT_flat[:, 2560:2560 + 4 * TOK].rearrange("p (b h t) -> p b h t", b=2, h=2)
        lvl_f = pT_flat[:, 0:2 * len(HALVES) * P].rearrange("p (d i t) -> p d i t", d=2, t=P)
        rows = pT_flat[:, 2048:2304].rearrange("p (a b) -> p a b", a=2)
        ck_row = pT_flat[:, 2304:2304 + DEPTH * P].rearrange("p (l t) -> p l t", l=DEPTH)
        slot_row = i_tok[:, :, :].rearrange("p t e -> p (t e)").rearrange("p (i s) -> p i s", s=P)
        slot_tile = v_tok[:, :, :].rearrange("p t e -> p (t e)")[:, 0:TT * TOPK * MT].rearrange("p (i j) -> p i j", j=MT)
        xg = pT_flat[:, 0:XB * D].rearrange("p (b d) -> p b d", b=XB)
        sg = pT_flat[:, 4096:4608].rearrange("p (b f) -> p b f", b=2)
        hid = pT_flat[:, 4608:5120].rearrange("p (b f) -> p b f", b=2)
        yb = pT_flat[:, 5632:7680].rearrange("p (b d) -> p b d", b=2)
        hrow = scr_flat[:, 0:2048].rearrange("p (b d) -> p b d", b=2)
        y1 = scr_flat[:, 2048:4096].rearrange("p (b d) -> p b d", b=2)
        y2 = scr_flat[:, 4096:6144].rearrange("p (b d) -> p b d", b=2)

        ps = ctx.enter_context(nc.psum_tensor("ps", [P, 8 * 512], F32))

        x_split = nc.alloc_sbuf_tensor_at("x_split", [P, 2, 2, KC, P], F32R, offset=hT_at)
        hid_split = nc.alloc_sbuf_tensor_at("hid_split", [P, 2, 2, 2, P], F32R, offset=hT_at + 4 * 4096)
        w_split = [nc.alloc_sbuf_tensor_at(f"w_split{b}", [P, 2, 1024], F32R,
                                           offset=decayed_at if b == WB - 1 else scr_at + 8192 * b) for b in range(WB)]

        def bank(b, n=512, off=0):
            return ps[:, b * 512 + off:b * 512 + off + n]

        h_dram = nc.dram_tensor("h_rows", (TOK, D), F32).ap()
        y_dram = nc.dram_tensor("y_rows", (SLOTS, D), F32).ap()

        consts_in = sem("consts_in"); params_in = sem("params_in"); x_in = sem("x_in")
        late_in = sem("late_in")
        slot_in = [sem(f"slot_in{i}") for i in range(RING)]
        ada_ps = sem("ada_ps"); ada_sb = sem("ada_sb"); ada_tr = sem("ada_tr")
        zero_done = sem("zero_done")
        xt_ps = sem("xt_ps"); xt_act = sem("xt_act"); xt_dve = sem("xt_dve")
        par_ps = sem("par_ps"); par_sb = sem("par_sb")
        cond_e = sem("cond_e"); cond_ok = sem("cond_ok"); lb_d = sem("lb_d"); lb_e = sem("lb_e")
        mods_ok = sem("mods_ok")
        nsq = sem("nsq"); nsum = sem("nsum"); nrs = sem("nrs"); nscaled = sem("nscaled"); h_ok = sem("h_ok")
        proj_ps = sem("proj_ps"); proj_act = sem("proj_act"); proj_dve = sem("proj_dve")
        qsq = sem("qsq"); qsum = sem("qsum"); qrs = sem("qrs"); qnorm = sem("qnorm")
        qrot = sem("qrot"); qcos = sem("qcos"); qk_ok = sem("qk_ok")
        ck_ps = sem("ck_ps"); ck_sb = sem("ck_sb"); cache_out = sem("cache_out"); ko_sb = sem("ko_sb"); rt_e = sem("rt_e")
        sc_ps = sem("sc_ps"); sc_max = sem("sc_max"); sc_exp = sem("sc_exp"); sc_norm = sem("sc_norm")
        pt_ps = sem("pt_ps"); pt_sb = sem("pt_sb"); av_ps = sem("av_ps"); av_sb = sem("av_sb")
        sl_e = sem("sl_e"); sl_ok = sem("sl_ok")
        gt_in = sem("gt_in"); gt_e = sem("gt_e"); gt_den = sem("gt_den"); gt_ln = sem("gt_ln"); gt_ok = sem("gt_ok")
        dk_d = sem("dk_d"); dk_e = sem("dk_e"); dk_ok = sem("dk_ok")
        lv_d = sem("lv_d"); lv_e = sem("lv_e"); lv_ok = sem("lv_ok")
        g_ps = sem("g_ps"); kz_zero = sem("kz_zero"); dg_in = sem("dg_in"); g_used = sem("g_used"); s_ok = sem("s_ok")
        inter_ps = sem("inter_ps"); intra_ps = sem("intra_ps")
        on_sq = sem("on_sq"); on_sum = sem("on_sum"); on_rs = sem("on_rs"); on_ok = sem("on_ok")
        state_out = sem("state_out")
        f_ab = sem("f_ab"); f_abs = sem("f_abs"); f_z = sem("f_z"); f_zs = sem("f_zs"); f_o = sem("f_o"); f_os = sem("f_os")
        op_ps = sem("op_ps"); x_mid = sem("x_mid")
        lgt_ps = sem("lgt_ps"); lgt_sb = sem("lgt_sb"); lg_ps = sem("lg_ps"); lg_sb = sem("lg_sb"); rt_m = sem("rt_m"); rk_ps = sem("rk_ps"); rt_ok = sem("rt_ok")
        hr_ps = sem("hr_ps"); hr_sb = sem("hr_sb"); hr_out = [sem(f"hr_out{i}") for i in range(2)]
        tb_in = sem("tb_in"); tb_ps = sem("tb_ps"); tb_ok = sem("tb_ok")
        xg_in = [sem(f"xg_in{i}") for i in range(XB)]; xg_ps = sem("xg_ps"); xg_sb = sem("xg_sb")
        w_hi = sem("w_hi"); w_lo = {"dve": sem("w_lo_dve"), "pool": sem("w_lo_pool")}; w_used = sem("w_used")
        xg_lo = sem("xg_lo"); gu_s = sem("gu_s"); hid_ok = sem("hid_ok"); hid_ps = sem("hid_ps"); hid_sb = sem("hid_sb")
        dn_sb = sem("dn_sb"); y_out = [sem(f"y_out{i}") for i in range(2)]
        y_in = [sem(f"y_in{i}") for i in range(2)]; y_w = sem("y_w"); y_sum = sem("y_sum"); yt_ps = sem("yt_ps"); x_new = sem("x_new")
        fin_ps = sem("fin_ps"); fin_sb = sem("fin_sb"); fin_out = sem("fin_out")
        dve_step = sem("dve_step"); act_step = sem("act_step"); pool_step = sem("pool_step")

        N_CONST = len(CONSTS) - 1

        def item_dmas(n):
            kind, l, i = STREAM[n]
            return 4 if kind == "in" and IN_ORDER[i] < 2 else 3 if kind == "out" else 1

        landed, slot_total = [], [0] * RING
        for n in range(len(STREAM)):
            slot_total[n % RING] += 16 * item_dmas(n)
            landed.append(slot_total[n % RING])

        def free_slot(eng, n):
            kind, l, i = STREAM[n]
            if kind == "ada":
                eng.wait_ge(ada_ps, l * 2 * ADA_HALF + i + 1)
            elif kind == "in":
                eng.wait_ge(proj_ps, 2 * (l * IN_ITEMS + i + 1))
            elif kind == "out":
                eng.wait_ge(op_ps, 2 * (l * OUT_ITEMS + i + 1))
            else:
                for h in range(2):
                    eng.wait_ge(w_lo[REST_BY[kind, h]], REST_COUNT[kind, l, i, h])

        def multiplied(eng, kind, l, i):
            eng.wait_ge(w_used, UNIT[kind, l, i, 1] + 1)

        def unit_parts(kind, l, i, h):
            return slot(ITEM[kind, l, i])[:, 1024 * h:1024 * h + 1024], w_split[UNIT[kind, l, i, h] % WB]

        def rest(eng, engine, name, kind, l, i, h):
            src, dst = unit_parts(kind, l, i, h)
            eng.wait_ge(w_hi, UNIT[kind, l, i, h] + 1)
            engine.tensor_tensor(dst[:, 1, :], src, dst[:, 0, :], ALU.subtract).then_inc(w_lo[name], 1)

        def slot(n):
            return ring[:, n % RING, :]

        def x_whole(eng, l):
            if l == 0:
                eng.wait_ge(xt_act, 3)
                eng.wait_ge(xt_dve, 2)
            else:
                eng.wait_ge(x_new, KC * TT * l)

        block = ctx.enter_context(nc.Block())

        @block.sync
        def _(sp):
            sp.dma_start(K["ident"][:], C["ident"]).then_inc(x_in, 16)
            sp.dma_start(xrow[:, 0, :], A["x_prompt"][0]).then_inc(x_in, 16)
            sp.dma_start(xrow[:, 1:TT, :], A["x_sample"][0].rearrange("(t p) d -> p t d", p=P)).then_inc(x_in, 16)
            for n in CONSTS[1:]:
                sp.dma_start(lvl_f if n == "lvl" else K[n][:], C[n]).then_inc(consts_in, 16)

            def next_item(n):
                if n >= RING:
                    free_slot(sp, n - RING)
                return slot(n), slot_in[n % RING]

            experts = [None, None]
            for n, (kind, l, i) in enumerate(STREAM):
                dst, s = next_item(n)
                cols = dst.rearrange("p (k n) -> p k n", k=KC)
                if kind == "ada":
                    sp.dma_start(cols, A["w_ada"][l].rearrange("(k p) n -> p k n", p=P)[:, :, 256 * i:256 * i + 256]).then_inc(s, 16)
                elif kind == "in":
                    w_in = A["w_in"][l].rearrange("(k p) n -> p k n", p=P)
                    c0 = IN_ORDER[i]
                    if c0 < 2:
                        view = dst.rearrange("p (k c b j) -> p k c b j", k=KC, c=2, b=2)
                        for b in range(2):
                            for c in range(2):
                                at = 256 * b + 128 * c0 + 64 * c
                                sp.dma_start(view[:, :, c, b, :], w_in[:, :, at:at + 64]).then_inc(s, 16)
                    else:
                        sp.dma_start(cols, w_in[:, :, 256 * c0:256 * c0 + 256]).then_inc(s, 16)
                elif kind == "out":
                    w_out = A["w_out"][l]
                    for b in range(2):
                        sp.dma_start(cols[64 * b:64 * b + 64, 0:4, :],
                                     w_out[256 * b:256 * b + 256, 256 * i:256 * i + 256]
                                     .rearrange("(c p) n -> p c n", p=64)).then_inc(s, 16)
                    sp.dma_start(cols[:, 4:8, :], w_out[512:1024, 256 * i:256 * i + 256]
                                 .rearrange("(c p) n -> p c n", p=P)).then_inc(s, 16)
                else:
                    if kind == "gate":
                        if i == 0:
                            sp.wait_ge(rt_ok, l + 1)
                        experts[i % 2] = sp.value_load(tile_e[0:1, i:i + 1], min_val=0, max_val=NE - 1)
                    name = {"gate": "w_gate", "up": "w_up", "down": "w_down"}[kind]
                    sp.dma_start(dst.rearrange("p (k n) -> p k n", k=2 if kind == "down" else KC),
                                 A[name][l, bass.ds(experts[i % 2], 1)].rearrange("e (k p) n -> p (e k) n", p=P)).then_inc(s, 16)
            sp.wait_ge(cache_out, 16 * 2 * DEPTH)
            sp.wait_ge(state_out, 16 * 8 * DEPTH)
            all_of(sp, hr_out, DEPTH - 1, TT, 16)
            all_of(sp, y_out, DEPTH - 1, MT, 16)
            sp.wait_ge(fin_out, 16 * TT)

        @block.gpsimd
        def _(pool):
            steps = [0]

            def seq(ins):
                steps[0] += 1
                ins.then_inc(pool_step, 1)
                pool.wait_ge(pool_step, steps[0])

            nc.gpsimd.memset(wft[:], 0.0).then_inc(zero_done, 1)
            nc.gpsimd.memset(s_init[:], 0.0).then_inc(zero_done, 1)
            nc.gpsimd.memset(eps_t[:], EPS).then_inc(zero_done, 1)
            pool.wait_ge(zero_done, 3)
            for l in range(DEPTH):
                for g in range(4):
                    h = 64 * (g % 2)
                    pool.dma_start(wft[h:h + 64, l, g // 2, h:h + 64], A["w_ft"][l, g]).then_inc(late_in, 16)
                    for d, name in enumerate(("state_fwd", "state_bwd")):
                        pool.dma_start(s_init[h:h + 64, l, d, g // 2, h:h + 64], A[name][0, l, g]).then_inc(late_in, 16)
                pool.dma_start(wr[:, l, :, 0:NEG], A["w_gr"][l].rearrange("(k p) g -> p k g", p=P)).then_inc(late_in, 16)
                pool.dma_start(wr[:, l, :, NEG:], A["w_er"][l].rearrange("(k p) g -> p k g", p=P)).then_inc(late_in, 16)
                pool.dma_start(br[0:1, l, 0:NEG], A["b_gr"][l:l + 1]).then_inc(late_in, 16)
                pool.dma_start(br[0:1, l, NEG:], A["b_er"][l:l + 1]).then_inc(late_in, 16)
            pool.wait_ge(consts_in, 16 * N_CONST)

            for l in range(DEPTH):
                for i, c in enumerate(QK_CHUNKS):
                    n = l * 5 + i
                    pool.wait_ge(qnorm, n + 1)
                    if n >= 2:
                        pool.wait_ge(qk_ok, n - 1)
                    nc.gpsimd.tensor_tensor(scr[:, 2 + i % 2, 0:NS], pT[:, c, NP:], K["cosT"][:], ALU.mult).then_inc(qcos, 1)
                pool.wait_ge(proj_ps, 18 * (l + 1))
                nc.gpsimd.memset(hT_flat[:, 2560:], 0.0).then_inc(kz_zero, 1)
                for p in range(2):
                    for d in range(2):
                        u = (l * 2 + p) * 2 + d
                        if p == 0 and d == 0:
                            pool.wait_ge(gt_ok, 4 * l + 4)
                            pool.wait_ge(qk_ok, 5 * (l + 1))
                        b = pT[:, C_HF + 2 * d + p, :]
                        for i, m in enumerate(HALVES):
                            if i == 2:
                                if u % 4 == 0:
                                    pool.wait_ge(pt_ps, NU * (l + 1))
                                    pool.wait_ge(sl_ok, 4 * (l + 1))
                                if u >= 1:
                                    pool.wait_ge(g_ps, 9 * (u - 1) + 3)
                                nc.gpsimd.tensor_tensor(scr[:, 4, :], pT[:, C_HQ + p, :], decayed[:, 2 * d + p, :],
                                                        ALU.mult).then_inc(dg_in, 1)
                            n = u * 6 + i
                            if n >= 2:
                                pool.wait_ge(lv_ok, 3 * (n - 1))
                            bv = b.rearrange("p (n m) -> p n m", m=2 * m)
                            dv = scr[:, 2 + i % 2, :].rearrange("p (n m) -> p n m", m=2 * m)
                            nb = TOK // (2 * m)
                            if d == 0:
                                ref = bv[:, :, m - 1:m].to_broadcast([P, nb, m])
                                q, k = slice(m, 2 * m), slice(0, m)
                            else:
                                ref = bv[:, :, m:m + 1].to_broadcast([P, nb, m])
                                q, k = slice(0, m), slice(m, 2 * m)
                            nc.gpsimd.tensor_tensor(dv[:, :, q], bv[:, :, q], ref, ALU.subtract).then_inc(lv_d, 1)
                            nc.gpsimd.tensor_tensor(dv[:, :, k], ref, bv[:, :, k], ALU.subtract).then_inc(lv_d, 1)
                pool.wait_ge(tb_ok, l + 1)
                all_of(pool, hr_out, l, TT, 16)
                def gather(j):
                    if j >= XB:
                        pool.wait_ge(xg_ps, l * MT + j - XB + 1)
                    pool.indirect_dma_start(xg[:, j % XB, :], None, h_dram,
                                            bass.IndirectOffsetOnAxis(ap=slot_tok[:, j:j + 1], axis=0)).then_inc(xg_in[j % XB], 16)

                pool.wait_ge(x_mid, 2 * KC * (l + 1))
                gather(0)
                gather(1)
                for j in range(MT):
                    if j + 2 < MT:
                        gather(j + 2)
                    if j >= 1:
                        if j >= 3:
                            rest(pool, nc.gpsimd, "pool", "down", l, j - 3, 0)
                        rest(pool, nc.gpsimd, "pool", "gate", l, j - 1, 1)
                for j in range(MT, MT + 3):
                    rest(pool, nc.gpsimd, "pool", "down", l, j - 3, 0)
                    if j == MT:
                        rest(pool, nc.gpsimd, "pool", "gate", l, j - 1, 1)
                all_of(pool, y_out, l, MT, 16)
                for t in range(TT):
                    n = l * TT + t
                    if n >= 2:
                        pool.wait_ge(y_sum, n - 1)
                    for c, dst in enumerate((y1, y2)):
                        if t >= 2 and c == 1:
                            pool.wait_ge(yt_ps, n - 1)
                        pool.indirect_dma_start(dst[:, t % 2, :], None, y_dram,
                                                bass.IndirectOffsetOnAxis(ap=slot_i[:, t, c:c + 1], axis=0)).then_inc(y_in[t % 2], 16)

        @block.scalar
        def _(act):
            steps = [0]

            def seq(ins):
                steps[0] += 1
                ins.then_inc(act_step, 1)
                act.wait_ge(act_step, steps[0])

            def A_(out, in_, f, **kw):
                return nc.scalar.activation(out, in_, f, **kw)

            r0 = rows[:, 0, :]
            n_par = 0
            for src, at, cnt in (("c_ctx", PA_COND, 8), ("c", PA_COND + 8, 8)):
                v = A[src] if src == "c_ctx" else A[src][0]
                act.dma_start(r0[at:at + cnt, :], v.rearrange("(k p) -> k p", p=P)).then_inc(params_in, 16)
                n_par += 1
            for src, at in (("norm1_w", PA_N1), ("norm2_w", PA_N2)):
                act.dma_start(r0[at:at + 16, :], A[src].rearrange("l (k p) -> (l k) p", p=P)).then_inc(params_in, 16)
                n_par += 1
            for src, at in (("q_norm_w", PA_QN), ("k_norm_w", PA_KN), ("hg_norm_w", PA_HN)):
                for b in range(2):
                    act.dma_start(r0[at:at + 2, 64 * b:64 * b + 64], A[src]).then_inc(params_in, 16)
                    n_par += 1
            act.dma_start(r0[PA_LB:PA_LB + 8, :], A["hg_lb"].rearrange("l d (k p) -> (l d k) p", p=P)).then_inc(params_in, 16)
            act.dma_start(rows[0:96, 1, :], A["b_ada"].rearrange("l (k p) -> (l k) p", p=P)).then_inc(params_in, 16)
            n_par += 2
            assert n_par == N_PARAM_DMAS
            for l in range(DEPTH):
                act.dma_start(ck_row[:, l, :], A["cache_k"][0, l].rearrange("t h d -> t (h d)")).then_inc(params_in, 16)
                act.dma_start(cv_tok[:, l, :], A["cache_v"][0, l].rearrange("t h d -> t (h d)")).then_inc(params_in, 16)

            act.wait_ge(par_sb, 1)
            A_(csc[:, 0, :], par[:, PA_COND:PA_COND + 16], ACT.Exp, scale=-1.0).then_inc(cond_e, 1)
            act.wait_ge(lb_d, 1)
            A_(lbt[:, 1, :], lbt[:, 0, :], ACT.Exp).then_inc(lb_e, 1)
            A_(lbt[:, 3, :], lbt[:, 2, :], ACT.Exp).then_inc(lb_e, 1)
            for t in range(TT):
                if t % 2 == 0:
                    act.wait_ge(xt_ps, t + 1)
                    A_(xT[:, :, t * P:(t + 1) * P], ps[:, 0:1024].rearrange("p (k t) -> p k t", k=KC), ACT.Copy).then_inc(xt_act, 1)

            def norm(l, which):
                n0 = (l * 2 + which) * KC
                for k in range(KC):
                    if n0 + k >= 2:
                        act.wait_ge(nsum, n0 + k - 1)
                    if which == 0:
                        x_whole(act, l)
                    else:
                        act.wait_ge(x_mid, l * 2 * KC + 2 * (k + 1))
                    A_(scr[:, k % 2, :], xT[:, k, :], ACT.Square).then_inc(nsq, 1)
                act.wait_ge(nsum, n0 + KC)
                rs = scr[:, 2, :]
                seq(A_(rs[:, 0:NS], bank(5), ACT.Ln, scale=1.0 / D, bias=eps_t[:, 0:1]))
                seq(A_(rs[:, NS:], bank(6, NP), ACT.Ln, scale=1.0 / D, bias=eps_t[:, 0:1]))
                A_(rs, rs, ACT.Exp, scale=-0.5).then_inc(nrs, 1)
                for k in range(KC):
                    act.wait_ge(nscaled, 2 * (n0 + k + 1))
                    for g, a, b in GROUPS:
                        A_(hT[:, k, a:b], hT[:, k, a:b], ACT.Identity,
                           bias=mods[:, l, 3 * which, k, g:g + 1]).then_inc(h_ok, 1)

            def ada(l, half, first=0, end=ADA_HALF):
                for i in range(first, end):
                    n = (2 * l + half) * ADA_HALF + i
                    act.wait_ge(ada_ps, n + 1)
                    if n >= 2:
                        act.wait_ge(ada_tr, n - 1)
                    A_(mrow[:, i % 2, :], bank(4 + i % 2, 256)[0:2, :], ACT.Copy).then_inc(ada_sb, 1)

            def evacuated(l, u):
                act.wait_ge(proj_act if u % 2 == 0 else proj_dve, 9 * l + u // 2 + 1)

            def gate(l, i):
                n = 4 * l + i
                act.wait_ge(gt_in, 2 * (n + 1))
                for j in range(2):
                    A_(scr[:, 2 + j, :], scr[:, 4 + j, :], ACT.Exp).then_inc(gt_e, 1)
                act.wait_ge(gt_den, n + 1)
                A_(scr[:, 6, :], scr[:, 7, :], ACT.Ln).then_inc(gt_ln, 1)
                if l > 0:
                    A_(scr[:, 8, :], scr[:, 9, :], ACT.Ln).then_inc(gt_ln, 1)

            def silu(l, i):
                n = 4 * l + i
                if n >= 2:
                    act.wait_ge(sl_ok, n - 1)
                evacuated(l, 4 + i)
                A_(scr[:, i % 2, :], pT[:, GATE_CHUNKS[i], :], ACT.Exp, scale=-1.0).then_inc(sl_e, 1)

            def qk(l, i):
                if i == 5:
                    return
                n, c = l * 5 + i, QK_CHUNKS[i]
                r = scr[:, i % 2, :]
                if n >= 2:
                    act.wait_ge(qnorm, n - 1)
                evacuated(l, 8 if c == 4 else 10 + c)
                act.wait_ge(sl_ok, 4 * (l + 1))
                A_(r, pT[:, c, :], ACT.Square).then_inc(qsq, 1)
                act.wait_ge(qsum, n + 1)
                seq(A_(r, ps[:, 3072:3072 + TOK], ACT.Ln, scale=1.0 / HD, bias=eps_t[:, 0:1]))
                A_(r, r, ACT.Exp, scale=-0.5).then_inc(qrs, 1)

            act.wait_ge(zero_done, 3)
            ada(0, 0)
            for l in range(DEPTH):
                act.wait_ge(mods_ok, 2 * l + 1)
                norm(l, 0)
                if l == 0:
                    ada(0, 1)

                for u in range(18):
                    if u % 2 == 0:
                        act.wait_ge(proj_ps, 18 * l + u + 1)
                        dst, src = PROJ_EVAC[u](pT, v_tok, i_tok, ps)
                        A_(dst, src, ACT.Copy).then_inc(proj_act, 1)
                    if u in AFTER:
                        kind, i = AFTER[u]
                        {"gate": gate, "silu": silu, "qk": qk}[kind](l, i)
                act.wait_ge(proj_act, 9 * (l + 1))
                act.wait_ge(proj_dve, 9 * (l + 1))
                act.dma_start(o_cv[0, l].rearrange("t h d -> t (h d)"), v_tok[:, 0, :]).then_inc(cache_out, 16)
                act.wait_ge(ck_ps, l + 1)
                if l > 0:
                    act.wait_ge(cache_out, 16 * 2 * l)
                A_(kout, bank(5, P), ACT.Copy).then_inc(ko_sb, 1)
                act.wait_ge(ko_sb, l + 1)
                act.dma_start(o_ck[0, l].rearrange("t h d -> t (h d)"), kout).then_inc(cache_out, 16)

                for i in range(NU + 2):
                    if i < NU:
                        n = l * NU + i
                        w = P if i % TT == 0 else TOK
                        act.wait_ge(sc_max, n + 1)
                        if i >= 3:
                            act.wait_ge(pt_ps, n - 2)
                        A_(scr[:, PBUF[i % 3], 0:w], ps[:, 1024 * (i % 2):1024 * (i % 2) + w], ACT.Exp,
                           scale=HD ** -0.5, bias=st[:, i % 3, 1:2], accum_out=st[:, i % 3, 2:3]).then_inc(sc_exp, 1)
                    if i >= 2:
                        n = l * NU + i - 2
                        w = P if (i - 2) % TT == 0 else TOK
                        act.wait_ge(pt_ps, n + 1)
                        if i >= 4:
                            act.wait_ge(av_ps, n - 1)
                        A_(scr[:, 6 + i % 2, 0:w], ps[:, 2048:2048 + w], ACT.Copy).then_inc(pt_sb, 1)

                for p in range(2):
                    for d in range(2):
                        u = (l * 2 + p) * 2 + d
                        act.wait_ge(gt_ok, 4 * l + 4)
                        if u >= 1:
                            act.wait_ge(dk_ok, 2 * u)
                            act.wait_ge(s_ok, 8 * u)
                        A_(scr[:, 8, :], pT[:, C_HF + 2 * d + p, :], ACT.Exp).then_inc(dk_e, 1)
                        act.wait_ge(dk_d, u + 1)
                        A_(scr[:, 10, :], scr[:, 10, :], ACT.Exp).then_inc(dk_e, 1)
                        for i in range(6):
                            n = u * 6 + i
                            act.wait_ge(lv_d, 2 * (n + 1))
                            A_(scr[:, 2 + i % 2, :], scr[:, 2 + i % 2, :], ACT.Exp).then_inc(lv_e, 1)
                        act.wait_ge(s_ok, 8 * (u + 1))
                        for h in range(2):
                            hs = slice(64 * h, 64 * h + 64)
                            act.dma_start((o_sf, o_sb)[d][0, l, 2 * p + h], S[hs, 1, hs]).then_inc(state_out, 16)
                    n = 2 * l + p
                    act.wait_ge(intra_ps, 2 * n + 2)
                    r = scr[:, 0, :]
                    A_(r, ps[:, 3072:3072 + TOK], ACT.Square).then_inc(on_sq, 1)
                    act.wait_ge(on_sum, n + 1)
                    seq(A_(r, ps[:, 0:TOK], ACT.Ln, scale=1.0 / HD, bias=eps_t[:, 0:1]))
                    A_(r, r, ACT.Exp, scale=-0.5).then_inc(on_rs, 1)
                for p in range(2):
                    n = 2 * l + p
                    act.wait_ge(f_o, n + 1)
                    A_(pT[:, C_FT + p, NP:], bank(6), ACT.Copy).then_inc(f_os, 1)
                    A_(pT[:, C_FT + p, 0:NP], bank(7, NP), ACT.Copy).then_inc(f_os, 1)

                norm(l, 1)
                act.wait_ge(lgt_ps, l + 1)
                A_(lgt, ps[0:NEG + NE, 0:TOK], ACT.Copy).then_inc(lgt_sb, 1)
                for t in range(TT):
                    n = l * TT + t
                    act.wait_ge(hr_ps, n + 1)
                    if nth(l, TT, t) > 1:
                        act.wait_ge(hr_out[t % 2], 16 * (nth(l, TT, t) - 1))
                    A_(hrow[:, t % 2, :], ps[:, 1024 * (t % 2):1024 * (t % 2) + D], ACT.Copy).then_inc(hr_sb, 1)
                    act.wait_ge(hr_sb, n + 1)
                    act.dma_start(h_dram[t * P:(t + 1) * P, :], hrow[:, t % 2, :]).then_inc(hr_out[t % 2], 16)

                if l + 1 < DEPTH:
                    ada(l + 1, 0, 0, 5)
                act.wait_ge(rt_m, 2 * l + 1)
                A_(rt[:, 130:150], rt[:, 130:150], ACT.Exp).then_inc(rt_e, 1)
                A_(rt[:, 360:365], rt[:, 360:365], ACT.Exp).then_inc(rt_e, 1)
                if l + 1 < DEPTH:
                    ada(l + 1, 0, 5)

                def rounded(kind, i, h):
                    u = UNIT[kind, l, i, h]
                    src, dst = unit_parts(kind, l, i, h)
                    if h == 0:
                        act.wait_ge(slot_in[ITEM[kind, l, i] % RING], landed[ITEM[kind, l, i]])
                    if u >= WB:
                        act.wait_ge(w_used, u - WB + 1)
                    A_(dst[:, 0, :], src, ACT.Copy).then_inc(w_hi, 1)

                all_of(act, hr_out, l, TT, 16)
                rounded("gate", 0, 0)
                rounded("gate", 0, 1)
                for i in range(MT + 2):
                    if 1 <= i <= MT:
                        rounded("up", i - 1, 0)
                    if i < MT:
                        n = l * MT + i
                        act.wait_ge(xg_ps, n + 1)
                        if i >= 2:
                            multiplied(act, "up", l, i - 2)
                        A_(x_split[:, i % 2, 0], ps[:, 0:1024].rearrange("p (k t) -> p k t", k=KC), ACT.Copy).then_inc(xg_sb, 1)
                    if 1 <= i <= MT:
                        rounded("up", i - 1, 1)
                    if i >= 2:
                        rounded("down", i - 2, 0)
                        rounded("down", i - 2, 1)
                    if 1 <= i < MT:
                        rounded("gate", i, 0)
                        rounded("gate", i, 1)
                    if 1 <= i <= MT:
                        n = l * MT + i - 1
                        j = (i - 1) % 2
                        multiplied(act, "up", l, i - 1)
                        if n >= 2:
                            act.wait_ge(hid_ok, n - 1)
                        A_(sg[:, j, :], bank(2 + j, DE), ACT.Silu).then_inc(gu_s, 1)
                    if i >= 3:
                        n = l * MT + i - 3
                        j = (i - 3) % 2
                        act.wait_ge(dn_sb, n + 1)
                        act.dma_start(y_dram[(i - 3) * P:(i - 2) * P, :], yb[:, j, :]).then_inc(y_out[j], 16)
                j = (MT - 1) % 2
                act.wait_ge(dn_sb, MT * (l + 1))
                act.dma_start(y_dram[(MT - 1) * P:MT * P, :], yb[:, j, :]).then_inc(y_out[j], 16)
                def weigh(t):
                    act.wait_ge(y_in[t % 2], 32 * nth(l, TT, t))
                    A_(y1[:, t % 2, :], y1[:, t % 2, :], ACT.Copy, scale=wgt[:, t, 0:1]).then_inc(y_w, 1)

                def output(t):
                    act.wait_ge(fin_ps, t + 1)
                    A_(xrow[:, t, :], ps[:, 2048 + 1024 * (t % 2):2048 + 1024 * (t % 2) + D], ACT.Copy).then_inc(fin_sb, 1)
                    act.wait_ge(fin_sb, t + 1)
                    dst = y_prompt[0] if t == 0 else y_sample[0, (t - 1) * P:t * P, :]
                    act.dma_start(dst, xrow[:, t, :]).then_inc(fin_out, 16)

                if l + 1 < DEPTH:
                    ada(l + 1, 1, 0, ADA_AT[0])
                    weigh(0)
                    weigh(1)
                    for t in range(TT):
                        ada(l + 1, 1, ADA_AT[t], ADA_AT[t + 1])
                        if t + 2 < TT:
                            weigh(t + 2)
                else:
                    weigh(0)
                    for t in range(TT):
                        if t + 1 < TT:
                            weigh(t + 1)
                        output(t)


        @block.vector
        def _(dve):
            steps = [0]
            V = nc.vector

            def seq(ins):
                steps[0] += 1
                ins.then_inc(dve_step, 1)
                dve.wait_ge(dve_step, steps[0])

            dve.wait_ge(par_ps, 3)
            V.tensor_copy(ckT[:], bank(5, 2 * P).rearrange("p (l t) -> p l t", l=2)).then_inc(ck_sb, 1)
            seq(V.tensor_copy(par[:, PB0:PB0 + 96], bank(4, 96, PB0)))
            V.tensor_copy(par[:, 0:PA_ROWS], bank(4, PA_ROWS)).then_inc(par_sb, 1)
            dve.wait_ge(cond_e, 1)
            dve.wait_ge(par_sb, 1)
            seq(V.tensor_scalar(csc[:, 0, :], csc[:, 0, :], 1.0, None, ALU.add))
            seq(V.reciprocal(csc[:, 1, :], csc[:, 0, :]))
            V.tensor_tensor(cond[:].rearrange("p g k -> p (g k)"), par[:, PA_COND:PA_COND + 16], csc[:, 1, :],
                            ALU.mult).then_inc(cond_ok, 1)
            l0, l1 = par[:, PA_LB:PA_LB + 4], par[:, PA_LB + 4:PA_LB + 8]
            seq(V.tensor_tensor(lb[:, 0, :], l0, l1, ALU.max))
            seq(V.tensor_tensor(lbt[:, 0, :], l0, lb[:, 0, :], ALU.subtract))
            V.tensor_tensor(lbt[:, 2, :], l1, lb[:, 0, :], ALU.subtract).then_inc(lb_d, 1)
            dve.wait_ge(lb_e, 2)
            seq(V.tensor_tensor(lbt[:, 0, :], lbt[:, 1, :], lbt[:, 3, :], ALU.add))
            seq(V.reciprocal(lbt[:, 2, :], lbt[:, 0, :]))
            seq(V.tensor_tensor(lb[:, 1, :], lbt[:, 3, :], lbt[:, 2, :], ALU.mult))
            seq(V.memset(lb[:, 0, :], 0.0))
            seq(V.tensor_scalar(omlb[:], lb[:], -1.0, 1.0, ALU.mult, ALU.add))
            for t in range(TT):
                if t % 2 == 1:
                    dve.wait_ge(xt_ps, t + 1)
                    V.tensor_copy(xT[:, :, t * P:(t + 1) * P], ps[:, 1024:2048].rearrange("p (k t) -> p k t", k=KC)).then_inc(xt_dve, 1)
            dve.wait_ge(consts_in, 16 * N_CONST)
            seq(V.tensor_copy(K["lvl"][:], lvl_f))

            def norm(l, which):
                n0 = (l * 2 + which) * KC
                dve.wait_ge(nrs, 2 * l + which + 1)
                rs = scr[:, 2, :]
                for k in range(KC):
                    for g, a, b in GROUPS:
                        r = rs[:, NS:] if g == 0 else rs[:, 0:NS]
                        V.scalar_tensor_tensor(hT[:, k, a:b], xT[:, k, a:b], amul[:, l, which, k, g:g + 1], r,
                                               ALU.mult, ALU.mult).then_inc(nscaled, 1)

            def modulations(l, half):
                dve.wait_ge(ada_tr, (2 * l + half + 1) * ADA_HALF)
                at = PB0 + 48 * l + 24 * half
                bias = par[:, at:at + 24].unsqueeze(2).to_broadcast([P, 24, 2])
                seq(V.tensor_tensor(mods[:, l, 3 * half:3 * half + 3].rearrange("p s k g -> p (s k) g"),
                                    bank(7, 48).rearrange("p (n g) -> p n g", g=2), bias, ALU.add))
                at = (PA_N1, PA_N2)[half] + 8 * l
                w = par[:, at:at + 8].unsqueeze(2).to_broadcast([P, KC, 2])
                V.scalar_tensor_tensor(amul[:, l, half], mods[:, l, 3 * half + 1], 1.0, w, ALU.add, ALU.mult).then_inc(mods_ok, 1)
                dve.wait_ge(mods_ok, 2 * l + half + 1)

            def evacuated(l, u):
                dve.wait_ge(proj_act if u % 2 == 0 else proj_dve, 9 * l + u // 2 + 1)

            def silu(l, i):
                c, n, e = GATE_CHUNKS[i], 4 * l + i, scr[:, i % 2, :]
                dve.wait_ge(sl_e, n + 1)
                seq(V.tensor_scalar(e, e, 1.0, None, ALU.add))
                seq(V.reciprocal(e, e))
                V.tensor_tensor(pT[:, c, :], pT[:, c, :], e, ALU.mult).then_inc(sl_ok, 1)

            def gate(l, i):
                d, n = i // 2, 4 * l + i
                z = pT[:, C_HF + i, :]
                ep, en, tp, tn = (scr[:, j, :] for j in (2, 3, 4, 5))
                lnden, den, lnnum, num, rden = (scr[:, j, :] for j in (6, 7, 8, 9, 10))
                evacuated(l, i)
                V.tensor_scalar(tp, z, 0.0, None, ALU.min).then_inc(gt_in, 1)
                V.tensor_scalar(tn, z, -1.0, 0.0, ALU.mult, ALU.min).then_inc(gt_in, 1)
                dve.wait_ge(gt_e, 2 * (n + 1))
                if l > 0:
                    seq(V.scalar_tensor_tensor(num, en, lb[:, l, i:i + 1], ep, ALU.mult, ALU.add))
                V.tensor_tensor(den, ep, en, ALU.add).then_inc(gt_den, 1)
                dve.wait_ge(gt_den, n + 1)
                seq(V.reciprocal(rden, den))
                seq(V.scalar_tensor_tensor(decayed[:, i, :], en, omlb[:, l, i:i + 1], rden, ALU.mult, ALU.mult))
                dve.wait_ge(gt_ln, n + 1 if l == 0 else 4 + 2 * (n + 1 - 4))
                if l == 0:
                    seq(V.tensor_tensor(tn, tp, lnden, ALU.subtract))
                else:
                    seq(V.tensor_scalar(tp, z, 80.0, 0.0, ALU.add, ALU.min))
                    seq(V.tensor_tensor(tn, lnnum, lnden, ALU.subtract))
                    seq(V.tensor_tensor(tn, tn, tp, ALU.add))
                way = slice(None, None, 1 if d == 0 else -1)
                V.tensor_tensor_scan(out=z[:, way], data0=K["restart"][:], data1=tn[:, way], initial=0.0,
                                     op0=ALU.mult, op1=ALU.add).then_inc(gt_ok, 1)
                dve.wait_ge(gt_ok, n + 1)

            def qk(l, i):
                if i < 5:
                    n, c = l * 5 + i, QK_CHUNKS[i]
                    at = (PA_QN if c < 4 else PA_KN) + l
                    dve.wait_ge(qrs, n + 1)
                    V.scalar_tensor_tensor(pT[:, c, :], pT[:, c, :], par[:, at:at + 1], scr[:, i % 2, :],
                                           ALU.mult, ALU.mult).then_inc(qnorm, 1)
                if i >= 1:
                    n, c = l * 5 + i - 1, QK_CHUNKS[i - 1]
                    dve.wait_ge(qrot, n + 1)
                    if n >= 1:
                        dve.wait_ge(qk_ok, n)
                    seq(V.tensor_tensor(scr[:, 4, 0:NS], bank(4 + (i - 1) % 2), K["sinT"][:], ALU.mult))
                    dve.wait_ge(qcos, n + 1)
                    V.tensor_tensor(pT[:, c, NP:], scr[:, 4, 0:NS], scr[:, 2 + (i - 1) % 2, 0:NS], ALU.add).then_inc(qk_ok, 1)

            modulations(0, 0)
            for l in range(DEPTH):
                x_whole(dve, l)
                norm(l, 0)
                if l == 0:
                    modulations(0, 1)

                for u in range(18):
                    if u % 2 == 1:
                        dve.wait_ge(proj_ps, 18 * l + u + 1)
                        dst, src = PROJ_EVAC[u](pT, v_tok, i_tok, ps)
                        V.tensor_copy(dst, src).then_inc(proj_dve, 1)
                    if u in AFTER:
                        kind, i = AFTER[u]
                        {"gate": gate, "silu": silu, "qk": qk}[kind](l, i)

                for i in range(NU + 3):
                    if i < NU:
                        n = l * NU + i
                        w = P if i % TT == 0 else TOK
                        dve.wait_ge(sc_ps, n + 1)
                        if i >= 3:
                            dve.wait_ge(sc_exp, n - 2)
                        seq(V.tensor_reduce(st[:, i % 3, 0:1], ps[:, 1024 * (i % 2):1024 * (i % 2) + w], AX_X, ALU.max))
                        V.tensor_scalar(st[:, i % 3, 1:2], st[:, i % 3, 0:1], -HD ** -0.5, None, ALU.mult).then_inc(sc_max, 1)
                    if 1 <= i <= NU:
                        n = l * NU + i - 1
                        j = (i - 1) % 3
                        w = P if (i - 1) % TT == 0 else TOK
                        dve.wait_ge(sc_exp, n + 1)
                        seq(V.reciprocal(st[:, j, 3:4], st[:, j, 2:3]))
                        V.tensor_scalar(scr[:, PBUF[j], 0:w], scr[:, PBUF[j], 0:w], st[:, j, 3:4], None, ALU.mult).then_inc(sc_norm, 1)
                    if i >= 3:
                        n = l * NU + i - 3
                        h, t = (i - 3) // TT, (i - 3) % TT
                        c, b = h // 2, h % 2
                        dve.wait_ge(av_ps, n + 1)
                        V.tensor_copy(pT[64 * b:64 * b + 64, c, t * P:(t + 1) * P],
                                      bank(6 + (i - 3) % 2, P)[64 * b:64 * b + 64, :]).then_inc(av_sb, 1)

                def decay_keys(p, d):
                    u = (l * 2 + p) * 2 + d
                    end = CH - 1 if d == 0 else 0
                    bv = pT[:, C_HF + 2 * d + p, :].rearrange("p (n m) -> p n m", m=CH)
                    if u >= 1:
                        dve.wait_ge(g_ps, 9 * (u - 1) + 1)
                    V.tensor_tensor(scr[:, 10, :].rearrange("p (n m) -> p n m", m=CH),
                                    bv[:, :, end:end + 1].to_broadcast([P, NCH, CH]), bv, ALU.subtract).then_inc(dk_d, 1)

                dve.wait_ge(kz_zero, l + 1)
                decay_keys(0, 0)
                for p in range(2):
                    for d in range(2):
                        u = (l * 2 + p) * 2 + d
                        q, k = pT[:, C_HQ + p, :], decayed[:, 2 * d + p, :]
                        eb, qd, kd = scr[:, 8, :], scr[:, 9, :], scr[:, 10, :]
                        end = CH - 1 if d == 0 else 0
                        dve.wait_ge(dk_e, 2 * (u + 1))
                        V.tensor_tensor(kd, kd, k, ALU.mult).then_inc(dk_ok, 1)
                        if u >= 1:
                            dve.wait_ge(inter_ps, u)
                        V.tensor_tensor(qd, q, eb, ALU.mult).then_inc(dk_ok, 1)

                        def level(i):
                            m = HALVES[i]
                            n = u * 6 + i
                            dve.wait_ge(lv_e, n + 1)
                            if n >= 2:
                                dve.wait_ge(g_ps, (n - 2) // 6 * 9 + (n - 2) % 6 + 4)

                            def halves(x, which):
                                return x.rearrange("p (n m) -> p n m", m=2 * m)[:, :, which]
                            qs, ks = (slice(m, 2 * m), slice(0, m)) if d == 0 else (slice(0, m), slice(m, 2 * m))
                            e = scr[:, 2 + i % 2, :]
                            V.tensor_tensor(halves(scr[:, 6 + i % 2, :], qs), halves(q, qs), halves(e, qs), ALU.mult).then_inc(lv_ok, 1)
                            for h in range(2):
                                hs = slice(64 * h, 64 * h + 64)
                                V.tensor_tensor(halves(kz[hs, i % 2, h, :], ks), halves(k[hs, :], ks), halves(e[hs, :], ks),
                                                ALU.mult).then_inc(lv_ok, 1)
                        g0 = u * 9
                        level(0)
                        level(1)
                        dve.wait_ge(g_ps, g0 + 1)
                        if p == 0 and d == 0:
                            dve.wait_ge(cache_out, 16 * 2 * (l + 1))
                        V.tensor_copy(scr[:, 11, :], ps[:, 1536 * ((g0) % 2):1536 * ((g0) % 2) + TOK]).then_inc(g_used, 1)
                        dve.wait_ge(g_ps, g0 + 2)
                        o = 1536 * ((g0 + 1) % 2)
                        if u >= 1:
                            dve.wait_ge(state_out, 32 * u)
                        for i, cnt in ((1, 4), (0, 5)):
                            ins = V.tensor_tensor(S[:, i::2, :], ps[:, o + 1024 * i:o + 1024 * i + cnt * P].rearrange("p (n v) -> p n v", v=P),
                                                  blockones[:].unsqueeze(1).to_broadcast([P, cnt, P]), ALU.mult)
                            if i == 1:
                                seq(ins)
                        ins.then_inc(g_used, 1)
                        dve.wait_ge(g_used, g0 + 2)
                        order = chunk_order(d)

                        def state(j):
                            ch = order[j]
                            prev = s_init[:, l, d, p, :] if j == PROMPT_CH else S[:, j - 1, :]
                            if 8 * u + j > 1:
                                dve.wait_ge(s_ok, 8 * u + j - 1)
                            V.scalar_tensor_tensor(S[:, j, :], prev, eb[:, ch * CH + end:ch * CH + end + 1], S[:, j, :],
                                                   ALU.mult, ALU.add).then_inc(s_ok, 1)

                        for i in range(7):
                            g = g0 + 2 + i
                            o = 1536 * (g % 2)
                            dve.wait_ge(g_ps, g + 1)
                            if i == 0:
                                if u >= 1:
                                    dve.wait_ge(intra_ps, u)
                                V.tensor_tensor(aT, ident[:].unsqueeze(1).to_broadcast([P, 10, P]),
                                                ps[:, o:o + 10].unsqueeze(2).to_broadcast([P, 10, P]), ALU.mult).then_inc(g_used, 1)
                            else:
                                m, n = HALVES[i - 1], CH // HALVES[i - 1]
                                qs = slice(m, 2 * m) if d == 0 else slice(0, m)

                                def queries(x):
                                    return x.rearrange("p a (n m) -> p a n m", m=2 * m)[:, :, :, qs]
                                mask = queries(K["lvl"][:, d, i - 1:i, :]).to_broadcast([P, 2 * TT, n, m])
                                dve.wait_ge(g_used, g)
                                V.copy_predicated(queries(aT), mask,
                                                  queries(ps[:, o:o + 1280].rearrange("p (a t) -> p a t", t=P))).then_inc(g_used, 1)
                            if 1 <= i <= 4:
                                level(i + 1)
                            if i == 5 and (p, d) != (1, 1):
                                decay_keys(p + (d == 1), 1 - d)
                            if i < 4:
                                state(2 * i + 1)
                                state(2 * i + 2)
                    n = 2 * l + p
                    dve.wait_ge(on_rs, n + 1)
                    seq(V.scalar_tensor_tensor(scr[:, 1, :], ps[:, 3072:3072 + TOK], par[:, PA_HN + l:PA_HN + l + 1],
                                               scr[:, 0, :], ALU.mult, ALU.mult))
                    V.tensor_tensor(pT[:, C_HG + p, :], pT[:, C_HG + p, :], scr[:, 1, :], ALU.mult).then_inc(on_ok, 1)

                dve.wait_ge(f_ab, l + 1)
                V.tensor_copy(scr_flat[:, 0:512], bank(6)).then_inc(f_abs, 1)
                for p in range(2):
                    n = 2 * l + p
                    dve.wait_ge(f_z, n + 1)
                    V.tensor_copy(scr_flat[:, 1280 * (1 + p):1280 * (2 + p)], ps[:, 1536 * p:1536 * p + 1280]).then_inc(f_zs, 1)

                for c in range(KC):
                    n = l * KC + c
                    dve.wait_ge(op_ps, n + 1)
                    for g, a, b in GROUPS:
                        V.scalar_tensor_tensor(xT[:, c, a:b], ps[:, 1024 * (c % 3) + a:1024 * (c % 3) + b],
                                               mods[:, l, 2, c, g:g + 1], xT[:, c, a:b], ALU.mult, ALU.add).then_inc(x_mid, 1)
                dve.wait_ge(x_mid, 2 * KC * (l + 1))
                dve.wait_ge(state_out, 16 * 8 * (l + 1))
                norm(l, 1)

                dve.wait_ge(lg_ps, l + 1)
                R = lambda at, n: rt[:, at:at + n]
                lg = R(0, 100).rearrange("p (t e) -> p t e", t=TT)
                V.tensor_copy(lg, bank(7, 100).rearrange("p (t e) -> p t e", t=TT)).then_inc(lg_sb, 1)
                dve.wait_ge(lg_sb, l + 1)
                lgg, lge = lg[:, :, 0:NEG], lg[:, :, NEG:]
                gmax = R(100, 5).unsqueeze(2)
                t4 = R(110, 20).rearrange("p (t e) -> p t e", t=TT)
                u4 = R(130, 20).rearrange("p (t e) -> p t e", t=TT)
                s5 = R(150, 5).unsqueeze(2)
                ohg = R(160, 20).rearrange("p (t e) -> p t e", t=TT)
                gw = R(180, 5).unsqueeze(2)
                iota4 = K["tileno"][:, 32:36].unsqueeze(1).to_broadcast([P, TT, 4])

                def first_max(vals, mx, onehot):
                    seq(V.tensor_reduce(mx, vals, AX_X, ALU.max))
                    seq(V.tensor_tensor(t4, vals, mx.to_broadcast([P, TT, 4]), ALU.is_lt))
                    seq(V.scalar_tensor_tensor(t4, t4, 8.0, iota4, ALU.mult, ALU.add))
                    seq(V.tensor_reduce(s5, t4, AX_X, ALU.min))
                    seq(V.tensor_tensor(onehot, iota4, s5.to_broadcast([P, TT, 4]), ALU.is_equal))

                first_max(lgg, gmax, ohg)
                seq(V.tensor_tensor(u4, lgg, gmax.to_broadcast([P, TT, 4]), ALU.subtract))
                les = R(190, 20).rearrange("p (t e) -> p t e", t=TT)
                big = R(210, 80).rearrange("p (t e g) -> p t e g", t=TT, e=4)
                for t in range(TT):
                    seq(V.tensor_tensor(big[:, t], lge[:, t].rearrange("p (g e) -> p e g", g=4),
                                        ohg[:, t:t + 1, :].to_broadcast([P, 4, 4]), ALU.mult))
                seq(V.tensor_reduce(les, big, AX_X, ALU.add))
                m1, m2 = R(290, 5).unsqueeze(2), R(295, 5).unsqueeze(2)
                oh1 = R(300, 20).rearrange("p (t e) -> p t e", t=TT)
                oh2 = R(320, 20).rearrange("p (t e) -> p t e", t=TT)
                le2 = R(340, 20).rearrange("p (t e) -> p t e", t=TT)
                first_max(les, m1, oh1)
                seq(V.tensor_scalar(le2, oh1, -1.0, 1.0, ALU.mult, ALU.add))
                seq(V.tensor_tensor(le2, le2, les, ALU.mult))
                seq(V.scalar_tensor_tensor(le2, oh1, -BIG, le2, ALU.mult, ALU.add))
                first_max(le2, m2, oh2)
                V.tensor_tensor(R(360, 5).unsqueeze(2), m2, m1, ALU.subtract).then_inc(rt_m, 1)
                o1 = R(400, 80).rearrange("p (t e) -> p t e", t=TT)
                o2 = R(480, 80).rearrange("p (t e) -> p t e", t=TT)
                both = R(560, 80)
                for t in range(TT):
                    for o, oh in ((o1, oh1), (o2, oh2)):
                        seq(V.tensor_tensor(o[:, t].rearrange("p (g e) -> p g e", g=4),
                                            ohg[:, t, :].unsqueeze(2).to_broadcast([P, 4, 4]),
                                            oh[:, t:t + 1, :].to_broadcast([P, 4, 4]), ALU.mult))
                V.tensor_tensor(both, R(400, 80), R(480, 80), ALU.add).then_inc(rt_m, 1)
                dve.wait_ge(rt_e, 2 * (l + 1))
                e4 = R(130, 20).rearrange("p (t e) -> p t e", t=TT)
                seq(V.tensor_reduce(gw, e4, AX_X, ALU.add))
                e21 = R(360, 5).unsqueeze(2)
                seq(V.tensor_scalar(R(365, 5), R(360, 5), 1.0, None, ALU.add))
                seq(V.tensor_tensor(R(370, 5), R(365, 5), R(180, 5), ALU.mult))
                seq(V.reciprocal(R(375, 5), R(370, 5)))
                seq(V.tensor_copy(wgt[:, :, 0], R(375, 5)))
                seq(V.tensor_tensor(wgt[:, :, 1], R(375, 5), R(360, 5), ALU.mult))
                dve.wait_ge(rk_ps, l + 1)
                cnt, ntl, inc, exc = R(640, 16), R(656, 16), R(672, 16), R(100, 16)
                seq(V.tensor_copy(cnt, bank(6, 16, 80)))
                seq(V.tensor_scalar(ntl, cnt, 0.0, None, ALU.is_gt))
                for j in range(1, TT):
                    seq(V.scalar_tensor_tensor(ntl, cnt, float(P * j), ntl, ALU.is_gt, ALU.add))
                seq(V.tensor_tensor_scan(out=inc, data0=ones[:, 0:16], data1=ntl, initial=0.0, op0=ALU.mult, op1=ALU.add))
                seq(V.tensor_tensor(exc, inc, ntl, ALU.subtract))
                cmp = scr_flat[:, 7000:7000 + MT * 16].rearrange("p (j e) -> p j e", e=16)
                seq(V.tensor_tensor(cmp, inc.unsqueeze(1).to_broadcast([P, MT, 16]),
                                    K["tileno"][:, 0:MT].unsqueeze(2).to_broadcast([P, MT, 16]), ALU.is_le))
                seq(V.tensor_reduce(scr_flat[:, 7552:7552 + MT], cmp, AX_X, ALU.add))
                seq(V.tensor_scalar(scr_flat[:, 7552:7552 + MT], scr_flat[:, 7552:7552 + MT], float(NE - 1), None, ALU.min))
                V.tensor_copy(tile_e[:, 0:MT], scr_flat[:, 7552:7552 + MT]).then_inc(rt_ok, 1)

                pos = R(210, 80)
                seq(V.scalar_tensor_tensor(pos.rearrange("p (t e) -> p t e", t=TT),
                                           exc.unsqueeze(1).to_broadcast([P, TT, 16]), float(P),
                                           bank(6, 80).rearrange("p (t e) -> p t e", t=TT), ALU.mult, ALU.add))
                for c, o in enumerate((R(400, 80), R(480, 80))):
                    seq(V.tensor_tensor(o, o, pos, ALU.mult))
                    seq(V.tensor_reduce(R(380 + 5 * c, 5), o.rearrange("p (t e) -> p t e", t=TT), AX_X, ALU.add))
                    if l > 0 and c == 0:
                        all_of(dve, y_in, l - 1, TT, 32)
                    seq(V.tensor_copy(slot_i[:, :, c], R(380 + 5 * c, 5)))
                sl, q, tile, row = R(380, 10), R(400, 10), R(410, 10), R(420, 10)
                at_or_below = scr_flat[:, 7000:7000 + 10 * MT].rearrange("p (i j) -> p i j", j=MT)
                places = scr_flat[:, 7424:7424 + P]
                seq(V.tensor_scalar(q, sl, 1.0 / P, None, ALU.mult))
                seq(V.tensor_tensor(at_or_below, K["tileno"][:, 0:MT].unsqueeze(1).to_broadcast([P, 10, MT]),
                                    q.unsqueeze(2).to_broadcast([P, 10, MT]), ALU.is_le))
                seq(V.tensor_reduce(tile, at_or_below, AX_X, ALU.add))
                seq(V.scalar_tensor_tensor(row, tile, -float(P), sl, ALU.mult, ALU.add))
                seq(V.tensor_scalar(tile, tile, -1.0, None, ALU.add))
                seq(V.tensor_tensor_scan(out=places, data0=ones[:], data1=ones[:], initial=-float(P) - 1.0,
                                         op0=ALU.mult, op1=ALU.add))
                for i in range(TOPK * TT):
                    V.tensor_scalar(slot_row[:, i, :], places, row[:, i:i + 1], None, ALU.is_equal)
                    ins = V.tensor_scalar(slot_tile[:, i, :], K["tileno"][:, 0:MT], tile[:, i:i + 1],
                                          K["tileno"][:, 40 + i % TT:41 + i % TT], ALU.is_equal, ALU.mult)
                ins.then_inc(tb_in, 1)
                dve.wait_ge(tb_ps, l + 1)
                V.tensor_copy(slot_tok[:], bank(6, MT, P)).then_inc(tb_ok, 1)

                if l + 1 < DEPTH:
                    modulations(l + 1, 0)
                rest(dve, V, "dve", "gate", l, 0, 0)
                for i in range(MT + 2):
                    if 1 <= i <= MT:
                        rest(dve, V, "dve", "up", l, i - 1, 0)
                    if i >= 2:
                        n = l * MT + i - 2
                        dst, src = hid_split[:, i % 2], bank(4, 256).rearrange("p (k t) -> p k t", k=2)
                        dve.wait_ge(hid_ps, n + 1)
                        if i >= 4:
                            multiplied(dve, "down", l, i - 4)
                        V.tensor_copy(dst[:, 0], src).then_inc(hid_sb, 1)
                        dve.wait_ge(hid_sb, 2 * n + 1)
                        V.tensor_tensor(dst[:, 1], src, dst[:, 0], ALU.subtract).then_inc(hid_sb, 1)
                    if i < MT:
                        dve.wait_ge(xg_sb, l * MT + i + 1)
                        V.tensor_tensor(x_split[:, i % 2, 1], ps[:, 0:1024].rearrange("p (k t) -> p k t", k=KC), x_split[:, i % 2, 0],
                                        ALU.subtract).then_inc(xg_lo, 1)
                    if 1 <= i <= MT:
                        rest(dve, V, "dve", "up", l, i - 1, 1)
                    if i >= 2:
                        rest(dve, V, "dve", "down", l, i - 2, 1)
                    if 1 <= i < MT:
                        rest(dve, V, "dve", "gate", l, i, 0)
                    if 1 <= i <= MT:
                        n = l * MT + i - 1
                        j = (i - 1) % 2
                        dve.wait_ge(gu_s, n + 1)
                        if n >= 2:
                            dve.wait_ge(hid_ps, n - 1)
                        V.tensor_tensor(hid[:, j, :], bank(2 + j, DE, DE), sg[:, j, :], ALU.mult).then_inc(hid_ok, 1)
                    if i >= 2:
                        n = l * MT + i - 2
                        j = i % 2
                        multiplied(dve, "down", l, i - 2)
                        if nth(l, MT, i - 2) > 1:
                            dve.wait_ge(y_out[j], 16 * (nth(l, MT, i - 2) - 1))
                        V.tensor_copy(yb[:, j, :], ps[:, 2560:2560 + D]).then_inc(dn_sb, 1)
                for t in range(TT):
                    n = l * TT + t
                    j = t % 2
                    dve.wait_ge(y_w, n + 1)
                    V.scalar_tensor_tensor(y2[:, j, :], y2[:, j, :], wgt[:, t, 1:2], y1[:, j, :], ALU.mult, ALU.add).then_inc(y_sum, 1)
                    dve.wait_ge(yt_ps, n + 1)
                    g = 0 if t == 0 else 1
                    for k in range(KC):
                        V.scalar_tensor_tensor(xT[:, k, t * P:(t + 1) * P],
                                               ps[:, 1024 * j + k * P:1024 * j + (k + 1) * P],
                                               mods[:, l, 5, k, g:g + 1], xT[:, k, t * P:(t + 1) * P],
                                               ALU.mult, ALU.add).then_inc(x_new, 1)
                if l + 1 < DEPTH:
                    modulations(l + 1, 1)

        @block.tensor
        def _(pe):
            mm = nc.tensor.matmul

            def item(n):
                pe.wait_ge(slot_in[n % RING], landed[n])
                return slot(n)

            def columns(out, lhs, rhs, parts, start, stop, **kw):
                for a, b in parts:
                    ins = mm(out[:, a:b], lhs, rhs[:, a:b], start=start, stop=stop, **kw)
                return ins

            WIDE = ((0, 512), (512, TOK))

            pe.wait_ge(x_in, 48)
            pe.wait_ge(params_in, 16 * (N_PARAM_DMAS + 4))
            nc.tensor.transpose(bank(4, PA_ROWS), rows[0:PA_ROWS, 0, :], ident[0:PA_ROWS, 0:PA_ROWS]).then_inc(par_ps, 1)
            nc.tensor.transpose(bank(4, 96, PB0), rows[0:96, 1, :], ident[0:96, 0:96]).then_inc(par_ps, 1)
            for l in range(DEPTH):
                last = nc.tensor.transpose(bank(5, P, P * l), ck_row[:, l, :], ident[:])
            last.then_inc(par_ps, 1)
            for t in range(TT):
                if t >= 2:
                    pe.wait_ge(xt_act if t % 2 == 0 else xt_dve, t // 2)
                for k in range(KC):
                    last = nc.tensor.transpose(ps[:, 1024 * (t % 2) + k * P:1024 * (t % 2) + (k + 1) * P],
                                               xrow[:, t, k * P:(k + 1) * P], ident[:])
                last.then_inc(xt_ps, 1)
            pe.wait_ge(cond_ok, 1)
            pe.wait_ge(ck_sb, 1)

            def norm(l, which):
                n0 = (l * 2 + which) * KC
                for k in range(KC):
                    pe.wait_ge(nsq, n0 + k + 1)
                    sq = scr[:, k % 2, :]
                    mm(bank(5), ones[:], sq[:, NP:], start=(k == 0), stop=(k == KC - 1))
                    mm(bank(6, NP), ones[:], sq[:, 0:NP], start=(k == 0), stop=(k == KC - 1)).then_inc(nsum, 1)

            def ada(l, half, first, end):
                for i in range(first, end + (end == ADA_HALF)):
                    n = (2 * l + half) * ADA_HALF + i
                    if i < ADA_HALF:
                        w = item(ITEM["ada", l, ADA_HALF * half + i]).rearrange("p (k n) -> p k n", k=KC)
                        if n >= 2:
                            pe.wait_ge(ada_sb, n - 1)
                        for k in range(KC):
                            last = mm(bank(4 + i % 2, 256)[0:2, :], cond[:, :, k], w[:, k, :], start=(k == 0), stop=(k == KC - 1))
                        last.then_inc(ada_ps, 1)
                    if i >= 1:
                        pe.wait_ge(ada_sb, n)
                        for j in range(2):
                            last = nc.tensor.transpose(bank(7, 2, 4 * (i - 1) + 2 * j), mrow[:, (i - 1) % 2, j * P:(j + 1) * P],
                                                       ident[0:2, 0:2])
                        last.then_inc(ada_tr, 1)

            def output(t):
                pe.wait_ge(x_new, KC * (TT * (DEPTH - 1) + t + 1))
                if t >= 2:
                    pe.wait_ge(fin_sb, t - 1)
                if t == 0:
                    pe.wait_ge(dn_sb, MT * DEPTH)
                for k in range(KC):
                    last = nc.tensor.transpose(ps[:, 2048 + 1024 * (t % 2) + k * P:2048 + 1024 * (t % 2) + (k + 1) * P],
                                               xT[:, k, t * P:(t + 1) * P], ident[:])
                last.then_inc(fin_ps, 1)

            ada(0, 0, 0, ADA_HALF)
            pe.wait_ge(consts_in, 16 * N_CONST)
            pe.wait_ge(late_in, 16 * 16 * DEPTH)
            for l in range(DEPTH):
                norm(l, 0)
                if l == 0:
                    pe.wait_ge(mods_ok, 1)
                    pe.wait_ge(nrs, 1)
                    ada(0, 1, 0, ADA_HALF)

                def unit(u):
                    if u >= 2:
                        pe.wait_ge(proj_act if u % 2 == 0 else proj_dve, 9 * l + (u - 2) // 2 + 1)
                    return ps[:, 1024 * (u % 2):1024 * (u % 2) + 1024]

                def qk(i):
                    if i < 5:
                        n = l * 5 + i
                        pe.wait_ge(qsq, n + 1)
                        if i >= 1:
                            pe.wait_ge(qrs, n)
                        columns(ps[:, 3072:4096], blockones[:], scr[:, i % 2, :], WIDE, True, True).then_inc(qsum, 1)
                    if i >= 1:
                        n, c = l * 5 + i - 1, QK_CHUNKS[i - 1]
                        pe.wait_ge(qnorm, n + 1)
                        if i >= 3:
                            pe.wait_ge(qk_ok, n - 1)
                        mm(bank(4 + (i - 1) % 2), rot[:], pT[:, c, NP:], start=True, stop=True).then_inc(qrot, 1)

                for i, c0 in enumerate(IN_ORDER):
                    w = item(ITEM["in", l, i]).rearrange("p (k n) -> p k n", k=KC)
                    for j in range(2):
                        u = 2 * i + j
                        out = unit(u)
                        if c0 != 6 and (c0, j) != (2, 1):
                            for k in range(KC):
                                if u == 0:
                                    pe.wait_ge(h_ok, 4 * KC * l + 2 * (k + 1))
                                last = columns(out, w[:, k, j * P:(j + 1) * P], hT[:, k, :], WIDE, k == 0, k == KC - 1)
                        else:
                            if c0 == 2:
                                tiles, a, width = range(TT), P, P
                            else:
                                tiles, a, width = (range(4) if j == 0 else range(4, 5)), 0, 256
                            for s, t in enumerate(tiles):
                                for k in range(KC):
                                    last = mm(out[:, s * width:(s + 1) * width], hT[:, k, t * P:(t + 1) * P],
                                              w[:, k, a:a + width], start=(k == 0), stop=(k == KC - 1))
                        last.then_inc(proj_ps, 1)
                        if u in AFTER and AFTER[u][0] == "qk":
                            qk(AFTER[u][1])
                pe.wait_ge(qk_ok, 5 * (l + 1))
                nc.tensor.transpose(bank(5, P), pT[:, C_K, 0:NP], ident[:]).then_inc(ck_ps, 1)
                pe.wait_ge(proj_act, 9 * (l + 1))
                pe.wait_ge(proj_dve, 9 * (l + 1))

                for i in range(NU + 3):
                    if i < NU:
                        n = l * NU + i
                        h, t = i // TT, i % TT
                        c, b = h // 2, slice(64 * (h % 2), 64 * (h % 2) + 64)
                        if i >= 2:
                            pe.wait_ge(sc_exp, n - 1)
                        out = ps[:, 1024 * (i % 2):1024 * (i % 2) + 1024]
                        q = pT[b, c, t * P:(t + 1) * P]
                        if t == 0:
                            last = mm(out[:, 0:P], q, pT[b, C_K, 0:NP], start=True, stop=True)
                        else:
                            mm(out[:, 0:NS], q, pT[b, C_K, NP:], start=True, stop=True)
                            last = mm(out[:, NS:NS + P], q, ckT[b, l, :], start=True, stop=True)
                        last.then_inc(sc_ps, 1)
                    if 2 <= i <= NU + 1:
                        n = l * NU + i - 2
                        if i == 2:
                            pe.wait_ge(ko_sb, l + 1)
                        pe.wait_ge(sc_norm, n + 1)
                        if i >= 3:
                            pe.wait_ge(pt_sb, n)
                        for s in range(1 if (i - 2) % TT == 0 else 5):
                            last = nc.tensor.transpose(ps[:, 2048 + s * P:2048 + (s + 1) * P],
                                                       scr[:, PBUF[(i - 2) % 3], s * P:(s + 1) * P], ident[:])
                        last.then_inc(pt_ps, 1)
                    if i >= 3:
                        n = l * NU + i - 3
                        h, t = (i - 3) // TT, (i - 3) % TT
                        b = slice(64 * (h % 2), 64 * (h % 2) + 64)
                        pe.wait_ge(pt_sb, n + 1)
                        if i >= 5:
                            pe.wait_ge(av_sb, n - 1)
                        keys = [v_tok[:, 0, b]] if t == 0 else [v_tok[:, 1 + s, b] for s in range(4)] + [cv_tok[:, l, b]]
                        for s, v in enumerate(keys):
                            last = mm(bank(6 + (i - 3) % 2, P)[b, :], v, scr[:, 6 + (i - 3) % 2, s * P:(s + 1) * P],
                                      start=(s == 0), stop=(s == len(keys) - 1))
                        last.then_inc(av_ps, 1)

                pe.wait_ge(av_sb, NU * (l + 1))
                pe.wait_ge(sl_ok, 4 * (l + 1))
                for p in range(2):
                    for d in range(2):
                        u = (l * 2 + p) * 2 + d
                        q, k = pT[:, C_HQ + p, :], decayed[:, 2 * d + p, :]
                        g0 = u * 9
                        pe.wait_ge(gt_ok, 4 * (l + 1))

                        def buffer(g):
                            if g >= 2:
                                pe.wait_ge(g_used, g - 1)
                            return ps[:, 1536 * (g % 2):1536 * (g % 2) + 1536]
                        if d == 0 and u > 0:
                            pe.wait_ge(on_ok, 2 * l + p)
                        out = buffer(g0)
                        pe.wait_ge(dk_ok, 2 * u + 1)
                        for t in range(TT):
                            last = nc.tensor.transpose(out[:, t * P:(t + 1) * P], scr[:, 10, t * P:(t + 1) * P], ident[:])
                        last.then_inc(g_ps, 1)
                        out = buffer(g0 + 1)
                        pe.wait_ge(g_used, g0 + 1)
                        order = chunk_order(d)
                        for i in range(9):
                            t, h = order[i] // 2, slice(64 * (order[i] % 2), 64 * (order[i] % 2) + 64)
                            at = 1024 * (i % 2) + (i // 2) * P
                            last = mm(out[:, at:at + P], scr[h, 11, t * P:(t + 1) * P],
                                      i_tok[h, t, p * P:(p + 1) * P], start=True, stop=True)
                        last.then_inc(g_ps, 1)
                        for i in range(7):
                            g = g0 + 2 + i
                            out = buffer(g)
                            if i == 0:
                                pe.wait_ge(dg_in, u + 1)
                                for t in range(TT):
                                    last = mm(out[:, t:t + 6:5], scr[:, 4, t * P:(t + 1) * P], blockones[:, 0:P:64], start=True, stop=True)
                            else:
                                pe.wait_ge(lv_ok, 3 * (u * 6 + i))
                                for h in range(2):
                                    for t in range(TT):
                                        last = mm(out[:, (h * TT + t) * P:(h * TT + t + 1) * P], kz[:, (i - 1) % 2, h, t * P:(t + 1) * P],
                                                  scr[:, 6 + (i - 1) % 2, t * P:(t + 1) * P], start=True, stop=True)
                            last.then_inc(g_ps, 1)
                            if i == 5:
                                pe.wait_ge(s_ok, 8 * (u + 1))
                                pe.wait_ge(dk_ok, 2 * u + 2)
                                for j, ch in enumerate(order):
                                    if j == 0:
                                        continue
                                    state = (S[:, 0, :] if j == 1 else s_init[:, l, d, p, :] if j == PROMPT_CH
                                             else S[:, j - 1, :])
                                    last = mm(ps[:, 3072 + ch * CH:3072 + (ch + 1) * CH], state,
                                              scr[:, 9, ch * CH:(ch + 1) * CH], start=(d == 0 and ch in (1, 8)),
                                              stop=False, skip_group_check=True)
                                last.then_inc(inter_ps, 1)
                        pe.wait_ge(g_used, g0 + 9)
                        for h in range(2):
                            for t in range(TT):
                                last = mm(ps[64 * h:64 * h + 64, 3072 + t * P:3072 + (t + 1) * P],
                                          i_tok[:, t, p * P + 64 * h:p * P + 64 * h + 64], aT[:, h * TT + t, :],
                                          start=False, stop=(d == 1), skip_group_check=True)
                        last.then_inc(intra_ps, 1)
                    n = 2 * l + p
                    pe.wait_ge(on_sq, n + 1)
                    pe.wait_ge(g_used, (u + 1) * 9)
                    columns(ps[:, 0:1024], blockones[:], scr[:, 0, :], WIDE, True, True).then_inc(on_sum, 1)

                pe.wait_ge(on_ok, 2 * (l + 1))
                for p in range(2):
                    for s in range(2):
                        last = mm(bank(6, P, (2 * p + s) * P), K["dft64"][:, s, :], wft[:, l, p, :], start=True, stop=True)
                last.then_inc(f_ab, 1)
                pe.wait_ge(f_abs, l + 1)
                for p in range(2):
                    for t in range(TT):
                        last = mm(ps[:, 1536 * p + 256 * t:1536 * p + 256 * t + 256], pT[:, C_FT + p, t * P:(t + 1) * P],
                                  scr_flat[:, 256 * p:256 * p + 256], start=True, stop=True)
                    last.then_inc(f_z, 1)
                for p in range(2):
                    n = 2 * l + p
                    pe.wait_ge(f_zs, n + 1)
                    if p == 1:
                        pe.wait_ge(f_os, 2 * n)
                    z = scr_flat[:, 1280 * (1 + p):1280 * (2 + p)].rearrange("p (t s e) -> p t s e", t=TT, s=2)
                    for i, (t, s) in enumerate((t, s) for t in range(4) for s in range(2)):
                        mm(bank(6), z[:, 1 + t, s, :], K["dft_s"][:, s, t, :], start=(i == 0), stop=(i == 7))
                    for s in range(2):
                        last = mm(bank(7, NP), z[:, 0, s, :], K["dft_p"][:, s, 0, :], start=(s == 0), stop=(s == 1))
                    last.then_inc(f_o, 1)
                pe.wait_ge(f_os, 4 * (l + 1))

                for i in range(OUT_ITEMS):
                    w = item(ITEM["out", l, i]).rearrange("p (k n) -> p k n", k=KC)
                    for j in range(2):
                        c = 2 * i + j
                        if c >= 3:
                            pe.wait_ge(x_mid, l * 2 * KC + 2 * (c - 2))
                        out = ps[:, 1024 * (c % 3):1024 * (c % 3) + 1024]
                        for k in range(KC):
                            last = columns(out, w[:, k, j * P:(j + 1) * P], pT[:, MIX[k], :], WIDE, k == 0, k == KC - 1)
                        last.then_inc(op_ps, 1)
                pe.wait_ge(x_mid, 2 * KC * (l + 1))
                norm(l, 1)
                for k in range(KC):
                    pe.wait_ge(h_ok, 2 * KC * (2 * l + 1) + 2 * (k + 1))
                    last = columns(ps[0:NEG + NE, 0:1024], wr[:, l, k, :], hT[:, k, :], WIDE, k == 0, k == KC - 1)
                last.then_inc(lgt_ps, 1)
                pe.wait_ge(lgt_sb, l + 1)
                for t in range(TT):
                    mm(bank(7, 20, 20 * t), lgt[:, t * P:(t + 1) * P], ident[0:NEG + NE, 0:NEG + NE], start=True, stop=False)
                    last = mm(bank(7, 20, 20 * t), ones[0:1, :], br[0:1, l, :], start=False, stop=True)
                last.then_inc(lg_ps, 1)
                for t in range(TT):
                    n = l * TT + t
                    if t >= 2:
                        pe.wait_ge(hr_sb, n - 1)
                    for k in range(KC):
                        last = nc.tensor.transpose(ps[:, 1024 * (t % 2) + k * P:1024 * (t % 2) + (k + 1) * P],
                                                   hT[:, k, t * P:(t + 1) * P], ident[:])
                    last.then_inc(hr_ps, 1)
                if l + 1 < DEPTH:
                    pe.wait_ge(lg_sb, l + 1)
                    ada(l + 1, 0, 0, 5)
                pe.wait_ge(rt_m, 2 * (l + 1))
                pe.wait_ge(nrs, 2 * l + 2)
                both = rt[:, 560:640].rearrange("p (t e) -> p t e", t=TT)
                for t in range(TT + 1):
                    out = bank(6, 16, 16 * t)
                    for s in range(t):
                        last = mm(out, ones[:], both[:, s, :], start=(s == 0), stop=(t == TT and s == TT - 1))
                    if t < TT:
                        mm(out, tri[:], both[:, t, :], start=(t == 0), stop=True)
                last.then_inc(rk_ps, 1)
                if l + 1 < DEPTH:
                    ada(l + 1, 0, 5, 8)
                pe.wait_ge(tb_in, l + 1)
                for i in range(TOPK * TT):
                    last = mm(bank(6, MT, P), slot_row[:, i, :], slot_tile[:, i, :], start=(i == 0), stop=(i == TOPK * TT - 1))
                last.then_inc(tb_ps, 1)
                if l + 1 < DEPTH:
                    ada(l + 1, 0, 8, ADA_HALF)
                    pe.wait_ge(mods_ok, 2 * l + 3)

                pe.wait_ge(hr_sb, TT * (l + 1))
                pe.wait_ge(rt_ok, l + 1)
                def products(out, x, w, start, stop):
                    mm(out, x[0], w[0], start=start, stop=False)
                    mm(out, x[0], w[1], start=False, stop=False)
                    return mm(out, x[1], w[0], start=False, stop=stop)

                def unit_split(kind, i, h):
                    pe.wait_ge(w_lo[REST_BY[kind, h]], REST_COUNT[kind, l, i, h])
                    return w_split[UNIT[kind, l, i, h] % WB]

                for i in range(MT + 2):
                    if i < MT:
                        n = l * MT + i
                        pe.wait_ge(xg_in[i % XB], 16 * nth(l, MT, i, XB))
                        if i >= 1:
                            pe.wait_ge(xg_lo, n)
                        for k in range(KC):
                            last = nc.tensor.transpose(ps[:, k * P:(k + 1) * P], xg[:, i % XB, k * P:(k + 1) * P], ident[:])
                        last.then_inc(xg_ps, 1)
                    if i >= 2:
                        n = l * MT + i - 2
                        pe.wait_ge(hid_ok, n + 1)
                        if i >= 3:
                            pe.wait_ge(hid_sb, 2 * n)
                        for k in range(2):
                            last = nc.tensor.transpose(bank(4, P, k * P), hid[:, i % 2, k * P:(k + 1) * P], ident[:])
                        last.then_inc(hid_ps, 1)
                    if 1 <= i <= MT:
                        n = l * MT + i - 1
                        j = (i - 1) % 2
                        pe.wait_ge(xg_lo, n + 1)
                        if i >= 3:
                            pe.wait_ge(hid_ok, n - 1)
                        for kind, at in (("gate", 0), ("up", DE)):
                            for h in range(2):
                                w = unit_split(kind, i - 1, h)[:, :, :].rearrange("p s (k n) -> p s k n", k=4)
                                for k in range(4):
                                    last = products(bank(2 + j, DE, at), [x_split[:, j, s, 4 * h + k, :] for s in range(2)],
                                                    [w[:, s, k, :] for s in range(2)], h == 0 and k == 0, h == 1 and k == 3)
                                last.then_inc(w_used, 1)
                    if i >= 2:
                        n = l * MT + i - 2
                        pe.wait_ge(hid_sb, 2 * n + 2)
                        if i >= 3:
                            pe.wait_ge(dn_sb, n)
                        for h in range(2):
                            w = unit_split("down", i - 2, h)
                            for half in range(2):
                                last = products(bank(5 + half), [hid_split[:, i % 2, s, h, :] for s in range(2)],
                                                [w[:, s, 512 * half:512 * half + 512] for s in range(2)], h == 0, h == 1)
                            last.then_inc(w_used, 1)
                if l + 1 < DEPTH:
                    pe.wait_ge(dn_sb, MT * (l + 1))
                    ada(l + 1, 1, 0, ADA_AT[0])
                for t in range(TT):
                    n = l * TT + t
                    pe.wait_ge(y_sum, n + 1)
                    if t >= 2:
                        pe.wait_ge(x_new, 8 * (n - 1))
                    for k in range(KC):
                        last = nc.tensor.transpose(ps[:, 1024 * (t % 2) + k * P:1024 * (t % 2) + (k + 1) * P],
                                                   y2[:, t % 2, k * P:(k + 1) * P], ident[:])
                    last.then_inc(yt_ps, 1)
                    if l + 1 < DEPTH:
                        ada(l + 1, 1, ADA_AT[t], ADA_AT[t + 1])
                    elif t >= 1:
                        output(t - 1)

            output(TT - 1)


_INS = ["x_prompt", "x_sample", "cache_k", "cache_v", "state_fwd", "state_bwd", "c", "c_ctx", "w_ada", "b_ada",
        "norm1_w", "norm2_w", "w_in", "q_norm_w", "k_norm_w", "hg_lb", "hg_norm_w", "w_ft", "w_out",
        "w_gr", "b_gr", "w_er", "b_er", "w_gate", "w_up", "w_down"]
_OUTS = [(1, NP, D), (1, NS, D), (1, DEPTH, NP, 2, HD), (1, DEPTH, NP, 2, HD), (1, DEPTH, 4, HD, HD), (1, DEPTH, 4, HD, HD)]


def kernel(**inputs):
    import numpy as _np
    import concourse.bacc as _bacc
    from concourse import mybir as _mybir
    from concourse.bass_utils import run_bass_kernel_spmd as _run

    nc = _bacc.Bacc("TRN2", target_bir_lowering=False, num_devices=1)
    arrays, A, C = {}, {}, {}
    for name in _INS:
        a = _np.ascontiguousarray(inputs[name])
        arrays[f"in_{name}_dram"] = a
        A[name] = nc.dram_tensor(f"in_{name}_dram", a.shape, _mybir.dt.from_np(a.dtype), kind="ExternalInput").ap()
    for name, a in shape_constants().items():
        arrays[f"const_{name}_dram"] = a
        C[name] = nc.dram_tensor(f"const_{name}_dram", a.shape, _mybir.dt.from_np(a.dtype), kind="ExternalInput").ap()
    outs = [nc.dram_tensor(f"out_{i}_dram", s, _mybir.dt.float32, kind="ExternalOutput").ap() for i, s in enumerate(_OUTS)]
    build_program(nc, A, C, outs)
    r = _run(nc, [arrays], core_ids=[0])
    return tuple(r.results[0][f"out_{i}_dram"] for i in range(len(_OUTS)))
```
